# Optimizing a Trainium2 kernel written in Bass

```python
import math
import jax, jax.numpy as jnp
from jax import lax
import numpy as np

D_MODEL = 2048
BATCH = 1
SEQ = 256
DEPTH = 1

CHUNK = 64
LEFT_CHUNKS = 8
BAND = LEFT_CHUNKS + 1

MIX_WIDTH = D_MODEL
ATTN_WIDTH = MIX_WIDTH // 2
POOL_WIDTH = MIX_WIDTH - ATTN_WIDTH
HEAD_DIM = 128
N_HEADS = ATTN_WIDTH // HEAD_DIM
REL_CLIP = 128
POOL_WINDOWS = (2, 4, 8, 16)
N_POOL_GROUPS = len(POOL_WINDOWS)
POOL_GROUP = POOL_WIDTH // N_POOL_GROUPS
IN_WIDTH = 3 * ATTN_WIDTH + POOL_WIDTH

D_FF = 5632
CONV_WIDTH = 3
NORM_EPS = 1e-6


def rms_norm(x, g):
    xf = x.astype(jnp.float32)
    y = xf * lax.rsqrt(jnp.mean(xf * xf, axis=-1, keepdims=True) + NORM_EPS)
    return (y * g.astype(jnp.float32)).astype(x.dtype)

def _band_bias_index():
    q_pos = np.arange(CHUNK) + LEFT_CHUNKS * CHUNK
    k_pos = np.arange(BAND * CHUNK)
    rel = np.clip(q_pos[:, None] - k_pos[None, :], -REL_CLIP, REL_CLIP)
    return (rel + REL_CLIP).astype(np.int32)

def chunked_attention(q, k, v, rel_bias):
    B, S, H, Dh = q.shape
    N = S // CHUNK
    qc = q.reshape(B, N, CHUNK, H, Dh)
    pad = ((0, 0), (LEFT_CHUNKS * CHUNK, 0), (0, 0), (0, 0))
    kc = jnp.pad(k, pad).reshape(B, N + LEFT_CHUNKS, CHUNK, H, Dh)
    vc = jnp.pad(v, pad).reshape(B, N + LEFT_CHUNKS, CHUNK, H, Dh)
    scale = 1.0 / math.sqrt(Dh)
    scores = jnp.concatenate(
        [jnp.einsum('bnqhd,bnkhd->bnhqk', qc, kc[:, j:j + N],
                    preferred_element_type=jnp.float32) for j in range(BAND)],
        axis=-1) * scale
    bias = rel_bias.astype(jnp.float32)[:, _band_bias_index()]
    scores = scores + bias[None, None]
    key_chunk = np.repeat(np.arange(BAND), CHUNK)
    valid = (jnp.arange(N)[:, None] + key_chunk[None, :]) >= LEFT_CHUNKS
    scores = jnp.where(valid[None, :, None, None, :], scores, jnp.float32(-1e30))
    probs = jax.nn.softmax(scores, axis=-1).astype(v.dtype)
    out = 0.0
    for j in range(BAND):
        out = out + jnp.einsum('bnhqk,bnkhd->bnqhd',
                               probs[..., j * CHUNK:(j + 1) * CHUNK], vc[:, j:j + N])
    return out.reshape(B, S, H, Dh)

def multiscale_pool(u, pool_w, pool_scale):
    B, S, _ = u.shape
    uf = u.astype(jnp.float32)
    cs = jnp.cumsum(uf, axis=1)
    pos_count = jnp.arange(1, S + 1, dtype=jnp.float32)
    groups = []
    for g, w in enumerate(POOL_WINDOWS):
        sl = slice(g * POOL_GROUP, (g + 1) * POOL_GROUP)
        csg = cs[..., sl]
        shifted = jnp.pad(csg, ((0, 0), (w, 0), (0, 0)))[:, :S]
        count = jnp.minimum(pos_count, jnp.float32(w))[None, :, None]
        groups.append((csg - shifted) / count - uf[..., sl])
    pooled = jnp.stack(groups, axis=2).astype(u.dtype)
    mixed = jnp.einsum('bsgc,gcd->bsgd', pooled, pool_w).reshape(B, S, POOL_WIDTH)
    return mixed * pool_scale

def causal_dwconv(u, conv_w, conv_b):
    S = u.shape[1]
    up = jnp.pad(u, ((0, 0), (CONV_WIDTH - 1, 0), (0, 0)))
    out = conv_b
    for t in range(CONV_WIDTH):
        out = out + up[:, t:t + S] * conv_w[t]
    return out

def first_inputs(seed: int = 0) -> dict:
    key = jax.random.key(seed)
    ks = jax.random.split(key, 16)
    f32 = jnp.float32
    nrm = lambda k, shape, s: jax.random.normal(k, shape, f32) * s
    gain = lambda k, n: 1.0 + 0.02 * jax.random.normal(k, (DEPTH, n), f32)
    return {
        "x": nrm(ks[0], (BATCH, SEQ, D_MODEL), 1.0),
        "pre_mix_g": gain(ks[1], D_MODEL),
        "w_in": nrm(ks[2], (DEPTH, D_MODEL, IN_WIDTH), D_MODEL ** -0.5),
        "rel_bias": nrm(ks[3], (DEPTH, N_HEADS, 2 * REL_CLIP + 1), 0.1),
        "pool_w": nrm(ks[4], (DEPTH, N_POOL_GROUPS, POOL_GROUP, POOL_GROUP), POOL_GROUP ** -0.5),
        "pool_scale": gain(ks[5], POOL_WIDTH),
        "w_o": nrm(ks[6], (DEPTH, MIX_WIDTH, D_MODEL), MIX_WIDTH ** -0.5),
        "post_mix_g": gain(ks[7], D_MODEL),
        "pre_ffn_g": gain(ks[8], D_MODEL),
        "w_up": nrm(ks[9], (DEPTH, D_MODEL, 2 * D_FF), D_MODEL ** -0.5),
        "conv_w": nrm(ks[10], (DEPTH, CONV_WIDTH, 2 * D_FF), CONV_WIDTH ** -0.5),
        "conv_b": nrm(ks[11], (DEPTH, 2 * D_FF), 0.01),
        "w_down": nrm(ks[12], (DEPTH, D_FF, D_MODEL), D_FF ** -0.5),
        "post_ffn_g": gain(ks[13], D_MODEL),
    }

def first_block(x, pre_mix_g, w_in, rel_bias, pool_w, pool_scale, w_o, post_mix_g,
              pre_ffn_g, w_up, conv_w, conv_b, w_down, post_ffn_g):
    B, S, _ = x.shape
    for l in range(DEPTH):
        h = rms_norm(x, pre_mix_g[l])
        z = h @ w_in[l]
        q = z[..., :ATTN_WIDTH].reshape(B, S, N_HEADS, HEAD_DIM)
        k = z[..., ATTN_WIDTH:2 * ATTN_WIDTH].reshape(B, S, N_HEADS, HEAD_DIM)
        v = z[..., 2 * ATTN_WIDTH:3 * ATTN_WIDTH].reshape(B, S, N_HEADS, HEAD_DIM)
        u = z[..., 3 * ATTN_WIDTH:]
        a = chunked_attention(q, k, v, rel_bias[l]).reshape(B, S, ATTN_WIDTH)
        p = multiscale_pool(u, pool_w[l], pool_scale[l])
        m = jnp.concatenate([a, p], axis=-1) @ w_o[l]
        x = x + rms_norm(m, post_mix_g[l])
        h = rms_norm(x, pre_ffn_g[l])
        up = causal_dwconv(h @ w_up[l], conv_w[l], conv_b[l])
        y = (jax.nn.gelu(up[..., :D_FF], approximate=True) * up[..., D_FF:]) @ w_down[l]
        x = x + rms_norm(y, post_ffn_g[l])
    return x


CTX_LEN = 256
GRID_W = 64
Q_BLOCK = 128
ROPE_THETA = 10000.0
EPS = 1e-6
ADA_CHUNKS = 6

A_HEADS = 16
A_KV_HEADS = 4
A_HEAD_DIM = 128
B_HEADS = 8
B_HEAD_DIM = 64
B_V_DIM = 2 * B_HEAD_DIM

A_Q = A_HEADS * A_HEAD_DIM
A_KV = A_KV_HEADS * A_HEAD_DIM
B_QK = B_HEADS * 2 * B_HEAD_DIM
B_V = B_HEADS * B_V_DIM
KV_WIDTH = 2 * A_KV + B_QK + B_V
IN_WIDTH_2 = KV_WIDTH + A_Q + B_QK + 2 * D_MODEL

D_FF_2 = -(-8 * D_MODEL // (3 * 256)) * 256


def rms_norm_2(x, g):
    xf = x.astype(jnp.float32)
    y = xf * lax.rsqrt(jnp.mean(xf * xf, axis=-1, keepdims=True) + EPS)
    return (y * g.astype(jnp.float32)).astype(x.dtype)

def modulate(h, shift, scale):
    return h * (1 + scale) + shift

def adaln(cond, w_ada, b_ada):
    return jnp.split(jax.nn.silu(cond) @ w_ada + b_ada, ADA_CHUNKS, axis=-1)

def axial_rope(rows, head_dim):
    n_freq = head_dim // 4
    freqs = ROPE_THETA ** (-jnp.arange(n_freq, dtype=jnp.float32) / n_freq)
    row = jnp.repeat(jnp.arange(rows, dtype=jnp.float32), GRID_W)
    col = jnp.tile(jnp.arange(GRID_W, dtype=jnp.float32), rows)
    ang = jnp.concatenate([row[:, None] * freqs, col[:, None] * freqs], axis=-1)
    return jnp.cos(ang), jnp.sin(ang)

def apply_rope(x, cos, sin):
    half = x.shape[-1] // 2
    shape = (cos.shape[0],) + (1,) * (x.ndim - 3) + (half,)
    cos = cos.reshape(shape).astype(x.dtype)
    sin = sin.reshape(shape).astype(x.dtype)
    x1, x2 = x[..., :half], x[..., half:]
    return jnp.concatenate([x1 * cos - x2 * sin, x2 * cos + x1 * sin], axis=-1)

def split_kv(p_kv, k_norm_a, k_norm_b):
    b, n = p_kv.shape[:2]
    k_a, v_a, k_b, v_b = jnp.split(p_kv, [A_KV, 2 * A_KV, 2 * A_KV + B_QK], axis=-1)
    k_a = rms_norm_2(k_a.reshape(b, n, A_KV_HEADS, A_HEAD_DIM), k_norm_a)
    v_a = v_a.reshape(b, n, A_KV_HEADS, A_HEAD_DIM)
    k_b = rms_norm_2(k_b.reshape(b, n, B_HEADS, 2, B_HEAD_DIM), k_norm_b)
    v_b = v_b.reshape(b, n, B_HEADS, B_V_DIM)
    return k_a, v_a, k_b, v_b

def split_qg(p_qg, q_norm_a, q_norm_b):
    b, n = p_qg.shape[:2]
    q_a, q_b, g_a, g_b = jnp.split(p_qg, [A_Q, A_Q + B_QK, A_Q + B_QK + D_MODEL], axis=-1)
    q_a = rms_norm_2(q_a.reshape(b, n, A_HEADS, A_HEAD_DIM), q_norm_a)
    q_b = rms_norm_2(q_b.reshape(b, n, B_HEADS, 2, B_HEAD_DIM), q_norm_b)
    return q_a, q_b, g_a, g_b

def gqa(q, k, v):
    b, n, hq, d = q.shape
    hkv = k.shape[2]
    qg = q.reshape(b, n, hkv, hq // hkv, d)
    s = jnp.einsum('bnkgd,bmkd->bkgnm', qg, k).astype(jnp.float32) * (d ** -0.5)
    p = jax.nn.softmax(s, axis=-1).astype(v.dtype)
    o = jnp.einsum('bkgnm,bmkd->bnkgd', p, v)
    return o.reshape(b, n, hq * d)

def diff_attn(q, k, v, lam, lam_init, subln_g):
    b, n, h, _, dh = q.shape
    s = jnp.einsum('bnhid,bmhid->bhinm', q, k).astype(jnp.float32) * (dh ** -0.5)
    p = jax.nn.softmax(s, axis=-1)
    a = (p[:, :, 0] - lam * p[:, :, 1]).astype(v.dtype)
    o = jnp.einsum('bhnm,bmhe->bnhe', a, v)
    o = rms_norm_2(o, subln_g) * (1 - lam_init)
    return o.reshape(b, n, h * B_V_DIM)

def sweep_query_blocks(attn_fn, q):
    b, s = q.shape[:2]
    nblk = s // Q_BLOCK
    qb = jnp.moveaxis(q.reshape((b, nblk, Q_BLOCK) + q.shape[2:]), 1, 0)
    o = lax.map(attn_fn, qb)
    return jnp.moveaxis(o, 0, 1).reshape(b, s, o.shape[-1])

def merge_branches(o_a, o_b, g_a, g_b, w_br_a, w_br_b, w_out):
    merged = jax.nn.sigmoid(g_a) * (o_a @ w_br_a) + jax.nn.sigmoid(g_b) * (o_b @ w_br_b)
    return merged @ w_out

def swiglu_sublayer(x, shift, scale, gate, norm_g, w_ff_gate, w_ff_up, w_ff_down):
    h = modulate(rms_norm_2(x, norm_g), shift, scale)
    return x + gate * ((jax.nn.silu(h @ w_ff_gate) * (h @ w_ff_up)) @ w_ff_down)

def second_inputs(seed: int = 0) -> dict:
    key = jax.random.key(seed)
    ks = jax.random.split(key, 24)
    f32 = jnp.float32
    L = DEPTH

    def w(k, shape, fan_in, s=1.0):
        return jax.random.normal(k, shape, f32) * (s * fan_in ** -0.5)

    def gain(k, shape):
        return 1.0 + 0.05 * jax.random.normal(k, shape, f32)

    return {
        'x': jax.random.normal(ks[0], (BATCH, SEQ, D_MODEL), f32),
        'c': jax.random.normal(ks[1], (BATCH, D_MODEL), f32),
        'ctx': jax.random.normal(ks[2], (BATCH, CTX_LEN, D_MODEL), f32),
        'c_ctx': jax.random.normal(ks[3], (D_MODEL,), f32),
        'w_ada': w(ks[4], (L, D_MODEL, ADA_CHUNKS * D_MODEL), D_MODEL, 0.5),
        'b_ada': 0.02 * jax.random.normal(ks[5], (L, ADA_CHUNKS * D_MODEL), f32),
        'norm1_g': gain(ks[6], (L, D_MODEL)),
        'w_in': w(ks[7], (L, D_MODEL, IN_WIDTH_2), D_MODEL),
        'q_norm_a': gain(ks[8], (L, A_HEAD_DIM)),
        'k_norm_a': gain(ks[9], (L, A_HEAD_DIM)),
        'q_norm_b': gain(ks[10], (L, B_HEAD_DIM)),
        'k_norm_b': gain(ks[11], (L, B_HEAD_DIM)),
        'lam_q1': 0.1 * jax.random.normal(ks[12], (L, B_HEAD_DIM), f32),
        'lam_k1': 0.1 * jax.random.normal(ks[13], (L, B_HEAD_DIM), f32),
        'lam_q2': 0.1 * jax.random.normal(ks[14], (L, B_HEAD_DIM), f32),
        'lam_k2': 0.1 * jax.random.normal(ks[15], (L, B_HEAD_DIM), f32),
        'subln_g': gain(ks[16], (L, B_V_DIM)),
        'w_br_a': w(ks[17], (L, A_Q, D_MODEL), A_Q),
        'w_br_b': w(ks[18], (L, B_V, D_MODEL), B_V),
        'w_out': w(ks[19], (L, D_MODEL, D_MODEL), D_MODEL),
        'norm2_g': gain(ks[20], (L, D_MODEL)),
        'w_ff_gate': w(ks[21], (L, D_MODEL, D_FF_2), D_MODEL),
        'w_ff_up': w(ks[22], (L, D_MODEL, D_FF_2), D_MODEL),
        'w_ff_down': w(ks[23], (L, D_FF_2, D_MODEL), D_FF_2),
    }

def second_block(x, c, ctx, c_ctx, w_ada, b_ada, norm1_g, w_in, q_norm_a, k_norm_a, q_norm_b, k_norm_b,
              lam_q1, lam_k1, lam_q2, lam_k2, subln_g, w_br_a, w_br_b, w_out, norm2_g,
              w_ff_gate, w_ff_up, w_ff_down):
    rows = x.shape[1] // GRID_W
    cos_a, sin_a = axial_rope(rows, A_HEAD_DIM)
    cos_b, sin_b = axial_rope(rows, B_HEAD_DIM)

    for l in range(DEPTH):
        last = l == DEPTH - 1
        lam_init = 0.8 - 0.6 * math.exp(-0.3 * l)
        lam = (jnp.exp(jnp.sum(lam_q1[l].astype(jnp.float32) * lam_k1[l].astype(jnp.float32)))
               - jnp.exp(jnp.sum(lam_q2[l].astype(jnp.float32) * lam_k2[l].astype(jnp.float32)))
               + lam_init)
        m_lat = [m[:, None, :] for m in adaln(c, w_ada[l], b_ada[l])]
        m_ctx = adaln(c_ctx, w_ada[l], b_ada[l])
        w_in_l = w_in[l]

        hc = modulate(rms_norm_2(ctx, norm1_g[l]), m_ctx[0], m_ctx[1])
        pc = hc @ (w_in_l[:, :KV_WIDTH] if last else w_in_l)
        ka_c, va_c, kb_c, vb_c = split_kv(pc[..., :KV_WIDTH], k_norm_a[l], k_norm_b[l])

        h = modulate(rms_norm_2(x, norm1_g[l]), m_lat[0], m_lat[1])
        p = h @ w_in_l
        ka, va, kb, vb = split_kv(p[..., :KV_WIDTH], k_norm_a[l], k_norm_b[l])
        qa, qb, ga, gb = split_qg(p[..., KV_WIDTH:], q_norm_a[l], q_norm_b[l])
        qa = apply_rope(qa, cos_a, sin_a)
        ka = apply_rope(ka, cos_a, sin_a)
        qb = apply_rope(qb, cos_b, sin_b)
        kb = apply_rope(kb, cos_b, sin_b)

        ka_all = jnp.concatenate([ka_c, ka], axis=1)
        va_all = jnp.concatenate([va_c, va], axis=1)
        kb_all = jnp.concatenate([kb_c, kb], axis=1)
        vb_all = jnp.concatenate([vb_c, vb], axis=1)
        sg = subln_g[l]
        oa = sweep_query_blocks(lambda qblk: gqa(qblk, ka_all, va_all), qa)
        ob = sweep_query_blocks(lambda qblk: diff_attn(qblk, kb_all, vb_all, lam, lam_init, sg), qb)
        x_new = x + m_lat[2] * merge_branches(oa, ob, ga, gb, w_br_a[l], w_br_b[l], w_out[l])
        x_new = swiglu_sublayer(x_new, m_lat[3], m_lat[4], m_lat[5], norm2_g[l],
                                w_ff_gate[l], w_ff_up[l], w_ff_down[l])

        if not last:
            qa_c, qb_c, ga_c, gb_c = split_qg(pc[..., KV_WIDTH:], q_norm_a[l], q_norm_b[l])
            oa_c = gqa(qa_c, ka_c, va_c)
            ob_c = diff_attn(qb_c, kb_c, vb_c, lam, lam_init, sg)
            ctx = ctx + m_ctx[2] * merge_branches(oa_c, ob_c, ga_c, gb_c, w_br_a[l], w_br_b[l], w_out[l])
            ctx = swiglu_sublayer(ctx, m_ctx[3], m_ctx[4], m_ctx[5], norm2_g[l],
                                  w_ff_gate[l], w_ff_up[l], w_ff_down[l])
        x = x_new
    return x


def setup_inputs(seed=0):
    out = dict(first_inputs(seed))
    for name, value in second_inputs(seed + 1).items():
        if name != "x":
            out[name + "_2"] = value
    return out


def reference(
    x, pre_mix_g, w_in, rel_bias, pool_w, pool_scale, w_o, post_mix_g, pre_ffn_g, w_up, conv_w,
    conv_b, w_down, post_ffn_g, c_2, ctx_2, c_ctx_2, w_ada_2, b_ada_2, norm1_g_2, w_in_2,
    q_norm_a_2, k_norm_a_2, q_norm_b_2, k_norm_b_2, lam_q1_2, lam_k1_2, lam_q2_2, lam_k2_2,
    subln_g_2, w_br_a_2, w_br_b_2, w_out_2, norm2_g_2, w_ff_gate_2, w_ff_up_2, w_ff_down_2,
):
    x = first_block(
        x, pre_mix_g, w_in, rel_bias, pool_w, pool_scale, w_o, post_mix_g, pre_ffn_g, w_up,
        conv_w, conv_b, w_down, post_ffn_g,
    )
    return second_block(
        x, c_2, ctx_2, c_ctx_2, w_ada_2, b_ada_2, norm1_g_2, w_in_2, q_norm_a_2, k_norm_a_2,
        q_norm_b_2, k_norm_b_2, lam_q1_2, lam_k1_2, lam_q2_2, lam_k2_2, subln_g_2, w_br_a_2,
        w_br_b_2, w_out_2, norm2_g_2, w_ff_gate_2, w_ff_up_2, w_ff_down_2,
    )


_drawn_inputs = setup_inputs


def setup_inputs(seed=0):
    import zlib

    import numpy as np

    out = dict(_drawn_inputs(seed))
    spreads = {}
    factors = {'pre_mix_g': 3.209,
     'rel_bias': 4.182,
     'pool_scale': 3.354,
     'post_mix_g': 3.404,
     'pre_ffn_g': 3.423,
     'conv_b': 6.772,
     'post_ffn_g': 4.788,
     'ctx_2': 3.079,
     'b_ada_2': 4.583,
     'norm1_g_2': 8.0,
     'q_norm_a_2': 8.0,
     'k_norm_a_2': 8.0,
     'q_norm_b_2': 8.0,
     'k_norm_b_2': 8.0,
     'lam_q1_2': 8.0,
     'lam_k1_2': 6.489,
     'lam_q2_2': 8.0,
     'lam_k2_2': 8.0,
     'subln_g_2': 29.412,
     'norm2_g_2': 6.624}
    for name, (base, spread) in spreads.items():
        noise = np.random.default_rng([zlib.crc32(name.encode()), seed]).standard_normal(out[name].shape)
        drawn = base * np.exp(spread * noise) if base else spread * noise
        out[name] = __import__('jax').numpy.asarray(drawn.astype(out[name].dtype))
    for name, factor in factors.items():
        out[name] = (out[name] * factor).astype(out[name].dtype)
    return out
```

```python
from contextlib import ExitStack
import math

import numpy as np
import concourse.bass as bass
from concourse import mybir

F32 = mybir.dt.float32
F32R = mybir.dt.float32r
ALU = mybir.AluOpType
ACT = mybir.ActivationFunctionType
AX = mybir.AxisListType
ds = bass.ds

P = 128
S = 256
D = 2048
KT = D // P
DFF = 5632
FT = DFF // P
UK = 4
GW = 256
RING = 4
HD = 128
H1 = 8
HA, HB = 16, 8
EPS = 1e-6
WINDOWS = (2, 4, 8, 16)
FIRST_HALF = 24
KVW, QW, GATEW = 3072, 3072, 4096
ADA_CTX = 16
ADA_ITEMS = 64
LAM_INIT = 0.8 - 0.6 * math.exp(-0.3 * 0)

VEC = {}
_at = 0
for _name, _n in (("pre_mix", KT), ("post_mix", KT), ("pre_ffn", KT), ("post_ffn", KT), ("norm1", KT), ("norm2", KT),
                  ("conv_w", 3 * 2 * FT), ("conv_b", 2 * FT), ("pool_scale", 8), ("q_a", 1), ("k_a", 1), ("q_b", 1),
                  ("k_b", 1), ("cond", 2 * KT), ("lam", 4), ("b_ada", 2 * ADA_ITEMS), ("subln", 1)):
    VEC[_name] = _at
    _at += _n
NVEC = _at

C_FLIP, C_ROPE = 256, 768
NCONST = C_ROPE + 4 * S


class Stage:

    def __init__(self, name, src, groups, units, kind, per_body=2, ada=0, who=0, act=False, tile0=0, feat0=0, op=None, after=None):
        self.name, self.src, self.G, self.U, self.kind = name, src, groups, units, kind
        self.GB, self.ada, self.who, self.act = per_body, ada, who, act
        self.tile0, self.feat0 = tile0, feat0
        self.op = op
        self.after = after
        self.bodies = groups // per_body
        self.upb = units * per_body
        assert groups % per_body == 0 and self.upb % RING == 0


V_STEPS = {"scale": 1, "mix_out": 3, "conv": (5, 8), "down1": 0, "down2": 4, "kv": 0, "q": 0, "gate": 0,
           "branch_a": 1, "branch_b": 2, "out": 5, "glu": (0, 3), "down_x": 2}
A_STEPS = {"conv": (3, 2), "gate": (1, 1), "glu": (1, 0)}


def steps(table, kind, gb):
    n = table.get(kind, 0)
    return n[gb % 2] if isinstance(n, tuple) else n


def number(stages):
    u = g = v = a = t = n = 0
    for st in stages:
        st.ub, st.gb, st.vb, st.ab, st.tb, st.ib = u, g, v, a, t, n
        st.vpb = sum(steps(V_STEPS, st.kind, i) for i in range(st.GB))
        st.apb = sum(steps(A_STEPS, st.kind, i) for i in range(st.GB))
        st.tpb = 0 if st.kind == "kv" else st.GB
        u += st.upb * st.bodies
        g += st.G
        v += st.vpb * st.bodies
        a += st.apb * st.bodies
        t += st.tpb * st.bodies
        n += st.ada * st.bodies
    assert n == ADA_ITEMS
    return stages


def build(nc, xT, ctxT, vec, cst, rel, w_in, pool_w, w_o, w_up, w_down, w_ada, w_in2, w_bra, w_brb, w_out2,
          w_fg, w_fu, w_fd, out):
    km = lambda w: w.rearrange("(k p) n -> p k n", p=P)
    W = {k: km(v) for k, v in dict(w_in=w_in, w_o=w_o, w_up=w_up, w_down=w_down, w_in2=w_in2, bra=w_bra, brb=w_brb,
                                   out=w_out2, fg=w_fg, fu=w_fu, fd=w_fd).items()}
    ada_src = km(w_ada)

    def cols(w, k, c0, stride):
        return lambda b, GB, gb, u: W[w][:, k + UK * u:k + UK * u + UK, ds((b * GB + gb) * stride + c0, GW)]

    def pairs(wg, wu, g0, u0):
        return lambda b, GB, gb, u: W[(wg, wu)[gb % 2]][:, UK * u:UK * u + UK,
                                                          ds(b * GW + (g0, u0)[gb % 2], GW)]

    h1c = FIRST_HALF // 2 * GW
    n1, n2 = FIRST_HALF // 2, (FT - FIRST_HALF) // 2
    st_in = Stage("w_in", cols("w_in", 0, 0, GW), 16, 4, "scale", ada=1, op=0)
    st_o = Stage("w_o", cols("w_o", 0, 0, GW), 8, 4, "mix_out", ada=1, op=16)
    st_up1a = Stage("up1a", pairs("w_up", "w_up", 0, DFF), 8, 4, "conv", ada=1, op=32)
    st_up1b = Stage("up1b", pairs("w_up", "w_up", 4 * GW, DFF + 4 * GW), 2 * n1 - 8, 4, "conv", ada=1, tile0=8, feat0=8)
    st_dn1 = Stage("down1", cols("w_down", 0, 0, GW), 8, 6, "down1", act=True, after=st_up1a)
    st_up2 = Stage("up2", pairs("w_up", "w_up", h1c, DFF + h1c), 2 * n2, 4, "conv", ada=1, feat0=FIRST_HALF)
    st_dn2 = Stage("down2", cols("w_down", FIRST_HALF, 0, GW), 8, 5, "down2", per_body=4, act=True, after=st_up2)
    st_kv = Stage("kv", cols("w_in2", 0, 0, GW), KVW // GW, 4, "kv", op=64)
    st_q1 = Stage("q_first", cols("w_in2", 0, KVW, GW), 4, 4, "q", ada=1, tile0=8)
    st_q2 = Stage("q_rest", cols("w_in2", 0, KVW + 1024, GW), 8, 4, "q", ada=1, tile0=32)
    st_ga = Stage("gate_a", cols("w_in2", 0, KVW + QW, GW), 8, 4, "gate", ada=1, tile0=16)
    st_gb = Stage("gate_b", cols("w_in2", 0, KVW + QW + D, GW), 8, 4, "gate", ada=1, tile0=48)
    st_ba = Stage("branch_a", cols("bra", 0, 0, GW), 8, 4, "branch_a", ada=1, op=88)
    st_bb = Stage("branch_b", cols("brb", 0, 0, GW), 8, 2, "branch_b", per_body=4, ada=1, who=1)
    st_out = Stage("out", cols("out", 0, 0, GW), 8, 4, "out", ada=1, op=104)
    st_u1a = Stage("glu1a", pairs("fg", "fu", 0, 0), 12, 4, "glu", ada=1, op=120)
    st_u1b = Stage("glu1b", pairs("fg", "fu", 6 * GW, 6 * GW), 2 * n1 - 12, 4, "glu", tile0=12)
    st_d1 = Stage("fdown1", cols("fd", 0, 0, GW), 8, 6, "down_x", act=True, after=st_u1a)
    st_u2 = Stage("glu2", pairs("fg", "fu", h1c, h1c), 2 * n2, 4, "glu")
    st_d2 = Stage("fdown2", cols("fd", FIRST_HALF, 0, GW), 8, 5, "down_x", per_body=4, act=True, after=st_u2)
    stages = number([st_in, st_o, st_up1a, st_up1b, st_dn1, st_up2, st_dn2, st_kv, st_q1, st_q2, st_ga, st_gb, st_ba, st_bb,
                     st_out, st_u1a, st_u1b, st_d1, st_u2, st_d2])

    with ExitStack() as ctx:
        place = {"at": 16512}

        def here(n_bytes):
            at = place["at"]
            place["at"] += n_bytes
            return at

        def sb(name, shape, dt, at):
            return nc.alloc_sbuf_tensor_at(name, shape, dt, offset=at)

        unit_b = UK * GW * 4
        raw = [sb(f"raw{i}", [P, UK, GW], F32, here(unit_b)) for i in range(RING)]
        whi = [sb(f"whi{i}", [P, UK, GW], F32R, here(unit_b)) for i in range(RING)]
        wlo = [sb(f"wlo{i}", [P, UK, GW], F32R, here(unit_b)) for i in range(RING)]
        X = sb("x_res", [P, KT, S], F32, here(KT * S * 4))
        xc_at = here(KT * 4 * S * 4)
        XC = sb("operand", [P, KT, 2, 2, S], F32R, xc_at)
        XC32 = sb("operand_scratch", [P, KT, 2, 2, S], F32, xc_at)
        r_at = here(72 * S * 4)
        R = sb("tiles", [P, 72, S], F32, r_at)
        FH = sb("ffn_act", [P, FIRST_HALF, 2, S], F32R, r_at)
        Zp = sb("conv_in", [P, 2, S + 2], F32, r_at + 48 * 1024)
        Cb = sb("conv_out", [P, 2, S], F32, r_at + 48 * 1024 + 2 * (S + 2) * 4 + 16)
        Gb = sb("gate_act", [P, 2, S], F32, r_at + 48 * 1024 + 2 * (S + 2) * 4 + 16 + 2048)
        T = sb("tmp", [P, 2, S], F32, here(2 * S * 4))
        IO = sb("ident_ones", [P, 256], F32, here(1024))
        RS = sb("rstd", [P, S], F32, here(S * 4))
        V = sb("vectors", [P, NVEC], F32, here(NVEC * 4 + 28 & ~31))
        MOD = sb("mods", [P, 2 * ADA_ITEMS], F32, here(2 * ADA_ITEMS * 4))
        CS = sb("cond_silu", [P, 2 * KT], F32, here(2 * KT * 4))
        GS = sb("gain_scale", [P, KT], F32, here(KT * 4))
        SM = sb("small", [P, 40], F32, here(160))
        assert place["at"] <= nc.sbuf_usable_end, (place["at"], nc.sbuf_usable_end)
        ident, ones = IO[:, 0:128], IO[:, 128:256]
        scr = lambda kt: XC32[:, kt, :, 1, :]
        ada_raw = [lambda k, s=s: XC32[:, 8 + 2 * s + k // 2, k % 2, 1, :] for s in range(2)]
        ada_acc = lambda par: XC32[:, 12, par, 1, :]
        flip = XC32[:, 13, 0, 1, 0:128]
        halves = XC32[:, 13, 0, 1, 128:256]
        hankel = lambda h: XC32[:, h // 2, h % 2, 1, :]
        poolfix = XC32[:, 13, 1, 1, :]
        EPS_C, NEGLAM = 20, 21
        Yt = 56

        PS = ctx.enter_context(nc.psum_tensor("acc", [P, 2, 2, 512], F32))
        TP = ctx.enter_context(nc.psum_tensor("turned", [P, 2, 512], F32))
        NB = ctx.enter_context(nc.psum_tensor("sums", [P, 512], F32))
        AB = ctx.enter_context(nc.psum_tensor("ada_sums", [P, 512], F32))

        def sem(name):
            return ctx.enter_context(nc.semaphore(name))

        raw_in = [sem(f"raw_in{i}") for i in range(RING)]
        hi_done = sem("hi_done")
        lo_done = sem("lo_done")
        used = sem("used")
        tmp_done = sem("tmp_done")
        evac_done = sem("evac_done")
        vstep = sem("vstep")
        astep = sem("astep")
        ada_in = [sem("ada_in0"), sem("ada_in1")]
        ada_ops = sem("ada_ops")
        ada_red = sem("ada_red")
        mods_done = sem("mods_done")
        silu_done = sem("silu_done")
        in_x, in_vec, in_cst, in_att, in_ctx, in_rope = (sem(f"in_{n}") for n in ("x", "vec", "cst", "att", "ctx", "rope"))
        ready0 = sem("small_consts")
        sq_ready, acc_ready, sum_ready, root_ready, rstd_ready = (
            sem(n) for n in ("squares_ready", "acc_ready", "sum_ready", "root_ready", "rstd_ready"))
        cleared = sem("acc_cleared")
        op_hi = sem("operand_hi")
        opnd = sem("operand_ready")
        x_new = sem("residual_tile")
        y_normed = sem("normed_chunk")
        mod_t, mod_v, mod_hi, gains = sem("mod_scaled"), sem("mod_value"), sem("mod_hi"), sem("gains")
        q_scaled, vt_turned, vt_copied, masked, pooled, poolstep = (
            sem(n) for n in ("q_scaled", "vt_turned", "vt_copied", "masked", "pooled", "poolstep"))
        scored, neg_max, exped, inverse, probs, turned, pt_copied, summed = (
            sem(n) for n in ("scored", "neg_max", "exped", "inverse", "probs", "turned", "pt_copied", "summed"))
        v2_turned, v2_copied = sem("v2_turned"), sem("v2_copied")
        n_sq, n_sum, n_root, n_inv, n_scaled, n_swap, n_t1, n_t2, n_rope = (
            sem(n) for n in ("n_sq", "n_sum", "n_root", "n_inv", "n_scaled", "n_swap", "n_t1", "n_t2", "n_rope"))
        a_scored, a_neg, a_exp, a_inv, a_prob, a_turned, a_copied, a_summed, a_out = (
            sem(n) for n in ("a_scored", "a_neg", "a_exp", "a_inv", "a_prob", "a_turned", "a_copied", "a_summed",
                             "a_out"))
        b_scored, b_neg, b_exp, b_inv, b_nl, b_p1, b_prob, b_turned, b_copied, b_summed, b_out = (
            sem(n) for n in ("b_scored", "b_neg", "b_exp", "b_inv", "b_nl", "b_p1", "b_prob", "b_turned", "b_copied",
                             "b_summed", "b_out"))
        lam_exp, lam_sum, lam_vec = sem("lam_exp"), sem("lam_sum"), sem("lam_vec")
        o_sq, o_sum, o_root, o_inv, o_norm = (sem(n) for n in ("o_sq", "o_sum", "o_root", "o_inv", "o_norm"))
        split_hi = sem("split_hi")
        out_stored = sem("out_stored")

        def unit(st, b, j):
            return b * st.upb + (st.ub + j)

        def group(st, b, gb):
            return b * st.GB + (st.gb + gb)

        def vst(st, b, gb, i):
            return b * st.vpb + (st.vb + sum(steps(V_STEPS, st.kind, x) for x in range(gb)) + i + 1)

        def ast(st, b, gb, i):
            return b * st.apb + (st.ab + sum(steps(A_STEPS, st.kind, x) for x in range(gb)) + i + 1)

        def tgr(st, b, gb):
            return b * st.tpb + (st.tb + gb + 1)

        def filled(st, b, j):
            return b * (st.upb // RING * 16) + ((st.ub + j) // RING + 1) * 16

        def groups_before(st):
            return st.gb + 2

        def evacuated(st):
            return st.gb + st.G + 2

        def used_all(st):
            return st.ub + st.upb * st.bodies + RING

        def rep(ap, *n):
            return bass.AP(ap.tensor, ap.offset, [ap.ap[0]] + [[0, x] for x in n] + [ap.ap[-1]])

        ACC = (1, 2, 3, 5, 6, 7, 8)

        CH = [(0, 0, 1), (4, 0, 1), (8, 0, 0), (12, 0, 0), (32, 0, 0), (36, 0, 0),
              (16, 1, 1), (20, 1, 1), (24, 1, 1), (28, 1, 1), (40, 1, 0), (44, 1, 0)]
        quad = lambda ap: ap.rearrange("p (k a) n -> p k a n", a=2)
        sqb = lambda c: XC32[:, 6 * (c % 2):6 * (c % 2) + 2, :, 1, :]
        swapb, t1b = XC32[:, 2:4, :, 1, :], XC32[:, 4:6, :, 1, :]
        qa_tile = lambda h: 8 + h if h < 8 else 24 + h
        v_at = lambda j, t: R[:, 48 + 6 * t + j // 2, 128 * (j % 2):128 * (j % 2) + 128]
        v_cols = R[:, 48:72, :].rearrange("p (t j) (a d) -> p t j a d", t=4, a=2)
        NA, NB_ = 2 * HA, 2 * HB
        O_SRC = (8, 12, 32, 36)

        block = ctx.enter_context(nc.Block())

        @block.sync
        def _(sp):
            for st in stages:
                with sp.Fori(0, st.bodies) as b:
                    for j in range(st.upb):
                        gb, u = divmod(j, st.U)
                        sp.wait_ge(lo_done, unit(st, b, j) + 1)
                        sp.dma_start(raw[j % RING][:], st.src(b, st.GB, gb, u)).then_inc(raw_in[j % RING], 16)
            sp.wait_ge(evac_done, evacuated(st_d2))
            sp.dma_start(out, X[:]).then_inc(out_stored, 16)
            sp.wait_ge(out_stored, 16)

        @block.gpsimd
        def _(pool):
            pool.wait_ge(in_att, 64)
            pool.memset(XC32[64:128, 0:4, :, 1, 192:256], -1e30).then_inc(masked, 1)

            def item(n, column):
                for u in range(4):
                    pool.wait_ge(ada_ops, n * 16 + (4 * u + 4))
                    for h in range(2):
                        pool.dma_start(XC32[:, 8 + 2 * (u % 2) + h, :, 1, :],
                                       ada_src[:, UK * u + 2 * h:UK * u + 2 * h + 2, ds(column, GW)]
                                       ).then_inc(ada_in[u % 2], 16)

            def items(lo, hi):
                if lo < ADA_CTX:
                    with pool.Fori(lo, min(hi, ADA_CTX)) as n:
                        item(n, n * GW)
                if hi > ADA_CTX:
                    with pool.Fori(max(lo, ADA_CTX), hi) as n:
                        item(n, n * GW - ADA_CTX * GW)

            items(0, st_o.ib)

            pool.wait_ge(evac_done, evacuated(st_in))
            pool.wait_ge(in_cst, 48)
            pool.wait_ge(masked, 1)
            count = 0

            def step(ins):
                nonlocal count
                count += 1
                ins.then_inc(poolstep, 1)

            for g, w in enumerate(WINDOWS):
                u_t = R[:, 24 + 2 * g:26 + 2 * g, :]
                src, d, turn = u_t, 1, 0
                while d < w:
                    dst = R[:, 52 + 2 * turn:54 + 2 * turn, :]
                    if count:
                        pool.wait_ge(poolstep, count)
                    step(pool.tensor_copy(dst[:, :, 0:d], src[:, :, 0:d]))
                    step(pool.tensor_tensor(dst[:, :, d:S], src[:, :, d:S], src[:, :, 0:S - d], ALU.add))
                    src, d, turn = dst, 2 * d, 1 - turn
                pool.wait_ge(poolstep, count)
                fix = poolfix[:, 32 * g:32 * g + 32].rearrange("p (a t) -> p a t", a=2)[:, :, 0:w - 1]
                step(pool.tensor_tensor(src[:, :, 0:w - 1], src[:, :, 0:w - 1], fix, ALU.mult))
                pool.wait_ge(poolstep, count)
                step(pool.tensor_scalar(src, src, 1.0 / w, None, ALU.mult))
                pool.wait_ge(poolstep, count)
                step(pool.tensor_tensor(u_t, src, u_t, ALU.subtract))
                pool.wait_ge(poolstep, count)
                pool.sem_inc(pooled, 1)

            items(st_o.ib, st_q1.ib)
            pool.wait_ge(ada_ops, st_q1.ib * 16 + 8)
            pool.wait_ge(ada_red, st_q1.ib + 1)
            for who_half in range(2):
                pool.dma_start(XC32[:, 8 * who_half:8 * who_half + 8, 0, 1, :],
                               ctxT[:, 8 * who_half:8 * who_half + 8, :]).then_inc(in_ctx, 16)
            pool.wait_ge(used, used_all(st_kv))
            for kt in range(3):
                pool.dma_start(XC32[:, 13 + kt, :, 1, :], cst[:, C_FLIP + 512 * kt:C_FLIP + 512 * kt + 512].rearrange(
                    "p (a n) -> p a n", a=2)).then_inc(in_rope, 16)
            items(st_q1.ib, ADA_ITEMS)
            pool.wait_ge(in_rope, 48)

        @block.scalar
        def _(act):
            def hi(st, b, j):
                act.wait_ge(raw_in[j % RING], filled(st, b, j))
                act.wait_ge(used, unit(st, b, j) + 1)
                act.activation(whi[j % RING][:], raw[j % RING][:], ACT.Copy).then_inc(hi_done, 1)

            def tmp(st, b, gb):
                act.wait_ge(used, unit(st, b, st.U * (gb + 1)) + RING)
                act.wait_ge(evac_done, group(st, b, gb) + 2)
                if st.kind in ("gate", "glu"):
                    act.wait_ge(astep, ast(st, b, gb, -1))
                act.activation(T[:], PS[:, gb % 2, :, S:2 * S], ACT.Copy).then_inc(tmp_done, 1)

            def post(st, b, gb):
                g = group(st, b, gb)
                if st.kind == "conv":
                    t0 = b * 2 + (FT * (gb % 2) + st.feat0)
                    act.wait_ge(vstep, vst(st, b, gb, 1))
                    if gb % 2:
                        act.wait_ge(astep, ast(st, b, gb, -1))
                    for m in range(2):
                        act.activation(Cb[:, m, :], Zp[:, m, 2:S + 2], ACT.Identity,
                                       bias=V[:, ds(t0 + (VEC["conv_b"] + m), 1)],
                                       scale=V[:, ds(t0 + (VEC["conv_w"] + 4 * FT + m), 1)]).then_inc(astep, 1)
                    if gb % 2 == 0:
                        act.wait_ge(evac_done, g + 3)
                        act.activation(Gb[:], Cb[:], ACT.Gelu_apprx_tanh).then_inc(astep, 1)
                elif st.kind == "gate":
                    act.wait_ge(evac_done, g + 3)
                    act.activation(R[:, ds(b * 4 + (st.tile0 + 2 * gb), 2), :], T[:], ACT.Sigmoid).then_inc(astep, 1)
                elif st.kind == "glu" and gb % 2 == 0:
                    act.wait_ge(evac_done, g + 3)
                    act.activation(Gb[:], T[:], ACT.Silu).then_inc(astep, 1)

            def body(st, b, drop=0):
                for j in range(RING, RING + st.upb - drop):
                    hi(st, b, j)
                    if (j + 1 - RING) % st.U == 0 and st.kind != "kv":
                        tmp(st, b, (j + 1 - RING) // st.U - 1)
                        post(st, b, (j + 1 - RING) // st.U - 1)
                if drop:
                    for gb in range((st.upb - drop) // st.U, st.GB):
                        tmp(st, b, gb)
                        post(st, b, gb)

            def run(st, last=False):
                if st.ab:
                    act.wait_ge(astep, st.ab)
                with act.Fori(0, st.bodies - last) as b:
                    body(st, b)
                if last:
                    body(st, st.bodies - 1, drop=RING)

            def root(i, n=D):
                act.wait_ge(sum_ready, i + 1)
                act.activation(RS[:], NB[:, 0:S], ACT.Sqrt, bias=SM[:, EPS_C:EPS_C + 1],
                               scale=1.0 / n).then_inc(root_ready, 1)

            act.dma_start(X[:], xT).then_inc(in_x, 16)
            act.dma_start(V[:], vec).then_inc(in_vec, 16)
            act.dma_start(IO[:], cst[:, 0:256]).then_inc(in_cst, 16)
            for kt in range(4):
                act.dma_start(XC32[:, kt, :, 1, :], bass.AP(
                    rel.tensor, 2 * kt * rel.shape[1], [[1, P], [rel.shape[1], 2], [1, S]])).then_inc(in_att, 16)
            act.dma_start(XC32[:, 13, :, 1, :], cst[:, C_FLIP:C_FLIP + 512].rearrange(
                "p (a n) -> p a n", a=2)).then_inc(in_cst, 16)
            act.dma_start(R[:, 32:40, :], pool_w).then_inc(in_cst, 16)

            act.wait_ge(in_vec, 16)
            act.activation(CS[:], V[:, VEC["cond"]:VEC["cond"] + 2 * KT], ACT.Silu).then_inc(silu_done, 1)
            act.wait_ge(in_x, 16)
            for kt in range(KT):
                act.activation(XC[:, kt, 0, 0, :], X[:, kt, :], ACT.Copy,
                               scale=V[:, VEC["pre_mix"] + kt:VEC["pre_mix"] + kt + 1]).then_inc(op_hi, 1)
            for j in range(RING):
                hi(st_in, 0, j)
            act.activation(R[:, 0:KT, :], X[:], ACT.Square).then_inc(sq_ready, 1)
            act.wait_ge(cleared, 1)
            root(0)
            run(st_in)

            act.wait_ge(evac_done, evacuated(st_in))
            for j in range(4):
                act.wait_ge(vt_turned, j + 1)
                act.activation(R[:, 40 + 2 * j:42 + 2 * j, :], TP[:, j % 2, :].rearrange("p (a n) -> p a n", a=2),
                               ACT.Copy).then_inc(vt_copied, 1)
            N = 2 * H1
            for i in range(N + 3):
                if i < N:
                    w = 128 * (i % 2 + 1)
                    act.wait_ge(neg_max, i + 1)
                    if i >= 2:
                        act.wait_ge(turned, i - 1)
                    act.activation(R[:, 48 + i % 2, 0:w], PS[:, i % 2, 0, 0:w], ACT.Exp, bias=SM[:, i % 2:i % 2 + 1],
                                   accum_out=SM[:, 2 + i % 2:3 + i % 2]).then_inc(exped, 1)
                if 1 <= i <= N:
                    n = i - 1
                    w = 128 * (n % 2 + 1)
                    act.wait_ge(turned, n + 1)
                    if n >= 2:
                        act.wait_ge(summed, n - 1)
                    act.activation(R[:, 50 + n % 2, 0:w], TP[:, n % 2, 0:w], ACT.Copy).then_inc(pt_copied, 1)
                if i >= 3 and i % 2 == 1:
                    h = (i - 3) // 2
                    act.wait_ge(summed, 2 * h + 2)
                    act.activation(XC[:, h, 0, 0, :], PS[:, h % 2, 1, 0:S], ACT.Copy).then_inc(op_hi, 1)
            for j in range(8):
                act.wait_ge(summed, N + j + 1)
                act.activation(XC[:, 8 + j, 0, 0, :], PS[:, j % 2, 1, 0:S], ACT.Copy,
                               scale=V[:, VEC["pool_scale"] + j:VEC["pool_scale"] + j + 1]).then_inc(op_hi, 1)
            run(st_o)

            root(1)
            for kt in range(KT):
                act.wait_ge(x_new, kt + 1)
                act.activation(XC[:, kt, 0, 0, :], X[:, kt, :], ACT.Copy,
                               scale=V[:, VEC["pre_ffn"] + kt:VEC["pre_ffn"] + kt + 1]).then_inc(op_hi, 1)
            act.activation(R[:, Yt:Yt + KT, :], X[:], ACT.Square).then_inc(sq_ready, 1)
            root(2)
            run(st_up1a)
            run(st_up1b)
            run(st_dn1)
            run(st_up2)

            act.wait_ge(in_ctx, 32)
            act.wait_ge(evac_done, evacuated(st_up2))
            for c in range(2):
                if c:
                    act.wait_ge(acc_ready, 4)
                act.activation(R[:, 48:56, :], XC32[:, 8 * c:8 * c + 8, 0, 1, :], ACT.Square).then_inc(sq_ready, 1)
            root(3)

            def modulated_hi(m, who):
                for c in range(4):
                    act.wait_ge(mod_v, 4 * m + c + 1)
                    act.activation(XC[:, 4 * c:4 * c + 4, 0, who, :], XC32[:, 4 * c:4 * c + 4, 1, who, :],
                                   ACT.Copy).then_inc(mod_hi, 1)

            modulated_hi(0, 1)
            run(st_dn2)

            root(4)
            act.wait_ge(x_new, 2 * KT)
            act.activation(R[:, Yt:Yt + KT, :], X[:], ACT.Square).then_inc(sq_ready, 1)
            root(5)
            modulated_hi(1, 0)
            run(st_kv)
            for j in range(12):
                act.wait_ge(v2_turned, j + 1)
                act.activation(v_cols[:, :, j // 2, j % 2, :], TP[:, j % 2, :].rearrange("p (t d) -> p t d", t=4),
                               ACT.Copy).then_inc(v2_copied, 1)
            run(st_q1)
            run(st_q2)

            act.wait_ge(lam_sum, 1)
            act.activation(SM[:, 22:24], NB[:, 0:2], ACT.Exp).then_inc(lam_exp, 1)
            act.wait_ge(evac_done, evacuated(st_q2))
            for c in range(len(CH) + 1):
                if c < len(CH):
                    if c >= 2:
                        act.wait_ge(n_scaled, c - 1)
                    act.activation(sqb(c), quad(R[:, CH[c][0]:CH[c][0] + 4, :]), ACT.Square).then_inc(n_sq, 1)
                    act.wait_ge(n_sum, c + 1)
                    act.activation(sqb(c), PS[:, c % 2, :, :].rearrange("p k (a n) -> p k a n", a=2), ACT.Sqrt,
                                   bias=SM[:, EPS_C:EPS_C + 1], scale=1.0 / (64 if CH[c][1] else HD)
                                   ).then_inc(n_root, 1)
                if c >= 1:
                    t, br, is_k = CH[c - 1]
                    act.wait_ge(n_scaled, c)
                    if c >= 2:
                        act.wait_ge(n_rope, c - 1)
                    s = 32 if br else 64
                    for p in range(0, P, 2 * s):
                        for x, y in ((p, p + s), (p + s, p)):
                            src = quad(R[y:y + s, t:t + 4, :])
                            dst = swapb[x:x + s]
                            if is_k:
                                src, dst = src[:, :, 0, :], dst[:, :, 0, :]
                            last = act.activation(dst, src, ACT.Copy)
                    last.then_inc(n_swap, 1)

            for i in range(NA + 3):
                if i < NA:
                    act.wait_ge(a_neg, i + 1)
                    if i >= 2:
                        act.wait_ge(a_turned, i - 1)
                    act.activation(scr(i % 2), PS[:, i % 2, 0, :].rearrange("p (a n) -> p a n", a=2), ACT.Exp,
                                   bias=SM[:, i % 2:i % 2 + 1], accum_out=SM[:, 2 + i % 2:3 + i % 2]).then_inc(a_exp, 1)
                if 1 <= i <= NA:
                    n = i - 1
                    act.wait_ge(a_turned, n + 1)
                    if n >= 2:
                        act.wait_ge(a_summed, n - 1)
                    act.activation(scr(2 + n % 2), TP[:, n % 2, :].rearrange("p (a n) -> p a n", a=2),
                                   ACT.Copy).then_inc(a_copied, 1)
                if i >= 3 and i % 2 == 1:
                    h = (i - 3) // 2
                    act.wait_ge(a_summed, 2 * h + 2)
                    act.activation(R[:, qa_tile(h), :], PS[:, h % 2, 1, 0:S], ACT.Copy).then_inc(a_out, 1)
            for i in range(NB_ + 3):
                if i < NB_:
                    act.wait_ge(b_neg, i + 1)
                    if i >= 2:
                        act.wait_ge(b_turned, i - 1)
                    for x in range(2):
                        e = 2 * (i % 2) + x
                        act.activation(scr(e), PS[:, i % 2, x, :].rearrange("p (a n) -> p a n", a=2), ACT.Exp,
                                       bias=SM[:, 6 + e:7 + e], accum_out=SM[:, 10 + e:11 + e]).then_inc(b_exp, 1)
                if 1 <= i <= NB_:
                    n = i - 1
                    act.wait_ge(b_turned, n + 1)
                    if n >= 2:
                        act.wait_ge(b_summed, n - 1)
                    act.activation(scr(4 + n % 2), TP[:, n % 2, :].rearrange("p (a n) -> p a n", a=2),
                                   ACT.Copy).then_inc(b_copied, 1)
                if i >= 3 and i % 2 == 1:
                    h = (i - 3) // 2
                    act.wait_ge(b_summed, 2 * h + 2)
                    act.activation(R[:, 40 + h, :], (NB, AB)[h % 2][:, 0:S], ACT.Copy).then_inc(b_out, 1)
            act.wait_ge(b_out, HB)
            act.activation(R[:, 16:24, :], R[:, 40:48, :], ACT.Square).then_inc(o_sq, 1)
            act.wait_ge(o_sum, 1)
            act.activation(R[:, 24:32, :], PS[:].rearrange("p a m (h n) -> p (a m h) n", h=2), ACT.Sqrt,
                           bias=SM[:, EPS_C:EPS_C + 1], scale=1.0 / HD).then_inc(o_root, 1)
            act.wait_ge(o_norm, 1)
            for c in range(2):
                act.activation(XC[:, 4 * c:4 * c + 4, 0, 1, :], R[:, 40 + 4 * c:44 + 4 * c, :],
                               ACT.Copy).then_inc(split_hi, 1)
            run(st_ga)
            run(st_gb)
            for c in range(4):
                act.activation(XC[:, 4 * c:4 * c + 4, 0, 0, :], R[:, O_SRC[c]:O_SRC[c] + 4, :],
                               ACT.Copy).then_inc(split_hi, 1)
            run(st_ba)
            run(st_bb)
            act.wait_ge(evac_done, evacuated(st_bb))
            for c in range(4):
                act.activation(XC[:, 4 * c:4 * c + 4, 0, 0, :], R[:, 16 + 4 * c:20 + 4 * c, :],
                               ACT.Copy).then_inc(split_hi, 1)
            run(st_out)
            root(6)
            modulated_hi(2, 0)
            run(st_u1a)
            run(st_u1b)
            run(st_d1)
            run(st_u2)
            run(st_d2, last=True)

        @block.vector
        def _(dve):
            def lo(st, b, j):
                dve.wait_ge(hi_done, unit(st, b, j) + 1)
                dve.tensor_tensor(wlo[j % RING][:], raw[j % RING][:], whi[j % RING][:].bitcast(F32),
                                  ALU.subtract).then_inc(lo_done, 1)

            def evac(st, b, gb):
                g = group(st, b, gb)
                k = st.kind
                sums = PS[:, gb % 2, :, 0:S]
                tile = b * (2 * st.GB) + (st.tile0 + 2 * gb)
                if k == "kv":
                    dve.wait_ge(used, unit(st, b, st.U * (gb + 1)) + RING)
                    dve.tensor_copy(R[:, ds(b * (4 * st.GB) + 4 * gb, 4), :],
                                    PS[:, gb % 2, :, :].rearrange("p m (a n) -> p (m a) n", a=2)).then_inc(evac_done, 1)
                    return
                dve.wait_ge(evac_done, g + 2)
                dve.wait_ge(tmp_done, tgr(st, b, gb))
                i = 0

                def did(ins):
                    nonlocal i
                    ins.then_inc(vstep, 1)
                    i += 1

                def settled(n=1):
                    dve.wait_ge(vstep, vst(st, b, gb, i - n))

                def squares_into_rs(src):
                    did(dve.tensor_tensor(T[:], src, src, ALU.mult))
                    settled()
                    did(dve.tensor_tensor(RS[:], RS[:], T[:, 0, :], ALU.add))
                    settled()
                    dve.tensor_tensor(RS[:], RS[:], T[:, 1, :], ALU.add).then_inc(evac_done, 1)

                if k == "q":
                    dve.tensor_tensor(R[:, ds(tile, 2), :], sums, T[:], ALU.add).then_inc(evac_done, 1)
                elif k == "down1":
                    y = R[:, ds(tile + Yt, 2), :]
                    dve.tensor_tensor(y, sums, T[:], ALU.add).then_inc(evac_done, 1)
                elif k == "gate" or (k == "glu" and gb % 2 == 0):
                    dve.tensor_tensor(T[:], sums, T[:], ALU.add).then_inc(evac_done, 1)
                elif k == "mix_out":
                    y = R[:, ds(tile + Yt, 2), :]
                    did(dve.tensor_tensor(y, sums, T[:], ALU.add))
                    settled()
                    squares_into_rs(y)
                else:
                    did(dve.tensor_tensor(T[:], sums, T[:], ALU.add))
                    settled()
                    if k == "scale":
                        dve.tensor_tensor(R[:, ds(tile, 2), :], T[:], rep(RS[:], 2), ALU.mult).then_inc(evac_done, 1)
                    elif k == "down2":
                        y = R[:, ds(tile + Yt, 2), :]
                        did(dve.tensor_tensor(y, y, T[:], ALU.add))
                        settled()
                        squares_into_rs(y)
                    elif k == "branch_a":
                        ga = R[:, ds(tile + 16, 2), :]
                        dve.tensor_tensor(ga, T[:], ga, ALU.mult).then_inc(evac_done, 1)
                    elif k == "branch_b":
                        ga, gb_ = R[:, ds(tile + 16, 2), :], R[:, ds(tile + 48, 2), :]
                        did(dve.tensor_tensor(T[:], T[:], gb_, ALU.mult))
                        settled()
                        dve.tensor_tensor(ga, ga, T[:], ALU.add).then_inc(evac_done, 1)
                    elif k in ("out", "down_x"):
                        chunk = 2 if k == "out" else 5
                        for m in range(2):
                            x = X[:, ds(tile + m, 1), :].rearrange("p a n -> p (a n)")
                            ins = dve.scalar_tensor_tensor(
                                out=x, in0=T[:, m, :], scalar=MOD[:, ds(tile + (2 * ADA_CTX + KT * chunk + m), 1)],
                                in1=x, op0=ALU.mult, op1=ALU.add)
                            if m == 1 and k == "down_x":
                                ins.then_inc(evac_done, 1)
                            else:
                                did(ins)
                        if k == "out":
                            settled()
                            squares_into_rs(X[:, ds(tile, 2), :])
                    elif k == "conv":
                        did(dve.tensor_tensor(Zp[:, :, 2:S + 2], T[:], rep(RS[:], 2), ALU.mult))
                        settled()
                        t0 = b * 2 + (FT * (gb % 2) + st.feat0 + VEC["conv_w"])
                        for tap in (1, 0):
                            for m in range(2):
                                if tap:
                                    dve.wait_ge(astep, ast(st, b, gb, m))
                                else:
                                    settled(2)
                                ins = dve.scalar_tensor_tensor(
                                    out=Cb[:, m, :], in0=Zp[:, m, tap:S + tap],
                                    scalar=V[:, ds(t0 + (2 * FT * tap + m), 1)], in1=Cb[:, m, :],
                                    op0=ALU.mult, op1=ALU.add)
                                if gb % 2 == 0 and tap == 0 and m == 1:
                                    ins.then_inc(evac_done, 1)
                                else:
                                    did(ins)
                    if gb % 2 and k in ("conv", "glu"):
                        val = Cb if k == "conv" else T
                        dve.wait_ge(astep, ast(st, b, 0, 2 if k == "conv" else 0))
                        settled()
                        did(dve.tensor_tensor(val[:], val[:], Gb[:], ALU.mult))
                        settled()
                        f = b * 2 + st.tile0
                        fh, fl = FH[:, ds(f, 2), 0, :], FH[:, ds(f, 2), 1, :]
                        did(dve.tensor_copy(fh, val[:]))
                        settled()
                        dve.tensor_tensor(fl, val[:], fh.bitcast(F32), ALU.subtract).then_inc(evac_done, 1)

            def condition(st, b):
                n = b + st.ib
                sel = KT if st.ib >= ADA_CTX else 0
                for u in range(4):
                    dve.wait_ge(ada_in[u % 2], n * 64 + 32 * (u // 2 + 1))
                    if u == 0:
                        dve.wait_ge(ada_red, n + 1)
                    for x in range(UK):
                        kt = UK * u + x
                        par = kt % 2
                        c = CS[:, sel + kt:sel + kt + 1]
                        if kt < 2:
                            ins = dve.tensor_scalar(ada_acc(par), ada_raw[u % 2](x), c, None, ALU.mult)
                        else:
                            dve.wait_ge(ada_ops, n * 16 + (8 + kt - 1))
                            ins = dve.scalar_tensor_tensor(out=ada_acc(par), in0=ada_raw[u % 2](x), scalar=c,
                                                           in1=ada_acc(par), op0=ALU.mult, op1=ALU.add)
                        ins.then_inc(ada_ops, 1)

            def store_mods(st, b):
                n = b + st.ib
                dve.wait_ge(ada_red, n + 2)
                dve.tensor_tensor(MOD[:, ds(n * 2, 2)], AB[:, 0:2], V[:, ds(n * 2 + VEC["b_ada"], 2)],
                                  ALU.add).then_inc(mods_done, 1)

            def body(st, b, drop=0):
                for j in range(RING, RING + st.upb - drop):
                    lo(st, b, j)
                    if (j + 1 - RING) % st.U == 0:
                        gb = (j + 1 - RING) // st.U - 1
                        evac(st, b, gb)
                        if st.ada and gb == 0:
                            condition(st, b)
                        if st.ada and gb == st.GB - 1:
                            store_mods(st, b)
                if drop:
                    for gb in range((st.upb - drop) // st.U, st.GB):
                        evac(st, b, gb)

            def run(st, last=False):
                with dve.Fori(0, st.bodies - last) as b:
                    body(st, b)
                if last:
                    body(st, st.bodies - 1, drop=RING)

            def invert(i):
                dve.wait_ge(root_ready, i + 1)
                dve.reciprocal(RS[:], RS[:]).then_inc(rstd_ready, 1)
                dve.wait_ge(rstd_ready, i + 1)

            def reduce_squares(first, n_tiles, dst):
                return dve.tensor_reduce(dst, R[:, first:first + n_tiles, :].rearrange("p k n -> p n k"), AX.X, ALU.add)

            n_clear = 0

            def clear(ap, value=0.0):
                nonlocal n_clear
                dve.memset(ap, value).then_inc(cleared, 1)
                n_clear += 1
                dve.wait_ge(cleared, n_clear)

            dve.sem_inc(lo_done, RING)
            dve.sem_inc(evac_done, 2)
            dve.sem_inc(ada_ops, 8)
            dve.sem_inc(mods_done, 1)
            clear(SM[:, EPS_C:EPS_C + 1], EPS)
            dve.wait_ge(in_vec, 16)
            dve.tensor_scalar(SM[:, 30:31], V[:, VEC["q_a"]:VEC["q_a"] + 1], HD ** -0.5, None, ALU.mult)
            dve.tensor_scalar(SM[:, 31:32], V[:, VEC["q_b"]:VEC["q_b"] + 1], 64 ** -0.5, None, ALU.mult)
            dve.tensor_scalar(SM[:, 32:33], V[:, VEC["subln"]:VEC["subln"] + 1], 1 - LAM_INIT, None,
                              ALU.mult)
            dve.tensor_tensor(SM[:, 28:30], V[:, VEC["lam"]:VEC["lam"] + 4:2], V[:, VEC["lam"] + 1:VEC["lam"] + 4:2],
                              ALU.mult).then_inc(gains, 1)
            dve.wait_ge(gains, 1)

            def scaled_lo(kt, gain, n_hi, source):
                dve.wait_ge(op_hi, n_hi)
                dve.scalar_tensor_tensor(out=XC[:, kt, 1, 0, :], in0=source, scalar=gain,
                                         in1=XC[:, kt, 0, 0, :].bitcast(F32), op0=ALU.mult,
                                         op1=ALU.subtract).then_inc(opnd, 1)

            gain_col = lambda name, kt: V[:, VEC[name] + kt:VEC[name] + kt + 1]
            for kt in range(KT):
                scaled_lo(kt, gain_col("pre_mix", kt), kt + 1, X[:, kt, :])
            for j in range(RING):
                lo(st_in, 0, j)
            dve.wait_ge(sq_ready, 1)
            reduce_squares(0, KT, RS[:]).then_inc(acc_ready, 1)
            invert(0)
            dve.wait_ge(silu_done, 1)
            run(st_in)

            dve.wait_ge(evac_done, evacuated(st_in))
            dve.tensor_scalar(R[:, 0:8, :], R[:, 0:8, :], HD ** -0.5, None, ALU.mult).then_inc(q_scaled, 1)
            clear(RS[:])
            N = 2 * H1
            for i in range(N + 4):
                if i < N:
                    w = 128 * (i % 2 + 1)
                    dve.wait_ge(scored, i + 1)
                    dve.tensor_reduce(SM[:, i % 2:i % 2 + 1], PS[:, i % 2, 0, 0:w], AX.X, ALU.max,
                                      negate=True).then_inc(neg_max, 1)
                if 1 <= i <= N:
                    n = i - 1
                    w = 128 * (n % 2 + 1)
                    dve.wait_ge(exped, n + 1)
                    dve.reciprocal(SM[:, 4 + n % 2:5 + n % 2], SM[:, 2 + n % 2:3 + n % 2]).then_inc(inverse, 1)
                    dve.wait_ge(inverse, n + 1)
                    dve.tensor_scalar(R[:, 48 + n % 2, 0:w], R[:, 48 + n % 2, 0:w], SM[:, 4 + n % 2:5 + n % 2], None,
                                      ALU.mult).then_inc(probs, 1)
                if i >= 4 and i % 2 == 0:
                    h = (i - 4) // 2
                    dve.wait_ge(op_hi, KT + h + 1)
                    dve.tensor_tensor(XC[:, h, 1, 0, :], PS[:, h % 2, 1, 0:S], XC[:, h, 0, 0, :].bitcast(F32),
                                      ALU.subtract).then_inc(opnd, 1)
            for j in range(8):
                scaled_lo(8 + j, gain_col("pool_scale", j), KT + H1 + j + 1, PS[:, j % 2, 1, 0:S])
            run(st_o)

            def add_normed(i, name):
                dve.wait_ge(evac_done, evacuated(st_o if i == 0 else st_dn2))
                dve.sem_inc(acc_ready, 1)
                invert(1 if i == 0 else 4)
                for c in range(5):
                    if c < 4:
                        y = R[:, Yt + 4 * c:Yt + 4 * c + 4, :]
                        dve.tensor_tensor(y, y, rep(RS[:], 4), ALU.mult).then_inc(y_normed, 1)
                        dve.wait_ge(y_normed, 4 * i + c + 1)
                        for kt in range(4 * c, 4 * c + 4):
                            dve.scalar_tensor_tensor(out=X[:, kt, :], in0=R[:, Yt + kt, :], scalar=gain_col(name, kt),
                                                     in1=X[:, kt, :], op0=ALU.mult, op1=ALU.add).then_inc(x_new, 1)
                    if c >= 1 and i == 0:
                        for kt in range(4 * c - 4, 4 * c):
                            scaled_lo(kt, gain_col("pre_ffn", kt), 2 * KT + kt + 1, X[:, kt, :])

            add_normed(0, "post_mix")
            clear(Zp[:, :, 0:2])
            dve.wait_ge(sq_ready, 2)
            reduce_squares(Yt, KT, RS[:]).then_inc(acc_ready, 1)
            invert(2)
            run(st_up1a)
            run(st_up1b)
            run(st_dn1)
            run(st_up2)

            def modulate(m, src, who, gain, base, n_gains):
                dve.scalar_tensor_tensor(out=GS[:], in0=MOD[:, base + KT:base + 2 * KT], scalar=1.0,
                                         in1=V[:, VEC[gain]:VEC[gain] + KT], op0=ALU.add, op1=ALU.mult
                                         ).then_inc(gains, 1)
                dve.wait_ge(gains, n_gains)
                for c in range(5):
                    if c < 4:
                        k = slice(4 * c, 4 * c + 4)
                        dve.tensor_tensor(XC32[:, k, 1, who, :], src[:, k, :], rep(RS[:], 4),
                                          ALU.mult).then_inc(mod_t, 1)
                        dve.wait_ge(mod_t, 4 * m + c + 1)
                        for kt in range(4 * c, 4 * c + 4):
                            v = XC32[:, kt, 1, who, :]
                            last = dve.tensor_scalar(v, v, GS[:, kt:kt + 1], MOD[:, base + kt:base + kt + 1],
                                                     ALU.mult, ALU.add)
                        last.then_inc(mod_v, 1)
                    if c >= 1:
                        k = slice(4 * c - 4, 4 * c)
                        dve.wait_ge(mod_hi, 4 * m + c)
                        dve.tensor_tensor(XC[:, k, 1, who, :], XC32[:, k, 1, who, :], XC[:, k, 0, who, :].bitcast(F32),
                                          ALU.subtract).then_inc(opnd, 4)

            dve.wait_ge(evac_done, evacuated(st_up2))
            dve.wait_ge(mods_done, st_q1.ib + 1)
            dve.wait_ge(sq_ready, 3)
            reduce_squares(48, 8, RS[:]).then_inc(acc_ready, 1)
            dve.wait_ge(sq_ready, 4)
            reduce_squares(48, 8, T[:, 0, :]).then_inc(y_normed, 1)
            dve.wait_ge(y_normed, 5)
            dve.tensor_tensor(RS[:], RS[:], T[:, 0, :], ALU.add).then_inc(acc_ready, 1)
            invert(3)
            modulate(0, XC32[:, :, 0, 1, :], 1, "norm1", 0, 2)
            clear(RS[:])
            run(st_dn2)

            dve.wait_ge(evac_done, evacuated(st_dn2))
            dve.sem_inc(acc_ready, 1)
            invert(4)
            for c in range(4):
                y = R[:, Yt + 4 * c:Yt + 4 * c + 4, :]
                dve.tensor_tensor(y, y, rep(RS[:], 4), ALU.mult).then_inc(y_normed, 1)
                dve.wait_ge(y_normed, 6 + c)
                for kt in range(4 * c, 4 * c + 4):
                    dve.scalar_tensor_tensor(out=X[:, kt, :], in0=R[:, Yt + kt, :], scalar=gain_col("post_ffn", kt),
                                             in1=X[:, kt, :], op0=ALU.mult, op1=ALU.add).then_inc(x_new, 1)
            dve.wait_ge(sq_ready, 5)
            reduce_squares(Yt, KT, RS[:]).then_inc(acc_ready, 1)
            invert(5)
            modulate(1, X, 0, "norm1", 2 * ADA_CTX, 3)
            clear(RS[:])
            run(st_kv)
            run(st_q1)
            run(st_q2)

            dve.wait_ge(lam_exp, 1)
            dve.tensor_tensor(SM[:, 24:25], SM[:, 23:24], SM[:, 22:23], ALU.subtract).then_inc(lam_vec, 1)
            dve.wait_ge(lam_vec, 1)
            dve.tensor_scalar(SM[:, NEGLAM:NEGLAM + 1], SM[:, 24:25], -LAM_INIT, None, ALU.add).then_inc(lam_vec, 1)
            dve.wait_ge(lam_vec, 2)
            dve.wait_ge(evac_done, evacuated(st_q2))
            dve.wait_ge(in_rope, 48)
            for c in range(len(CH) + 1):
                if c < len(CH):
                    t, br, is_k = CH[c]
                    g = (gain_col("k_b" if br else "k_a", 0) if is_k else SM[:, 30 + br:31 + br])
                    chunk = quad(R[:, t:t + 4, :])
                    dve.wait_ge(n_root, c + 1)
                    dve.reciprocal(sqb(c), sqb(c)).then_inc(n_inv, 1)
                    dve.wait_ge(n_inv, c + 1)
                    dve.scalar_tensor_tensor(out=chunk, in0=chunk, scalar=g, in1=sqb(c), op0=ALU.mult,
                                             op1=ALU.mult).then_inc(n_scaled, 1)
                if c >= 1:
                    t, br, is_k = CH[c - 1]
                    chunk, sw, t1 = quad(R[:, t:t + 4, :]), swapb, t1b
                    dims = (2, 2)
                    if is_k:
                        chunk, sw, t1, dims = chunk[:, :, 0, :], sw[:, :, 0, :], t1[:, :, 0, :], (2,)
                    cos, sin = XC32[:, 14 + br, 0, 1, :], XC32[:, 14 + br, 1, 1, :]
                    dve.wait_ge(n_scaled, c)
                    if c >= 2:
                        dve.wait_ge(n_rope, c - 1)
                    dve.tensor_tensor(t1, chunk, rep(cos, *dims), ALU.mult).then_inc(n_t1, 1)
                    dve.wait_ge(n_swap, c)
                    dve.tensor_tensor(sw, sw, rep(sin, *dims), ALU.mult).then_inc(n_t2, 1)
                    dve.wait_ge(n_t1, c)
                    dve.wait_ge(n_t2, c)
                    dve.tensor_tensor(chunk, t1, sw, ALU.add).then_inc(n_rope, 1)
            dve.wait_ge(n_rope, len(CH))

            for i in range(NA + 1):
                if i < NA:
                    dve.wait_ge(a_scored, i + 1)
                    dve.tensor_reduce(SM[:, i % 2:i % 2 + 1], PS[:, i % 2, 0, :], AX.X, ALU.max,
                                      negate=True).then_inc(a_neg, 1)
                if i >= 1:
                    n = i - 1
                    dve.wait_ge(a_exp, n + 1)
                    dve.reciprocal(SM[:, 4 + n % 2:5 + n % 2], SM[:, 2 + n % 2:3 + n % 2]).then_inc(a_inv, 1)
                    dve.wait_ge(a_inv, n + 1)
                    dve.tensor_scalar(scr(n % 2), scr(n % 2), SM[:, 4 + n % 2:5 + n % 2], None,
                                      ALU.mult).then_inc(a_prob, 1)
            for i in range(NB_ + 1):
                if i < NB_:
                    dve.wait_ge(b_scored, i + 1)
                    e = 6 + 2 * (i % 2)
                    dve.tensor_reduce(SM[:, e:e + 2], PS[:, i % 2, :, :], AX.X, ALU.max,
                                      negate=True).then_inc(b_neg, 1)
                if i >= 1:
                    n = i - 1
                    e = 2 * (n % 2)
                    dve.wait_ge(b_exp, 2 * n + 2)
                    dve.reciprocal(SM[:, 14 + e:16 + e], SM[:, 10 + e:12 + e]).then_inc(b_inv, 1)
                    dve.wait_ge(b_inv, n + 1)
                    dve.tensor_tensor(SM[:, 18 + n % 2:19 + n % 2], SM[:, 15 + e:16 + e], SM[:, NEGLAM:NEGLAM + 1],
                                      ALU.mult).then_inc(b_nl, 1)
                    dve.wait_ge(b_nl, n + 1)
                    dve.tensor_scalar(scr(e + 1), scr(e + 1), SM[:, 18 + n % 2:19 + n % 2], None,
                                      ALU.mult).then_inc(b_p1, 1)
                    dve.wait_ge(b_p1, n + 1)
                    dve.scalar_tensor_tensor(out=scr(e), in0=scr(e), scalar=SM[:, 14 + e:15 + e], in1=scr(e + 1),
                                             op0=ALU.mult, op1=ALU.add).then_inc(b_prob, 1)
            dve.wait_ge(o_root, 1)
            dve.reciprocal(R[:, 24:32, :], R[:, 24:32, :]).then_inc(o_inv, 1)
            dve.wait_ge(o_inv, 1)
            dve.scalar_tensor_tensor(out=R[:, 40:48, :], in0=R[:, 40:48, :], scalar=SM[:, 32:33], in1=R[:, 24:32, :],
                                     op0=ALU.mult, op1=ALU.mult).then_inc(o_norm, 1)
            dve.wait_ge(o_norm, 1)

            def split_lo(k0, who, tile, n):
                dve.wait_ge(split_hi, n)
                dve.tensor_tensor(XC[:, k0:k0 + 4, 1, who, :], R[:, tile:tile + 4, :],
                                  XC[:, k0:k0 + 4, 0, who, :].bitcast(F32), ALU.subtract).then_inc(opnd, 4)

            for c in range(2):
                split_lo(4 * c, 1, 40 + 4 * c, c + 1)
            run(st_ga)
            run(st_gb)
            for c in range(4):
                split_lo(4 * c, 0, O_SRC[c], 3 + c)
            run(st_ba)
            run(st_bb)
            for c in range(4):
                split_lo(4 * c, 0, 16 + 4 * c, 7 + c)
            run(st_out)
            dve.wait_ge(evac_done, evacuated(st_out))
            dve.sem_inc(acc_ready, 1)
            invert(6)
            dve.wait_ge(mods_done, st_u1a.ib + 1)
            modulate(2, X, 0, "norm2", 2 * ADA_CTX + 3 * KT, 4)
            run(st_u1a)
            run(st_u1b)
            run(st_d1)
            run(st_u2)
            run(st_d2, last=True)

        @block.tensor
        def _(pe):
            def multiply(st, b, gb, u, fresh):
                j = st.U * gb + u
                pe.wait_ge(lo_done, unit(st, b, j) + 1 + RING)
                if fresh and st.op is not None:
                    pe.wait_ge(opnd, st.op + 4 * (u + 1))
                if fresh and st.act:
                    pe.wait_ge(evac_done, groups_before(st.after) + min(4 * (u + 1), st.gb - st.after.gb))
                for x in range(UK):
                    kt = UK * u + x
                    first, last = kt == 0, kt == UK * st.U - 1
                    h, l = whi[j % RING], wlo[j % RING]
                    for m in range(2):
                        f = slice(P * m, P * m + P)
                        both = PS[:, gb % 2, m, :].rearrange("p (a n) -> p a n", a=2)
                        if st.kind == "kv":
                            pe.matmul(both, h[:, x, f], XC[:, kt, 0, :, :], start=first, stop=False)
                            pe.matmul(both, h[:, x, f], XC[:, kt, 1, :, :], start=False, stop=False)
                            ins = pe.matmul(both, l[:, x, f], XC[:, kt, 0, :, :], start=False, stop=last)
                            continue
                        mov = FH[:, kt, :, :] if st.act else XC[:, kt, :, st.who, :]
                        if last:
                            pe.matmul(both[:, 0, :], l[:, x, f], mov[:, 0, :], start=False, stop=False)
                            ins = pe.matmul(both, h[:, x, f], mov, start=False, stop=True)
                        else:
                            pe.matmul(both, h[:, x, f], mov, start=first, stop=False)
                            ins = pe.matmul(both[:, 0, :], l[:, x, f], mov[:, 0, :], start=False, stop=False)
                ins.then_inc(used, 1)

            def take_condition(st, b):
                n = b + st.ib
                pe.wait_ge(ada_ops, n * 16 + (16 + 8))
                pe.wait_ge(mods_done, n + 1)
                for m in range(2):
                    for par in range(2):
                        ins = pe.matmul(AB[:, m:m + 1], ada_acc(par)[:, P * m:P * m + P], ones[:, 0:1],
                                        start=par == 0, stop=par == 1)
                ins.then_inc(ada_red, 1)

            def body(st, b, fresh=True, insert=None):
                for gb in range(st.GB):
                    pe.wait_ge(evac_done, group(st, b, gb) + 1)
                    for u in range(st.U):
                        multiply(st, b, gb, u, fresh and gb == 0)
                        if insert is not None and gb == u == 0:
                            sum_squares(insert)
                if st.ada:
                    take_condition(st, b)

            def run(st, insert=None):
                if insert is not None:
                    body(st, 0, insert=insert)
                    with pe.Fori(1, st.bodies) as b:
                        body(st, b, fresh=False)
                else:
                    with pe.Fori(0, st.bodies) as b:
                        body(st, b)

            def sum_squares(i):
                pe.wait_ge(acc_ready, ACC[i])
                pe.matmul(NB[:, 0:S], ones, RS[:], start=True, stop=True).then_inc(sum_ready, 1)

            pe.sem_inc(used, RING)
            pe.sem_inc(ada_red, 1)
            pe.wait_ge(in_cst, 48)
            run(st_in, insert=0)

            pe.wait_ge(evac_done, evacuated(st_in))
            pe.wait_ge(masked, 1)
            for j in range(4):
                if j >= 2:
                    pe.wait_ge(vt_copied, j - 1)
                for x in range(4):
                    h, tb = 4 * (j % 2) + x, j // 2
                    ins = pe.transpose(TP[:, j % 2, P * x:P * x + P], R[:, 16 + h, P * tb:P * tb + P], ident)
                ins.then_inc(vt_turned, 1)
            pe.wait_ge(q_scaled, 1)
            N = 2 * H1

            def score(n):
                h, b = divmod(n, 2)
                w = P * (b + 1)
                if n >= 2:
                    pe.wait_ge(exped, n - 1)
                pe.matmul(PS[:, n % 2, 0, 0:w], R[:, h, P * b:P * b + P], R[:, 8 + h, 0:w], start=True, stop=False)
                pe.matmul(PS[:, n % 2, 0, 0:w], flip, hankel(h)[:, P * (1 - b):P * (1 - b) + w], start=False,
                          stop=True).then_inc(scored, 1)

            score(0)
            score(1)
            pe.wait_ge(vt_copied, 4)
            for i in range(N + 1):
                if i < N:
                    pe.wait_ge(probs, i + 1)
                    if i >= 2:
                        pe.wait_ge(pt_copied, i - 1)
                    for t in range(i % 2 + 1):
                        ins = pe.transpose(TP[:, i % 2, P * t:P * t + P], R[:, 48 + i % 2, P * t:P * t + P], ident)
                    ins.then_inc(turned, 1)
                if i + 2 < N:
                    score(i + 2)
                if i >= 1:
                    n = i - 1
                    h, b = divmod(n, 2)
                    pe.wait_ge(pt_copied, n + 1)
                    if b == 0 and h >= 2:
                        pe.wait_ge(opnd, KT + h - 1)
                    for t in range(b + 1):
                        ins = pe.matmul(PS[:, h % 2, 1, P * b:P * b + P],
                                        R[:, 40 + 4 * t + h // 2, P * (h % 2):P * (h % 2) + P],
                                        R[:, 50 + n % 2, P * t:P * t + P], start=t == 0, stop=t == b)
                    ins.then_inc(summed, 1)
            for j in range(8):
                g = j // 2
                pe.wait_ge(pooled, g + 1)
                pe.wait_ge(opnd, KT + H1 + j - 1)
                for c in range(2):
                    ins = pe.matmul(PS[:, j % 2, 1, 0:S], R[:, 32 + 2 * g + c, P * (j % 2):P * (j % 2) + P],
                                    R[:, 24 + 2 * g + c, :], start=c == 0, stop=c == 1)
                ins.then_inc(summed, 1)
            pe.wait_ge(opnd, 2 * KT)
            run(st_o)
            sum_squares(1)
            run(st_up1a, insert=2)
            run(st_up1b)
            run(st_dn1)
            run(st_up2)
            sum_squares(3)
            run(st_dn2)
            sum_squares(4)
            sum_squares(5)
            pe.wait_ge(opnd, 4 * KT)
            run(st_kv)

            pe.wait_ge(evac_done, evacuated(st_kv))
            for j in range(12):
                if j >= 2:
                    pe.wait_ge(v2_copied, j - 1)
                tile = 8 + 2 * j if j < 4 else 24 + 2 * j
                for t in range(4):
                    ins = pe.transpose(TP[:, j % 2, P * t:P * t + P],
                                       R[:, tile + t // 2, P * (t % 2):P * (t % 2) + P], ident)
                ins.then_inc(v2_turned, 1)
            run(st_q1)
            run(st_q2)

            pe.wait_ge(gains, 1)
            pe.matmul(NB[:, 0:2], ones, SM[:, 28:30], start=True, stop=True).then_inc(lam_sum, 1)
            pe.wait_ge(in_rope, 48)
            pe.wait_ge(evac_done, evacuated(st_q2))
            for c, (t, br, is_k) in enumerate(CH):
                pe.wait_ge(n_sq, c + 1)
                if c >= 2:
                    pe.wait_ge(n_root, c - 1)
                for k in range(2):
                    ins = pe.matmul(PS[:, c % 2, k, :].rearrange("p (a n) -> p a n", a=2), halves if br else ones,
                                    sqb(c)[:, k, :, :], start=True, stop=True)
                ins.then_inc(n_sum, 1)

            def turn(n, buf, prob, copied, done):
                pe.wait_ge(prob, n + 1)
                if n >= 2:
                    pe.wait_ge(copied, n - 1)
                for t in range(4):
                    ins = pe.transpose(TP[:, n % 2, P * t:P * t + P], buf[:, t // 2, P * (t % 2):P * (t % 2) + P],
                                       ident)
                ins.then_inc(done, 1)

            def values(n, dst, j, buf, copied, done):
                pe.wait_ge(copied, n + 1)
                for t in range(4):
                    ins = pe.matmul(dst, v_at(j, t), buf[:, t // 2, P * (t % 2):P * (t % 2) + P],
                                    start=t == 0, stop=t == 3)
                ins.then_inc(done, 1)

            def score_a(n):
                h, b = divmod(n, 2)
                if n >= 2:
                    pe.wait_ge(a_exp, n - 1)
                pe.matmul(PS[:, n % 2, 0, :].rearrange("p (a n) -> p a n", a=2),
                          R[:, qa_tile(h), P * b:P * b + P], R[:, 2 * (h // 4):2 * (h // 4) + 2, :],
                          start=True, stop=True).then_inc(a_scored, 1)

            pe.wait_ge(n_rope, len(CH))
            pe.wait_ge(v2_copied, 12)
            score_a(0)
            score_a(1)
            for i in range(NA + 1):
                if i < NA:
                    turn(i, scr(i % 2), a_prob, a_copied, a_turned)
                if i + 2 < NA:
                    score_a(i + 2)
                if i >= 1:
                    n = i - 1
                    h, b = divmod(n, 2)
                    if b == 0 and h >= 2:
                        pe.wait_ge(a_out, h - 1)
                    values(n, PS[:, h % 2, 1, P * b:P * b + P], h // 4, scr(2 + n % 2), a_copied, a_summed)
            pe.wait_ge(a_out, HA)

            def score_b(n):
                h, b = divmod(n, 2)
                if n >= 2:
                    pe.wait_ge(b_exp, 2 * n - 2)
                for x in range(2):
                    rows = slice(64 * x, 64 * x + 64)
                    ins = pe.matmul(PS[:, n % 2, x, :].rearrange("p (a n) -> p a n", a=2),
                                    R[rows, 40 + h, P * b:P * b + P], R[rows, 16 + 2 * h:18 + 2 * h, :],
                                    start=True, stop=True)
                ins.then_inc(b_scored, 1)

            score_b(0)
            score_b(1)
            for i in range(NB_ + 1):
                if i < NB_:
                    turn(i, scr(2 * (i % 2)), b_prob, b_copied, b_turned)
                if i + 2 < NB_:
                    score_b(i + 2)
                if i >= 1:
                    n = i - 1
                    h, b = divmod(n, 2)
                    if b == 0 and h >= 2:
                        pe.wait_ge(b_out, h - 1)
                    values(n, (NB, AB)[h % 2][:, P * b:P * b + P], 4 + h, scr(4 + n % 2), b_copied, b_summed)
            pe.wait_ge(o_sq, 1)
            for t in range(4):
                ins = pe.matmul(PS[:, t // 2, t % 2, :].rearrange("p (a n) -> p a n", a=2), ones,
                                R[:, 16 + 2 * t:18 + 2 * t, :], start=True, stop=True)
            ins.then_inc(o_sum, 1)
            pe.wait_ge(o_root, 1)
            run(st_ga)
            run(st_gb)
            run(st_ba)
            run(st_bb)
            run(st_out)
            sum_squares(6)
            run(st_u1a)
            run(st_u1b)
            run(st_d1)
            run(st_u2)
            run(st_d2)


def rotations():
    rows = np.repeat(np.arange(S // 64, dtype=np.float32), 64)
    col = np.tile(np.arange(64, dtype=np.float32), S // 64)
    out = []
    for hd in (128, 64):
        n = hd // 4
        freqs = np.float32(10000.0) ** (-np.arange(n, dtype=np.float32) / np.float32(n))
        ang = np.concatenate([rows[:, None] * freqs, col[:, None] * freqs], axis=-1).T.astype(np.float32)
        p = np.arange(P)
        sign = np.where(p % hd < hd // 2, -1.0, 1.0).astype(np.float32)[:, None]
        out += [np.cos(ang)[p % (hd // 2)], sign * np.sin(ang)[p % (hd // 2)]]
    return out


def constants():
    p = np.arange(P)
    fix = np.ones((4, 2, 16), np.float32)
    for g, w in enumerate(WINDOWS):
        fix[g, :, :w - 1] = np.float32(w) / np.arange(1, w, dtype=np.float32)
    parts = [np.eye(P), np.ones((P, P)), np.eye(P)[::-1], (p[:, None] // 64 == p[None, :] // 64).astype(np.float32),
             np.tile(fix.reshape(1, -1), (P, 1)), np.zeros((P, 128))] + rotations()
    return np.ascontiguousarray(np.concatenate(parts, axis=1), dtype=np.float32)


def kernel(**inputs):
    import concourse.bacc as bacc
    from concourse.bass_utils import run_bass_kernel_spmd

    a = {k: np.asarray(v) for k, v in inputs.items()}
    tiles = lambda v: v.reshape(-1, P).T
    taps = lambda w: np.concatenate([tiles(r) for r in w], axis=1)
    b_ada = tiles(a["b_ada_2"][0])

    def column(v):
        c = np.zeros((P, 1), v.dtype)
        c[:v.size, 0] = v.reshape(-1)
        return c

    twice = lambda v: np.concatenate([v, v]).reshape(P, 1)
    vec = np.concatenate(
        [tiles(a[n][0]) for n in ("pre_mix_g", "post_mix_g", "pre_ffn_g", "post_ffn_g", "norm1_g_2", "norm2_g_2")]
        + [taps(a["conv_w"][0]), tiles(a["conv_b"][0]), tiles(a["pool_scale"][0]),
           column(a["q_norm_a_2"][0]), column(a["k_norm_a_2"][0]), twice(a["q_norm_b_2"][0]), twice(a["k_norm_b_2"][0]),
           tiles(a["c_ctx_2"]), tiles(a["c_2"][0])]
        + [column(a[n][0]) for n in ("lam_q1_2", "lam_k1_2", "lam_q2_2", "lam_k2_2")]
        + [b_ada[:, :2 * KT], b_ada, column(a["subln_g_2"][0])], axis=1)
    feature_major = lambda v: np.ascontiguousarray(v.T.reshape(KT, P, S).transpose(1, 0, 2))
    reach = a["rel_bias"].shape[2] // 2
    order = np.clip(S - 1 - np.arange(S + P - 1), -reach, reach) + reach
    arrays = {
        "xT": feature_major(a["x"][0]), "ctxT": feature_major(a["ctx_2"][0]), "vec": np.ascontiguousarray(vec),
        "cst": constants(), "rel": np.ascontiguousarray(a["rel_bias"][0][:, order]), "w_in": a["w_in"][0],
        "pool_w": np.ascontiguousarray(a["pool_w"][0].reshape(8, P, 256).transpose(1, 0, 2)),
        "w_o": a["w_o"][0], "w_up": a["w_up"][0], "w_down": a["w_down"][0], "w_ada": a["w_ada_2"][0],
        "w_in2": a["w_in_2"][0], "w_bra": a["w_br_a_2"][0], "w_brb": a["w_br_b_2"][0], "w_out2": a["w_out_2"][0],
        "w_fg": a["w_ff_gate_2"][0], "w_fu": a["w_ff_up_2"][0], "w_fd": a["w_ff_down_2"][0],
    }
    nc = bacc.Bacc("TRN2", target_bir_lowering=False, num_devices=1)
    args = {n: nc.dram_tensor(n, v.shape, mybir.dt.from_np(v.dtype), kind="ExternalInput").ap()
            for n, v in arrays.items()}
    args["out"] = nc.dram_tensor("out", (P, KT, S), F32, kind="ExternalOutput").ap()
    build(nc, **args)
    r = run_bass_kernel_spmd(nc, [arrays], core_ids=[0])
    got = r.results[0]["out"]
    return got.transpose(1, 0, 2).reshape(D, S).T.reshape(1, S, D)
```

```python
from contextlib import ExitStack
import math

import numpy as np
import concourse.bass as bass
from concourse import mybir

F32 = mybir.dt.float32
F32R = mybir.dt.float32r
ALU = mybir.AluOpType
ACT = mybir.ActivationFunctionType
AX = mybir.AxisListType
ds = bass.ds

P = 128
S = 256
D = 2048
KT = D // P
DFF = 5632
FT = DFF // P
UK = 4
GW = 256
RING = 4
HD = 128
H1 = 8
HA, HB = 16, 8
EPS = 1e-6
WINDOWS = (2, 4, 8, 16)
FIRST_HALF = 24
KVW, QW, GATEW = 3072, 3072, 4096
ADA_CTX = 16
ADA_ITEMS = 64
ADA_UNITS = KT // UK
ADA_AFTER = (0, 2, 4, 5)
ADA_ADDS = (2, 5, 8)
LAM_INIT = 0.8 - 0.6 * math.exp(-0.3 * 0)

VEC = {}
_at = 0
for _name, _n in (("pre_mix", KT), ("post_mix", KT), ("pre_ffn", KT), ("post_ffn", KT), ("norm1", KT), ("norm2", KT),
                  ("conv_w", 3 * 2 * FT), ("conv_b", 2 * FT), ("pool_scale", 8), ("q_a", 1), ("k_a", 1), ("q_b", 1),
                  ("k_b", 1), ("cond", 2 * KT), ("lam", 4), ("b_ada", 2 * ADA_ITEMS), ("subln", 1), ("q_a_sw", 1), ("q_b_sw", 1)):
    VEC[_name] = _at
    _at += _n
NVEC = _at

C_FLIP, C_ROPE = 256, 768
NCONST = C_ROPE + 4 * S


class Stage:

    def __init__(self, name, src, groups, units, kind, per_body=2, ada=0, who=0, act=False, tile0=0, feat0=0, op=None, after=None):
        self.name, self.src, self.G, self.U, self.kind = name, src, groups, units, kind
        self.GB, self.ada, self.who, self.act = per_body, ada, who, act
        self.tile0, self.feat0 = tile0, feat0
        self.op = op
        self.after = after
        self.bodies = groups // per_body
        self.entries, self.last, self.cond = [], [], []
        for j in range(units * per_body):
            self.entries.append(divmod(j, units))
            if j % units == units - 1:
                self.last.append(len(self.entries) - 1)
            if ada and j in ADA_AFTER:
                self.cond.append(len(self.entries))
                self.entries.append((None, ADA_AFTER.index(j)))
        self.upb = len(self.entries)
        assert groups % per_body == 0 and self.upb % RING == 0


V_STEPS = {"scale": 0, "mix_out": 3, "conv": (4, 7), "down1": 0, "down2": 3, "kv": 0, "q": 0, "gate": 0,
           "branch_a": 0, "branch_b": 1, "out": 4, "glu": (0, 2), "down_x": 1}
A_STEPS = {"conv": (3, 2), "gate": (1, 1), "glu": (1, 0)}


def steps(table, kind, gb):
    n = table.get(kind, 0)
    return n[gb % 2] if isinstance(n, tuple) else n


def number(stages):
    u = g = v = a = n = 0
    for st in stages:
        st.ub, st.gb, st.vb, st.ab, st.ib = u, g, v, a, n
        st.vpb = sum(steps(V_STEPS, st.kind, i) for i in range(st.GB))
        st.apb = sum(steps(A_STEPS, st.kind, i) for i in range(st.GB))
        u += st.upb * st.bodies
        g += st.G
        v += st.vpb * st.bodies
        a += st.apb * st.bodies
        n += st.ada * st.bodies
    for st, after in zip(stages, stages[1:] + [None]):
        st.next = after
    assert n == ADA_ITEMS
    return stages


def build(nc, xT, ctxT, vec, cst, rel, w_in, pool_w, w_o, w_up, w_down, w_ada, w_in2, w_bra, w_brb, w_out2,
          w_fg, w_fu, w_fd, out):
    km = lambda w: w.rearrange("(k p) n -> p k n", p=P)
    W = {k: km(v) for k, v in dict(w_in=w_in, w_o=w_o, w_up=w_up, w_down=w_down, w_in2=w_in2, bra=w_bra, brb=w_brb,
                                   out=w_out2, fg=w_fg, fu=w_fu, fd=w_fd).items()}
    ada_src = km(w_ada)

    def cols(w, k, c0, stride):
        return lambda b, GB, gb, u: W[w][:, k + UK * u:k + UK * u + UK, ds((b * GB + gb) * stride + c0, GW)]

    def pairs(wg, wu, g0, u0):
        return lambda b, GB, gb, u: W[(wg, wu)[gb % 2]][:, UK * u:UK * u + UK,
                                                          ds(b * GW + (g0, u0)[gb % 2], GW)]

    h1c = FIRST_HALF // 2 * GW
    n1, n2 = FIRST_HALF // 2, (FT - FIRST_HALF) // 2
    st_in = Stage("w_in", cols("w_in", 0, 0, GW), 16, 4, "scale", ada=1, op=0)
    st_o = Stage("w_o", cols("w_o", 0, 0, GW), 8, 4, "mix_out", ada=1, op=16)
    st_up1a = Stage("up1a", pairs("w_up", "w_up", 0, DFF), 8, 4, "conv", ada=1, op=32)
    st_up1b = Stage("up1b", pairs("w_up", "w_up", 4 * GW, DFF + 4 * GW), 2 * n1 - 8, 4, "conv", tile0=8, feat0=8)
    st_dn1 = Stage("down1", cols("w_down", 0, 0, GW), 8, 6, "down1", ada=1, act=True, after=st_up1a)
    st_up2 = Stage("up2", pairs("w_up", "w_up", h1c, DFF + h1c), 2 * n2, 4, "conv", ada=1, feat0=FIRST_HALF)
    st_dn2 = Stage("down2", cols("w_down", FIRST_HALF, 0, GW), 8, 5, "down2", per_body=4, ada=1, act=True, after=st_up2)
    st_kv = Stage("kv", cols("w_in2", 0, 0, GW), KVW // GW, 4, "kv", ada=1, op=64)
    st_q1 = Stage("q_first", cols("w_in2", 0, KVW, GW), 4, 4, "q", ada=1, tile0=8)
    st_q2 = Stage("q_rest", cols("w_in2", 0, KVW + 1024, GW), 8, 4, "q", ada=1, tile0=32)
    st_ga = Stage("gate_a", cols("w_in2", 0, KVW + QW, GW), 8, 4, "gate", ada=1, tile0=16)
    st_gb = Stage("gate_b", cols("w_in2", 0, KVW + QW + D, GW), 8, 4, "gate", ada=1, tile0=48)
    st_ba = Stage("branch_a", cols("bra", 0, 0, GW), 8, 4, "branch_a", ada=1, op=88)
    st_bb = Stage("branch_b", cols("brb", 0, 0, GW), 8, 2, "branch_b", per_body=4, ada=1, who=1)
    st_out = Stage("out", cols("out", 0, 0, GW), 8, 4, "out", op=104)
    st_u1a = Stage("glu1a", pairs("fg", "fu", 0, 0), 12, 4, "glu", ada=1, op=120)
    st_u1b = Stage("glu1b", pairs("fg", "fu", 6 * GW, 6 * GW), 2 * n1 - 12, 4, "glu", tile0=12)
    st_d1 = Stage("fdown1", cols("fd", 0, 0, GW), 8, 6, "down_x", act=True, after=st_u1a)
    st_u2 = Stage("glu2", pairs("fg", "fu", h1c, h1c), 2 * n2, 4, "glu")
    st_d2 = Stage("fdown2", cols("fd", FIRST_HALF, 0, GW), 8, 5, "down_x", per_body=4, act=True, after=st_u2)
    stages = number([st_in, st_o, st_up1a, st_up1b, st_dn1, st_up2, st_dn2, st_kv, st_q1, st_q2, st_ga, st_gb, st_ba, st_bb,
                     st_out, st_u1a, st_u1b, st_d1, st_u2, st_d2])

    with ExitStack() as ctx:
        place = {"at": 16512}

        def here(n_bytes):
            at = place["at"]
            place["at"] += n_bytes
            return at

        def sb(name, shape, dt, at):
            return nc.alloc_sbuf_tensor_at(name, shape, dt, offset=at)

        unit_b = UK * GW * 4
        raw = [sb(f"raw{i}", [P, UK, GW], F32, here(unit_b)) for i in range(RING)]
        whi = [sb(f"whi{i}", [P, UK, GW], F32R, here(unit_b)) for i in range(RING)]
        wlo = [sb(f"wlo{i}", [P, UK, GW], F32R, here(unit_b)) for i in range(RING)]
        prod = [sb(f"cond_products{i}", [P, UK, GW], F32, 16512 + (RING + i) * unit_b) for i in range(RING)]
        X = sb("x_res", [P, KT, S], F32, here(KT * S * 4))
        xc_at = here(KT * 4 * S * 4)
        XC = sb("operand", [P, KT, 2, 2, S], F32R, xc_at)
        XC32 = sb("operand_scratch", [P, KT, 2, 2, S], F32, xc_at)
        r_at = here(72 * S * 4)
        R = sb("tiles", [P, 72, S], F32, r_at)
        FH = sb("ffn_act", [P, FIRST_HALF, 2, S], F32R, r_at)
        Zp = sb("conv_in", [P, 2, S + 2], F32, r_at + 48 * 1024)
        Cb = sb("conv_out", [P, 2, S], F32, r_at + 48 * 1024 + 2 * (S + 2) * 4 + 16)
        Gb = sb("gate_act", [P, 2, S], F32, r_at + 48 * 1024 + 2 * (S + 2) * 4 + 16 + 2048)
        CA = sb("cond_sums", [P, 2, GW], F32, here(2 * GW * 4))
        IO = sb("ident_ones", [P, 256], F32, here(1024))
        RS = sb("rstd", [P, S], F32, here(S * 4))
        V = sb("vectors", [P, NVEC], F32, here(NVEC * 4 + 28 & ~31))
        MOD = sb("mods", [P, 2 * ADA_ITEMS], F32, here(2 * ADA_ITEMS * 4))
        CS = sb("cond_silu", [P, 2 * KT], F32, here(2 * KT * 4))
        GS = sb("gain_scale", [P, KT], F32, here(KT * 4))
        SM = sb("small", [P, 40], F32, here(160))
        assert place["at"] <= nc.sbuf_usable_end, (place["at"], nc.sbuf_usable_end)
        ident, ones = IO[:, 0:128], IO[:, 128:256]
        scr = lambda kt: XC32[:, kt, :, 1, :]
        flip = XC32[:, 13, 0, 1, 0:128]
        halves = XC32[:, 13, 0, 1, 128:256]
        hankel = lambda h: XC32[:, h // 2, h % 2, 1, :]
        poolfix = XC32[:, 13, 1, 1, :]
        EPS_C, NEGLAM = 20, 21
        Yt = 56

        PS = ctx.enter_context(nc.psum_tensor("acc", [P, 2, 2, 512], F32))
        TP = ctx.enter_context(nc.psum_tensor("turned", [P, 2, 512], F32))
        NB = ctx.enter_context(nc.psum_tensor("sums", [P, 512], F32))
        AB = ctx.enter_context(nc.psum_tensor("ada_sums", [P, 512], F32))

        def sem(name):
            return ctx.enter_context(nc.semaphore(name))

        raw_in = [sem(f"raw_in{i}") for i in range(RING)]
        hi_done = sem("hi_done")
        lo_done = sem("lo_done")
        used = sem("used")
        evac_done = sem("evac_done")
        vstep = sem("vstep")
        astep = sem("astep")
        ada_ops = sem("ada_ops")
        ada_sum = sem("ada_sum")
        ada_red = sem("ada_red")
        mods_done = sem("mods_done")
        silu_done = sem("silu_done")
        in_x = [sem(f"in_x{c}") for c in range(4)]
        in_vec, in_cst, in_att, in_ctx, in_rope = (sem(f"in_{n}") for n in ("vec", "cst", "att", "ctx", "rope"))
        sq_ready, acc_ready, sum_ready, root_ready, rstd_ready = (
            sem(n) for n in ("squares_ready", "acc_ready", "sum_ready", "root_ready", "rstd_ready"))
        cleared = sem("acc_cleared")
        op_hi = sem("operand_hi")
        opnd = sem("operand_ready")
        x_new = sem("residual_tile")
        y_normed = sem("normed_chunk")
        mod_t, mod_v, mod_hi, gains = sem("mod_scaled"), sem("mod_value"), sem("mod_hi"), sem("gains")
        q_scaled, vt_turned, vt_copied, masked, pooled, poolstep = (
            sem(n) for n in ("q_scaled", "vt_turned", "vt_copied", "masked", "pooled", "poolstep"))
        scored, neg_max, exped, inverse, probs, turned, pt_copied, summed = (
            sem(n) for n in ("scored", "neg_max", "exped", "inverse", "probs", "turned", "pt_copied", "summed"))
        v2_turned, v2_copied = sem("v2_turned"), sem("v2_copied")
        n_sq, n_sum, n_root, n_inv, n_scaled, n_swap, n_t1, n_t2, n_rope, n_bcast, n_table = (
            sem(n) for n in ("n_sq", "n_sum", "n_root", "n_inv", "n_scaled", "n_swap", "n_t1", "n_t2", "n_rope",
                             "n_bcast", "n_table"))
        a_scored, a_neg, a_exp, a_inv, a_prob, a_turned, a_copied, a_summed, a_out = (
            sem(n) for n in ("a_scored", "a_neg", "a_exp", "a_inv", "a_prob", "a_turned", "a_copied", "a_summed",
                             "a_out"))
        b_scored, b_neg, b_exp, b_inv, b_nl, b_p1, b_prob, b_turned, b_copied, b_summed, b_out = (
            sem(n) for n in ("b_scored", "b_neg", "b_exp", "b_inv", "b_nl", "b_p1", "b_prob", "b_turned", "b_copied",
                             "b_summed", "b_out"))
        a_max, b_max = sem("a_max"), sem("b_max")
        lam_exp, lam_sum, lam_vec = sem("lam_exp"), sem("lam_sum"), sem("lam_vec")
        o_sq, o_sum, o_root, o_inv, o_norm = (sem(n) for n in ("o_sq", "o_sum", "o_root", "o_inv", "o_norm"))
        split_hi = sem("split_hi")
        out_stored = sem("out_stored")

        def unit(st, b, j):
            return b * st.upb + (st.ub + j)

        def group(st, b, gb):
            return b * st.GB + (st.gb + gb)

        def vst(st, b, gb, i):
            return b * st.vpb + (st.vb + sum(steps(V_STEPS, st.kind, x) for x in range(gb)) + i + 1)

        def ast(st, b, gb, i):
            return b * st.apb + (st.ab + sum(steps(A_STEPS, st.kind, x) for x in range(gb)) + i + 1)

        def filled(st, b, j):
            return b * (st.upb // RING * 16) + ((st.ub + j) // RING + 1) * 16

        def grouped(st, b, gb):
            return unit(st, b, st.last[gb]) + 1 + RING

        def cond_silu(st, u, x):
            k = (KT if st.ib >= ADA_CTX else 0) + UK * u + x
            return CS[:, k:k + 1]

        def groups_before(st):
            return st.gb + 2

        def evacuated(st):
            return st.gb + st.G + 2

        def used_all(st):
            return st.ub + st.upb * st.bodies + RING

        def rep(ap, *n):
            return bass.AP(ap.tensor, ap.offset, [ap.ap[0]] + [[0, x] for x in n] + [ap.ap[-1]])

        ACC = (1, 2, 3, 5, 6, 7, 8)

        CH = [(0, 0, 1), (4, 0, 1), (16, 1, 1), (20, 1, 1), (24, 1, 1), (28, 1, 1),
              (8, 0, 0), (12, 0, 0), (32, 0, 0), (36, 0, 0), (40, 1, 0), (44, 1, 0)]
        NK = 6
        quad = lambda ap: ap.rearrange("p (k a) n -> p k a n", a=2)
        sqb = lambda c: XC32[:, 6 * (c % 2):6 * (c % 2) + 2, :, 1, :]
        swapb = lambda c: XC32[:, 2 + 2 * (c % 2):4 + 2 * (c % 2), :, 1, :]
        HR = XC32[:, 13, 1, 1, :]

        def hr_col(c, x, t):
            if c < 2:
                return 2 * (4 * c + x) + t
            if c < 6:
                return 16 + 2 * (2 * (4 * (c - 2) + x) + t)
            if c < 10:
                return 80 + 2 * (4 * (c - 6) + x) + t
            return 112 + 2 * (2 * (4 * (c - 10) + x) + t)
        qa_tile = lambda h: 8 + h if h < 8 else 24 + h
        v_at = lambda j, t: R[:, 48 + 6 * t + j // 2, 128 * (j % 2):128 * (j % 2) + 128]
        v_cols = R[:, 48:72, :].rearrange("p (t j) (a d) -> p t j a d", t=4, a=2)
        NA, NB_ = 2 * HA, 2 * HB
        O_SRC = (8, 12, 32, 36)

        block = ctx.enter_context(nc.Block())

        @block.sync
        def _(sp):
            for st in stages:
                with sp.Fori(0, st.bodies) as b:
                    for j, (gb, u) in enumerate(st.entries):
                        if gb is None:
                            src = ada_src[:, UK * u:UK * u + UK,
                                          ds((b + st.ib) * GW - (ADA_CTX * GW if st.ib >= ADA_CTX else 0), GW)]
                        else:
                            src = st.src(b, st.GB, gb, u)
                        sp.wait_ge(lo_done, unit(st, b, j) + 1)
                        sp.dma_start(raw[j % RING][:], src).then_inc(raw_in[j % RING], 16)
            sp.wait_ge(evac_done, evacuated(st_d2))
            sp.dma_start(out, X[:]).then_inc(out_stored, 16)
            sp.wait_ge(out_stored, 16)

        @block.gpsimd
        def _(pool):
            pool.wait_ge(in_att, 64)
            pool.memset(XC32[64:128, 0:4, :, 1, 192:256], -1e30).then_inc(masked, 1)
            pool.wait_ge(masked, 1)

            def add_condition(st):
                with pool.Fori(0, st.bodies) as b:
                    n = b + st.ib
                    for u in range(ADA_UNITS - 1):
                        j = st.cond[u]
                        w = prod[j % RING]
                        at = n * 8 + ((0,) + ADA_ADDS)[u]
                        pool.wait_ge(hi_done, unit(st, b, j) + 1)
                        pool.wait_ge(ada_ops, at + 1)
                        pool.tensor_tensor(w[:, 0:2, :], w[:, 0:2, :], w[:, 2:4, :], ALU.add).then_inc(ada_ops, 1)
                        pool.wait_ge(ada_ops, at + 2)
                        if u == 0:
                            pool.wait_ge(ada_red, n + 1)
                            pool.tensor_tensor(CA[:, 1, :], w[:, 0, :], w[:, 1, :], ALU.add).then_inc(ada_ops, 1)
                        else:
                            pool.tensor_tensor(w[:, 0, :], w[:, 0, :], w[:, 1, :], ALU.add).then_inc(ada_ops, 1)
                            pool.wait_ge(ada_ops, at + 3)
                            pool.tensor_tensor(CA[:, 1, :], CA[:, 1, :], w[:, 0, :], ALU.add).then_inc(ada_ops, 1)

            add_condition(st_in)

            pool.wait_ge(evac_done, evacuated(st_in))
            pool.wait_ge(in_cst, 48)
            count = 0

            def step(ins):
                nonlocal count
                count += 1
                ins.then_inc(poolstep, 1)

            for g, w in enumerate(WINDOWS):
                u_t = R[:, 24 + 2 * g:26 + 2 * g, :]
                src, d, turn = u_t, 1, 0
                while d < w:
                    dst = R[:, 52 + 2 * turn:54 + 2 * turn, :]
                    if count:
                        pool.wait_ge(poolstep, count)
                    step(pool.tensor_copy(dst[:, :, 0:d], src[:, :, 0:d]))
                    step(pool.tensor_tensor(dst[:, :, d:S], src[:, :, d:S], src[:, :, 0:S - d], ALU.add))
                    src, d, turn = dst, 2 * d, 1 - turn
                pool.wait_ge(poolstep, count)
                fix = poolfix[:, 32 * g:32 * g + 32].rearrange("p (a t) -> p a t", a=2)[:, :, 0:w - 1]
                step(pool.tensor_tensor(src[:, :, 0:w - 1], src[:, :, 0:w - 1], fix, ALU.mult))
                pool.wait_ge(poolstep, count)
                step(pool.tensor_scalar(src, src, 1.0 / w, None, ALU.mult))
                pool.wait_ge(poolstep, count)
                step(pool.tensor_tensor(u_t, src, u_t, ALU.subtract))
                pool.wait_ge(poolstep, count)
                pool.sem_inc(pooled, 1)

            add_condition(st_o)
            pool.wait_ge(evac_done, groups_before(st_o) + 1)
            for c in range(2):
                pool.dma_start(XC32[:, 8 * c:8 * c + 8, 0, 1, :], ctxT[:, 8 * c:8 * c + 8, :]).then_inc(in_ctx, 16)
            for st in (st_up1a, st_dn1, st_up2, st_dn2, st_kv):
                add_condition(st)
            pool.wait_ge(used, used_all(st_kv))
            for kt in range(3):
                pool.dma_start(XC32[:, 13 + kt, :, 1, :], cst[:, C_FLIP + 512 * kt:C_FLIP + 512 * kt + 512].rearrange(
                    "p (a n) -> p a n", a=2)).then_inc(in_rope, 16)
            for st in (st_q1, st_q2, st_ga, st_gb, st_ba, st_bb, st_u1a):
                add_condition(st)
            pool.wait_ge(in_rope, 48)

        @block.scalar
        def _(act):
            def hi(st, b, j):
                gb, u = st.entries[j % st.upb]
                if gb is None and u == ADA_UNITS - 1:
                    return
                act.wait_ge(raw_in[j % RING], filled(st, b, j))
                act.wait_ge(used, unit(st, b, j) + 1)
                if gb is None:
                    for x in range(UK):
                        ins = act.activation(prod[j % RING][:, x, :], raw[j % RING][:, x, :], ACT.Copy,
                                             scale=cond_silu(st, u, x))
                    ins.then_inc(hi_done, 1)
                    return
                if st.ada and RING <= j < st.upb and j - RING in st.cond[:-1]:
                    act.wait_ge(ada_ops, (b + st.ib) * 8 + (ADA_ADDS[st.cond.index(j - RING)] + 1))
                act.activation(whi[j % RING][:], raw[j % RING][:], ACT.Copy).then_inc(
                    hi_done, 2 if st.entries[j % st.upb - 1] == (None, ADA_UNITS - 1) else 1)

            def post(st, b, gb):
                g = group(st, b, gb)
                if st.kind == "conv":
                    t0 = b * 2 + (FT * (gb % 2) + st.feat0)
                    act.wait_ge(vstep, vst(st, b, gb, 0))
                    if gb % 2:
                        act.wait_ge(astep, ast(st, b, gb, -1))
                    for m in range(2):
                        act.activation(Cb[:, m, :], Zp[:, m, 2:S + 2], ACT.Identity,
                                       bias=V[:, ds(t0 + (VEC["conv_b"] + m), 1)],
                                       scale=V[:, ds(t0 + (VEC["conv_w"] + 4 * FT + m), 1)]).then_inc(astep, 1)
                    if gb % 2 == 0:
                        act.wait_ge(evac_done, g + 3)
                        act.activation(Gb[:], Cb[:], ACT.Gelu_apprx_tanh).then_inc(astep, 1)
                elif st.kind == "gate":
                    act.wait_ge(used, grouped(st, b, gb))
                    act.activation(R[:, ds(b * 4 + (st.tile0 + 2 * gb), 2), :], PS[:, gb % 2, :, 0:S],
                                   ACT.Sigmoid).then_inc(astep, 1)
                elif st.kind == "glu" and gb % 2 == 0:
                    act.wait_ge(used, grouped(st, b, gb))
                    act.wait_ge(evac_done, g + 2)
                    act.activation(Gb[:], PS[:, gb % 2, :, 0:S], ACT.Silu).then_inc(astep, 1)

            def body(st, b, final=False):
                for j in range(RING, RING + st.upb):
                    if j < st.upb or not final:
                        hi(st, b, j)
                    elif st.next is not None:
                        hi(st.next, 0, j - st.upb)
                    if j - RING in st.last:
                        post(st, b, st.last.index(j - RING))

            def run(st):
                alone = st.next is None or bool(st.next.ada) != bool(st.ada)
                with act.Fori(0, st.bodies - alone) as b:
                    body(st, b)
                if alone:
                    body(st, st.bodies - 1, final=True)

            def root(i, n=D):
                act.wait_ge(sum_ready, i + 1)
                act.activation(RS[:], NB[:, 0:S], ACT.Sqrt, bias=SM[:, EPS_C:EPS_C + 1],
                               scale=1.0 / n).then_inc(root_ready, 1)

            act.dma_start(V[:], vec).then_inc(in_vec, 16)
            for c in range(4):
                act.dma_start(X[:, 4 * c:4 * c + 4, :], xT[:, 4 * c:4 * c + 4, :]).then_inc(in_x[c], 16)
            act.dma_start(IO[:], cst[:, 0:256]).then_inc(in_cst, 16)
            for kt in range(4):
                act.dma_start(XC32[:, kt, :, 1, :], bass.AP(
                    rel.tensor, 2 * kt * rel.shape[1], [[1, P], [rel.shape[1], 2], [1, S]])).then_inc(in_att, 16)
            act.dma_start(XC32[:, 13, :, 1, :], cst[:, C_FLIP:C_FLIP + 512].rearrange(
                "p (a n) -> p a n", a=2)).then_inc(in_cst, 16)
            act.dma_start(R[:, 32:40, :], pool_w).then_inc(in_cst, 16)

            act.wait_ge(in_vec, 16)
            act.activation(CS[:], V[:, VEC["cond"]:VEC["cond"] + 2 * KT], ACT.Silu).then_inc(silu_done, 1)
            act.wait_ge(silu_done, 1)
            for c in range(4):
                act.wait_ge(in_x[c], 16)
                for kt in range(4 * c, 4 * c + 4):
                    act.activation(XC[:, kt, 0, 0, :], X[:, kt, :], ACT.Copy,
                                   scale=V[:, VEC["pre_mix"] + kt:VEC["pre_mix"] + kt + 1]).then_inc(op_hi, 1)
                hi(st_in, 0, c)
            act.activation(R[:, 0:KT, :], X[:], ACT.Square).then_inc(sq_ready, 1)
            act.wait_ge(cleared, 1)
            root(0)
            run(st_in)

            act.wait_ge(evac_done, evacuated(st_in))
            for j in range(4):
                act.wait_ge(vt_turned, j + 1)
                act.activation(R[:, 40 + 2 * j:42 + 2 * j, :], TP[:, j % 2, :].rearrange("p (a n) -> p a n", a=2),
                               ACT.Copy).then_inc(vt_copied, 1)
            N = 2 * H1
            for i in range(N + 3):
                if i < N:
                    w = 128 * (i % 2 + 1)
                    act.wait_ge(neg_max, i + 1)
                    if i >= 2:
                        act.wait_ge(turned, i - 1)
                    act.activation(R[:, 48 + i % 2, 0:w], PS[:, i % 2, 0, 0:w], ACT.Exp, bias=SM[:, i % 2:i % 2 + 1],
                                   accum_out=SM[:, 2 + i % 2:3 + i % 2]).then_inc(exped, 1)
                if 1 <= i <= N:
                    n = i - 1
                    w = 128 * (n % 2 + 1)
                    act.wait_ge(turned, n + 1)
                    if n >= 2:
                        act.wait_ge(summed, n - 1)
                    act.activation(R[:, 50 + n % 2, 0:w], TP[:, n % 2, 0:w], ACT.Copy).then_inc(pt_copied, 1)
                if i >= 3 and i % 2 == 1:
                    h = (i - 3) // 2
                    act.wait_ge(summed, 2 * h + 2)
                    act.activation(XC[:, h, 0, 0, :], PS[:, h % 2, 1, 0:S], ACT.Copy).then_inc(op_hi, 1)
            for j in range(8):
                act.wait_ge(summed, N + j + 1)
                act.activation(XC[:, 8 + j, 0, 0, :], PS[:, j % 2, 1, 0:S], ACT.Copy,
                               scale=V[:, VEC["pool_scale"] + j:VEC["pool_scale"] + j + 1]).then_inc(op_hi, 1)
            run(st_o)

            root(1)
            for kt in range(KT):
                act.wait_ge(x_new, kt + 1)
                act.activation(XC[:, kt, 0, 0, :], X[:, kt, :], ACT.Copy,
                               scale=V[:, VEC["pre_ffn"] + kt:VEC["pre_ffn"] + kt + 1]).then_inc(op_hi, 1)
            act.activation(R[:, Yt:Yt + KT, :], X[:], ACT.Square).then_inc(sq_ready, 1)
            root(2)
            run(st_up1a)
            run(st_up1b)
            run(st_dn1)
            run(st_up2)

            act.wait_ge(in_ctx, 32)
            act.wait_ge(evac_done, evacuated(st_up2))
            for c in range(2):
                if c:
                    act.wait_ge(acc_ready, 4)
                act.activation(R[:, 48:56, :], XC32[:, 8 * c:8 * c + 8, 0, 1, :], ACT.Square).then_inc(sq_ready, 1)
            root(3)

            def modulated_hi(m, who):
                for c in range(4):
                    act.wait_ge(mod_v, 4 * m + c + 1)
                    act.activation(XC[:, 4 * c:4 * c + 4, 0, who, :], XC32[:, 4 * c:4 * c + 4, 1, who, :],
                                   ACT.Copy).then_inc(mod_hi, 1)

            modulated_hi(0, 1)
            run(st_dn2)

            root(4)
            act.wait_ge(x_new, 2 * KT)
            act.activation(R[:, Yt:Yt + KT, :], X[:], ACT.Square).then_inc(sq_ready, 1)
            root(5)
            modulated_hi(1, 0)
            run(st_kv)
            for j in range(12):
                act.wait_ge(v2_turned, j + 1)
                act.activation(v_cols[:, :, j // 2, j % 2, :], TP[:, j % 2, :].rearrange("p (t d) -> p t d", t=4),
                               ACT.Copy).then_inc(v2_copied, 1)
            run(st_q1)
            run(st_q2)

            act.wait_ge(lam_sum, 1)
            act.activation(SM[:, 22:24], NB[:, 200:202], ACT.Exp).then_inc(lam_exp, 1)
            act.wait_ge(evac_done, evacuated(st_q2))
            act.wait_ge(in_rope, 48)

            def squares(c):
                if c >= 2:
                    act.wait_ge(n_sum, c - 1)
                act.activation(sqb(c), quad(R[:, CH[c][0]:CH[c][0] + 4, :]), ACT.Square).then_inc(n_sq, 1)

            def head_root(lo_col, mid, hi_col, n):
                act.wait_ge(n_sum, n)
                act.activation(HR[:, lo_col:mid], NB[:, lo_col:mid], ACT.Sqrt, bias=SM[:, EPS_C:EPS_C + 1],
                               scale=1.0 / HD)
                act.activation(HR[:, mid:hi_col], NB[:, mid:hi_col], ACT.Sqrt, bias=SM[:, EPS_C:EPS_C + 1],
                               scale=1.0 / 64).then_inc(n_root, 1)

            def swap(c):
                t, br, is_k = CH[c]
                if is_k:
                    act.wait_ge(n_scaled, c + 1)
                if c >= 2:
                    act.wait_ge(n_rope, c - 1)
                s = 32 if br else 64
                for p in range(0, P, 2 * s):
                    for x, y in ((p, p + s), (p + s, p)):
                        src = quad(R[y:y + s, t:t + 4, :])
                        dst = swapb(c)[x:x + s]
                        if is_k:
                            src, dst = src[:, :, 0, :], dst[:, :, 0, :]
                        last = act.activation(dst, src, ACT.Copy)
                last.then_inc(n_swap, 1)

            for c in range(NK):
                squares(c)
            head_root(0, 16, 80, NK)
            for c in range(NK):
                squares(NK + c)
                swap(c)
            head_root(80, 112, 144, 2 * NK)
            for c in range(NK, 2 * NK):
                swap(c)

            for i in range(NA + 3):
                if i < NA:
                    act.wait_ge(a_neg, i + 1)
                    if i >= 2:
                        act.wait_ge(a_turned, i - 1)
                    act.activation(scr(i % 2), PS[:, i % 2, 0, :].rearrange("p (a n) -> p a n", a=2), ACT.Exp,
                                   bias=SM[:, i % 2:i % 2 + 1], scale=HR[:, 80 + i:81 + i],
                                   accum_out=SM[:, 2 + i % 2:3 + i % 2]).then_inc(a_exp, 1)
                if 1 <= i <= NA:
                    n = i - 1
                    act.wait_ge(a_turned, n + 1)
                    if n >= 2:
                        act.wait_ge(a_summed, n - 1)
                    act.activation(scr(2 + n % 2), TP[:, n % 2, :].rearrange("p (a n) -> p a n", a=2),
                                   ACT.Copy).then_inc(a_copied, 1)
                if i >= 3 and i % 2 == 1:
                    h = (i - 3) // 2
                    act.wait_ge(a_summed, 2 * h + 2)
                    act.activation(R[:, qa_tile(h), :], PS[:, h % 2, 1, 0:S], ACT.Copy).then_inc(a_out, 1)
            for i in range(NB_ + 3):
                if i < NB_:
                    act.wait_ge(b_neg, i + 1)
                    if i >= 2:
                        act.wait_ge(b_turned, i - 1)
                    for x in range(2):
                        e = 2 * (i % 2) + x
                        act.activation(scr(e), PS[:, i % 2, x, :].rearrange("p (a n) -> p a n", a=2), ACT.Exp,
                                       bias=SM[:, 6 + e:7 + e], scale=HR[:, 112 + 2 * i + x:113 + 2 * i + x],
                                       accum_out=SM[:, 10 + e:11 + e]).then_inc(b_exp, 1)
                if 1 <= i <= NB_:
                    n = i - 1
                    act.wait_ge(b_turned, n + 1)
                    if n >= 2:
                        act.wait_ge(b_summed, n - 1)
                    act.activation(scr(4 + n % 2), TP[:, n % 2, :].rearrange("p (a n) -> p a n", a=2),
                                   ACT.Copy).then_inc(b_copied, 1)
                if i >= 3 and i % 2 == 1:
                    h = (i - 3) // 2
                    act.wait_ge(b_summed, 2 * h + 2)
                    act.activation(R[:, 40 + h, :], (NB, AB)[h % 2][:, 0:S], ACT.Copy).then_inc(b_out, 1)
            act.wait_ge(b_out, HB)
            act.activation(R[:, 16:24, :], R[:, 40:48, :], ACT.Square).then_inc(o_sq, 1)
            act.wait_ge(o_sum, 1)
            act.activation(R[:, 24:32, :], PS[:].rearrange("p a m (h n) -> p (a m h) n", h=2), ACT.Sqrt,
                           bias=SM[:, EPS_C:EPS_C + 1], scale=1.0 / HD).then_inc(o_root, 1)
            act.wait_ge(o_norm, 1)
            for c in range(2):
                act.activation(XC[:, 4 * c:4 * c + 4, 0, 1, :], R[:, 40 + 4 * c:44 + 4 * c, :],
                               ACT.Copy).then_inc(split_hi, 1)
            run(st_ga)
            run(st_gb)
            for c in range(4):
                act.activation(XC[:, 4 * c:4 * c + 4, 0, 0, :], R[:, O_SRC[c]:O_SRC[c] + 4, :],
                               ACT.Copy).then_inc(split_hi, 1)
            run(st_ba)
            run(st_bb)
            act.wait_ge(evac_done, evacuated(st_bb))
            for c in range(4):
                act.activation(XC[:, 4 * c:4 * c + 4, 0, 0, :], R[:, 16 + 4 * c:20 + 4 * c, :],
                               ACT.Copy).then_inc(split_hi, 1)
            run(st_out)
            root(6)
            modulated_hi(2, 0)
            run(st_u1a)
            run(st_u1b)
            run(st_d1)
            run(st_u2)
            run(st_d2)

        @block.vector
        def _(dve):
            def lo(st, b, j):
                gb, u = st.entries[j % st.upb]
                if gb is None:
                    if u == ADA_UNITS - 1:
                        n = b + (st.ib + j // st.upb)
                        dve.wait_ge(raw_in[j % RING], filled(st, b, j))
                        dve.wait_ge(ada_red, n + 1)
                        for x in range(UK):
                            w, c = raw[j % RING][:, x, :], cond_silu(st, u, x)
                            if x:
                                dve.wait_ge(ada_sum, n * (UK - 1) + x)
                                ins = dve.scalar_tensor_tensor(out=CA[:, 0, :], in0=w, scalar=c, in1=CA[:, 0, :],
                                                               op0=ALU.mult, op1=ALU.add)
                            else:
                                ins = dve.tensor_scalar(CA[:, 0, :], w, c, None, ALU.mult)
                            ins.then_inc(lo_done if x == UK - 1 else ada_sum, 1)
                    return
                dve.wait_ge(hi_done, unit(st, b, j) + 1)
                prev = st.entries[j % st.upb - 1]
                dve.tensor_tensor(wlo[j % RING][:], raw[j % RING][:], whi[j % RING][:].bitcast(F32),
                                  ALU.subtract).then_inc(lo_done, 2 if prev[0] is None and prev[1] < ADA_UNITS - 1
                                                         else 1)

            def evac(st, b, gb):
                g = group(st, b, gb)
                k = st.kind
                sums = PS[:, gb % 2, :, 0:S]
                tile = b * (2 * st.GB) + (st.tile0 + 2 * gb)
                if k == "kv":
                    dve.wait_ge(used, grouped(st, b, gb))
                    dve.tensor_copy(R[:, ds(b * (4 * st.GB) + 4 * gb, 4), :],
                                    PS[:, gb % 2, :, :].rearrange("p m (a n) -> p (m a) n", a=2)).then_inc(evac_done, 1)
                    return
                dve.wait_ge(evac_done, g + 2)
                dve.wait_ge(used, grouped(st, b, gb))
                i = 0

                def did(ins):
                    nonlocal i
                    ins.then_inc(vstep, 1)
                    i += 1

                def settled(n=1):
                    dve.wait_ge(vstep, vst(st, b, gb, i - n))

                def squares_into_rs(src):
                    did(dve.tensor_tensor(Cb[:], src, src, ALU.mult))
                    settled()
                    did(dve.tensor_tensor(RS[:], RS[:], Cb[:, 0, :], ALU.add))
                    settled()
                    dve.tensor_tensor(RS[:], RS[:], Cb[:, 1, :], ALU.add).then_inc(evac_done, 1)

                if k == "q":
                    dve.tensor_copy(R[:, ds(tile, 2), :], sums).then_inc(evac_done, 1)
                elif k == "down1":
                    dve.tensor_copy(R[:, ds(tile + Yt, 2), :], sums).then_inc(evac_done, 1)
                elif k == "gate" or (k == "glu" and gb % 2 == 0):
                    dve.wait_ge(astep, ast(st, b, gb, 0))
                    dve.sem_inc(evac_done, 1)
                elif k == "mix_out":
                    y = R[:, ds(tile + Yt, 2), :]
                    did(dve.tensor_copy(y, sums))
                    settled()
                    squares_into_rs(y)
                else:
                    if k == "scale":
                        dve.tensor_tensor(R[:, ds(tile, 2), :], sums, rep(RS[:], 2), ALU.mult).then_inc(evac_done, 1)
                    elif k == "down2":
                        y = R[:, ds(tile + Yt, 2), :]
                        did(dve.tensor_tensor(y, y, sums, ALU.add))
                        settled()
                        squares_into_rs(y)
                    elif k == "branch_a":
                        ga = R[:, ds(tile + 16, 2), :]
                        dve.tensor_tensor(ga, sums, ga, ALU.mult).then_inc(evac_done, 1)
                    elif k == "branch_b":
                        ga, gb_ = R[:, ds(tile + 16, 2), :], R[:, ds(tile + 48, 2), :]
                        did(dve.tensor_tensor(gb_, sums, gb_, ALU.mult))
                        settled()
                        dve.tensor_tensor(ga, ga, gb_, ALU.add).then_inc(evac_done, 1)
                    elif k in ("out", "down_x"):
                        chunk = 2 if k == "out" else 5
                        for m in range(2):
                            x = X[:, ds(tile + m, 1), :].rearrange("p a n -> p (a n)")
                            ins = dve.scalar_tensor_tensor(
                                out=x, in0=sums[:, m, :], scalar=MOD[:, ds(tile + (2 * ADA_CTX + KT * chunk + m), 1)],
                                in1=x, op0=ALU.mult, op1=ALU.add)
                            if m == 1 and k == "down_x":
                                ins.then_inc(evac_done, 1)
                            else:
                                did(ins)
                        if k == "out":
                            settled()
                            squares_into_rs(X[:, ds(tile, 2), :])
                    elif k == "conv":
                        did(dve.tensor_tensor(Zp[:, :, 2:S + 2], sums, rep(RS[:], 2), ALU.mult))
                        settled()
                        t0 = b * 2 + (FT * (gb % 2) + st.feat0 + VEC["conv_w"])
                        for tap in (1, 0):
                            for m in range(2):
                                if tap:
                                    dve.wait_ge(astep, ast(st, b, gb, m))
                                else:
                                    settled(2)
                                ins = dve.scalar_tensor_tensor(
                                    out=Cb[:, m, :], in0=Zp[:, m, tap:S + tap],
                                    scalar=V[:, ds(t0 + (2 * FT * tap + m), 1)], in1=Cb[:, m, :],
                                    op0=ALU.mult, op1=ALU.add)
                                if gb % 2 == 0 and tap == 0 and m == 1:
                                    ins.then_inc(evac_done, 1)
                                else:
                                    did(ins)
                    if gb % 2 and k in ("conv", "glu"):
                        val = Cb if k == "conv" else Gb
                        dve.wait_ge(astep, ast(st, b, 0, 2 if k == "conv" else 0))
                        if k == "conv":
                            settled()
                        did(dve.tensor_tensor(val[:], Cb[:] if k == "conv" else sums, Gb[:], ALU.mult))
                        settled()
                        f = b * 2 + st.tile0
                        fh, fl = FH[:, ds(f, 2), 0, :], FH[:, ds(f, 2), 1, :]
                        did(dve.tensor_copy(fh, val[:]))
                        settled()
                        dve.tensor_tensor(fl, val[:], fh.bitcast(F32), ALU.subtract).then_inc(evac_done, 1)

            def store_mods(st, b):
                n = b + st.ib
                dve.wait_ge(ada_red, n + 2)
                dve.tensor_tensor(MOD[:, ds(n * 2, 2)], AB[:, 0:2], V[:, ds(n * 2 + VEC["b_ada"], 2)],
                                  ALU.add).then_inc(mods_done, 1)

            def body(st, b, final=False):
                for j in range(RING, RING + st.upb):
                    if j < st.upb or not final:
                        lo(st, b, j)
                    elif st.next is not None:
                        lo(st.next, 0, j - st.upb)
                    if j - RING in st.last:
                        evac(st, b, st.last.index(j - RING))
                if st.ada:
                    store_mods(st, b)

            def run(st):
                alone = st.next is None or bool(st.next.ada) != bool(st.ada)
                with dve.Fori(0, st.bodies - alone) as b:
                    body(st, b)
                if alone:
                    body(st, st.bodies - 1, final=True)

            def invert(i):
                dve.wait_ge(root_ready, i + 1)
                dve.reciprocal(RS[:], RS[:]).then_inc(rstd_ready, 1)
                dve.wait_ge(rstd_ready, i + 1)

            def reduce_squares(first, n_tiles, dst):
                return dve.tensor_reduce(dst, R[:, first:first + n_tiles, :].rearrange("p k n -> p n k"), AX.X, ALU.add)

            n_clear = 0

            def clear(ap, value=0.0):
                nonlocal n_clear
                dve.memset(ap, value).then_inc(cleared, 1)
                n_clear += 1
                dve.wait_ge(cleared, n_clear)

            dve.sem_inc(lo_done, RING)
            dve.sem_inc(evac_done, 2)
            dve.sem_inc(ada_ops, 1)
            dve.sem_inc(mods_done, 1)
            clear(SM[:, EPS_C:EPS_C + 1], EPS)
            dve.wait_ge(in_vec, 16)
            dve.tensor_scalar(SM[:, 30:31], V[:, VEC["q_a"]:VEC["q_a"] + 1], HD ** -0.5, None, ALU.mult)
            dve.tensor_scalar(SM[:, 31:32], V[:, VEC["q_b"]:VEC["q_b"] + 1], 64 ** -0.5, None, ALU.mult)
            dve.tensor_scalar(SM[:, 33:34], V[:, VEC["q_a_sw"]:VEC["q_a_sw"] + 1], HD ** -0.5, None, ALU.mult)
            dve.tensor_scalar(SM[:, 34:35], V[:, VEC["q_b_sw"]:VEC["q_b_sw"] + 1], 64 ** -0.5, None, ALU.mult)
            dve.tensor_scalar(SM[:, 32:33], V[:, VEC["subln"]:VEC["subln"] + 1], 1 - LAM_INIT, None,
                              ALU.mult)
            dve.tensor_tensor(SM[:, 28:30], V[:, VEC["lam"]:VEC["lam"] + 4:2], V[:, VEC["lam"] + 1:VEC["lam"] + 4:2],
                              ALU.mult).then_inc(gains, 1)
            dve.wait_ge(gains, 1)

            def scaled_lo(kt, gain, n_hi, source):
                dve.wait_ge(op_hi, n_hi)
                dve.scalar_tensor_tensor(out=XC[:, kt, 1, 0, :], in0=source, scalar=gain,
                                         in1=XC[:, kt, 0, 0, :].bitcast(F32), op0=ALU.mult,
                                         op1=ALU.subtract).then_inc(opnd, 1)

            gain_col = lambda name, kt: V[:, VEC[name] + kt:VEC[name] + kt + 1]
            dve.wait_ge(silu_done, 1)
            for kt in range(KT):
                scaled_lo(kt, gain_col("pre_mix", kt), kt + 1, X[:, kt, :])
                if kt % 4 == 3:
                    lo(st_in, 0, kt // 4)
            dve.wait_ge(sq_ready, 1)
            reduce_squares(0, KT, RS[:]).then_inc(acc_ready, 1)
            invert(0)
            run(st_in)

            dve.wait_ge(evac_done, evacuated(st_in))
            dve.tensor_scalar(R[:, 0:8, :], R[:, 0:8, :], HD ** -0.5, None, ALU.mult).then_inc(q_scaled, 1)
            clear(RS[:])
            N = 2 * H1
            for i in range(N + 4):
                if i < N:
                    w = 128 * (i % 2 + 1)
                    dve.wait_ge(scored, i + 1)
                    dve.tensor_reduce(SM[:, i % 2:i % 2 + 1], PS[:, i % 2, 0, 0:w], AX.X, ALU.max,
                                      negate=True).then_inc(neg_max, 1)
                if 1 <= i <= N:
                    n = i - 1
                    w = 128 * (n % 2 + 1)
                    dve.wait_ge(exped, n + 1)
                    dve.reciprocal(SM[:, 4 + n % 2:5 + n % 2], SM[:, 2 + n % 2:3 + n % 2]).then_inc(inverse, 1)
                    dve.wait_ge(inverse, n + 1)
                    dve.tensor_scalar(R[:, 48 + n % 2, 0:w], R[:, 48 + n % 2, 0:w], SM[:, 4 + n % 2:5 + n % 2], None,
                                      ALU.mult).then_inc(probs, 1)
                if i >= 4 and i % 2 == 0:
                    h = (i - 4) // 2
                    dve.wait_ge(op_hi, KT + h + 1)
                    dve.tensor_tensor(XC[:, h, 1, 0, :], PS[:, h % 2, 1, 0:S], XC[:, h, 0, 0, :].bitcast(F32),
                                      ALU.subtract).then_inc(opnd, 1)
            for j in range(8):
                scaled_lo(8 + j, gain_col("pool_scale", j), KT + H1 + j + 1, PS[:, j % 2, 1, 0:S])
            run(st_o)

            def add_normed(i, name):
                dve.wait_ge(evac_done, evacuated(st_o if i == 0 else st_dn2))
                dve.sem_inc(acc_ready, 1)
                invert(1 if i == 0 else 4)
                for c in range(5):
                    if c < 4:
                        y = R[:, Yt + 4 * c:Yt + 4 * c + 4, :]
                        dve.tensor_tensor(y, y, rep(RS[:], 4), ALU.mult).then_inc(y_normed, 1)
                        dve.wait_ge(y_normed, 4 * i + c + 1)
                        for kt in range(4 * c, 4 * c + 4):
                            dve.scalar_tensor_tensor(out=X[:, kt, :], in0=R[:, Yt + kt, :], scalar=gain_col(name, kt),
                                                     in1=X[:, kt, :], op0=ALU.mult, op1=ALU.add).then_inc(x_new, 1)
                    if c >= 1 and i == 0:
                        for kt in range(4 * c - 4, 4 * c):
                            scaled_lo(kt, gain_col("pre_ffn", kt), 2 * KT + kt + 1, X[:, kt, :])

            add_normed(0, "post_mix")
            clear(Zp[:, :, 0:2])
            dve.wait_ge(sq_ready, 2)
            reduce_squares(Yt, KT, RS[:]).then_inc(acc_ready, 1)
            invert(2)
            run(st_up1a)
            run(st_up1b)
            run(st_dn1)
            run(st_up2)

            def modulate(m, src, who, gain, base, n_gains):
                dve.scalar_tensor_tensor(out=GS[:], in0=MOD[:, base + KT:base + 2 * KT], scalar=1.0,
                                         in1=V[:, VEC[gain]:VEC[gain] + KT], op0=ALU.add, op1=ALU.mult
                                         ).then_inc(gains, 1)
                dve.wait_ge(gains, n_gains)
                for c in range(5):
                    if c < 4:
                        k = slice(4 * c, 4 * c + 4)
                        dve.tensor_tensor(XC32[:, k, 1, who, :], src[:, k, :], rep(RS[:], 4),
                                          ALU.mult).then_inc(mod_t, 1)
                        dve.wait_ge(mod_t, 4 * m + c + 1)
                        for kt in range(4 * c, 4 * c + 4):
                            v = XC32[:, kt, 1, who, :]
                            last = dve.tensor_scalar(v, v, GS[:, kt:kt + 1], MOD[:, base + kt:base + kt + 1],
                                                     ALU.mult, ALU.add)
                        last.then_inc(mod_v, 1)
                    if c >= 1:
                        k = slice(4 * c - 4, 4 * c)
                        dve.wait_ge(mod_hi, 4 * m + c)
                        dve.tensor_tensor(XC[:, k, 1, who, :], XC32[:, k, 1, who, :], XC[:, k, 0, who, :].bitcast(F32),
                                          ALU.subtract).then_inc(opnd, 4)

            dve.wait_ge(evac_done, evacuated(st_up2))
            dve.wait_ge(mods_done, ADA_CTX + 1)
            dve.wait_ge(sq_ready, 3)
            reduce_squares(48, 8, RS[:]).then_inc(acc_ready, 1)
            dve.wait_ge(sq_ready, 4)
            second = XC32[:, 15, 1, 1, :]
            reduce_squares(48, 8, second).then_inc(y_normed, 1)
            dve.wait_ge(y_normed, 5)
            dve.tensor_tensor(RS[:], RS[:], second, ALU.add).then_inc(acc_ready, 1)
            invert(3)
            modulate(0, XC32[:, :, 0, 1, :], 1, "norm1", 0, 2)
            clear(RS[:])
            run(st_dn2)

            dve.wait_ge(evac_done, evacuated(st_dn2))
            dve.sem_inc(acc_ready, 1)
            invert(4)
            for c in range(4):
                y = R[:, Yt + 4 * c:Yt + 4 * c + 4, :]
                dve.tensor_tensor(y, y, rep(RS[:], 4), ALU.mult).then_inc(y_normed, 1)
                dve.wait_ge(y_normed, 6 + c)
                for kt in range(4 * c, 4 * c + 4):
                    dve.scalar_tensor_tensor(out=X[:, kt, :], in0=R[:, Yt + kt, :], scalar=gain_col("post_ffn", kt),
                                             in1=X[:, kt, :], op0=ALU.mult, op1=ALU.add).then_inc(x_new, 1)
            dve.wait_ge(sq_ready, 5)
            reduce_squares(Yt, KT, RS[:]).then_inc(acc_ready, 1)
            invert(5)
            dve.wait_ge(mods_done, st_kv.ib + 1)
            modulate(1, X, 0, "norm1", 2 * ADA_CTX, 3)
            clear(RS[:])
            run(st_kv)
            run(st_q1)
            run(st_q2)

            dve.wait_ge(lam_exp, 1)
            dve.tensor_tensor(SM[:, 24:25], SM[:, 23:24], SM[:, 22:23], ALU.subtract).then_inc(lam_vec, 1)
            dve.wait_ge(lam_vec, 1)
            dve.tensor_scalar(SM[:, NEGLAM:NEGLAM + 1], SM[:, 24:25], -LAM_INIT, None, ALU.add).then_inc(lam_vec, 1)
            dve.wait_ge(lam_vec, 2)
            dve.wait_ge(evac_done, evacuated(st_q2))
            dve.wait_ge(in_rope, 48)
            dve.wait_ge(n_root, 1)
            dve.reciprocal(HR[:, 0:80], HR[:, 0:80]).then_inc(n_inv, 1)

            def rotate(c):
                t, br, is_k = CH[c]
                chunk, sw, dims = quad(R[:, t:t + 4, :]), swapb(c), (2, 2)
                if is_k:
                    chunk, sw, dims = chunk[:, :, 0, :], sw[:, :, 0, :], (2,)
                cos, sin = XC32[:, 14 + br, 0, 1, :], XC32[:, 14 + br, 1, 1, :]
                dve.wait_ge(n_swap, c + 1)
                dve.tensor_tensor(chunk, chunk, rep(cos, *dims), ALU.mult).then_inc(n_t1, 1)
                dve.tensor_tensor(sw, sw, rep(sin, *dims), ALU.mult).then_inc(n_t2, 1)
                dve.wait_ge(n_t1, c + 1)
                dve.wait_ge(n_t2, c + 1)
                dve.tensor_tensor(chunk, chunk, sw, ALU.add).then_inc(n_rope, 1)

            for c in range(NK + 1):
                if c < NK:
                    t, br, _ = CH[c]
                    chunk = quad(R[:, t:t + 4, :])
                    dve.wait_ge(n_bcast, c + 1)
                    dve.scalar_tensor_tensor(
                        out=chunk, in0=chunk, scalar=gain_col("k_b" if br else "k_a", 0),
                        in1=PS[:, c % 2, :, :].rearrange("p k (a n) -> p k a n", a=2), op0=ALU.mult,
                        op1=ALU.mult).then_inc(n_scaled, 1)
                if c >= 1:
                    rotate(c - 1)
            dve.wait_ge(n_rope, NK)
            for br in range(2):
                dve.tensor_scalar(XC32[:, 14 + br, 0, 1, :], XC32[:, 14 + br, 0, 1, :], SM[:, 30 + br:31 + br], None,
                                  ALU.mult)
                last = dve.tensor_scalar(XC32[:, 14 + br, 1, 1, :], XC32[:, 14 + br, 1, 1, :],
                                         SM[:, 33 + br:34 + br], None, ALU.mult)
            last.then_inc(n_table, 1)
            dve.wait_ge(n_table, 1)
            dve.wait_ge(n_root, 2)
            dve.reciprocal(HR[:, 80:144], HR[:, 80:144]).then_inc(n_inv, 1)
            for c in range(NK, 2 * NK):
                rotate(c)
            dve.wait_ge(n_rope, len(CH))
            dve.wait_ge(n_inv, 2)

            for i in range(NA + 1):
                if i < NA:
                    dve.wait_ge(a_scored, i + 1)
                    dve.tensor_reduce(SM[:, i % 2:i % 2 + 1], PS[:, i % 2, 0, :], AX.X, ALU.max,
                                      negate=True).then_inc(a_max, 1)
                    dve.wait_ge(a_max, i + 1)
                    dve.tensor_tensor(SM[:, i % 2:i % 2 + 1], SM[:, i % 2:i % 2 + 1],
                                      HR[:, 80 + i:81 + i], ALU.mult).then_inc(a_neg, 1)
                if i >= 1:
                    n = i - 1
                    dve.wait_ge(a_exp, n + 1)
                    dve.reciprocal(SM[:, 4 + n % 2:5 + n % 2], SM[:, 2 + n % 2:3 + n % 2]).then_inc(a_inv, 1)
                    dve.wait_ge(a_inv, n + 1)
                    dve.tensor_scalar(scr(n % 2), scr(n % 2), SM[:, 4 + n % 2:5 + n % 2], None,
                                      ALU.mult).then_inc(a_prob, 1)
            for i in range(NB_ + 1):
                if i < NB_:
                    dve.wait_ge(b_scored, i + 1)
                    e = 6 + 2 * (i % 2)
                    dve.tensor_reduce(SM[:, e:e + 2], PS[:, i % 2, :, :], AX.X, ALU.max,
                                      negate=True).then_inc(b_max, 1)
                    dve.wait_ge(b_max, i + 1)
                    dve.tensor_tensor(SM[:, e:e + 2], SM[:, e:e + 2], HR[:, 112 + 2 * i:114 + 2 * i],
                                      ALU.mult).then_inc(b_neg, 1)
                if i >= 1:
                    n = i - 1
                    e = 2 * (n % 2)
                    dve.wait_ge(b_exp, 2 * n + 2)
                    dve.reciprocal(SM[:, 14 + e:16 + e], SM[:, 10 + e:12 + e]).then_inc(b_inv, 1)
                    dve.wait_ge(b_inv, n + 1)
                    dve.tensor_tensor(SM[:, 18 + n % 2:19 + n % 2], SM[:, 15 + e:16 + e], SM[:, NEGLAM:NEGLAM + 1],
                                      ALU.mult).then_inc(b_nl, 1)
                    dve.wait_ge(b_nl, n + 1)
                    dve.tensor_scalar(scr(e + 1), scr(e + 1), SM[:, 18 + n % 2:19 + n % 2], None,
                                      ALU.mult).then_inc(b_p1, 1)
                    dve.wait_ge(b_p1, n + 1)
                    dve.scalar_tensor_tensor(out=scr(e), in0=scr(e), scalar=SM[:, 14 + e:15 + e], in1=scr(e + 1),
                                             op0=ALU.mult, op1=ALU.add).then_inc(b_prob, 1)
            dve.wait_ge(o_root, 1)
            dve.reciprocal(R[:, 24:32, :], R[:, 24:32, :]).then_inc(o_inv, 1)
            dve.wait_ge(o_inv, 1)
            dve.scalar_tensor_tensor(out=R[:, 40:48, :], in0=R[:, 40:48, :], scalar=SM[:, 32:33], in1=R[:, 24:32, :],
                                     op0=ALU.mult, op1=ALU.mult).then_inc(o_norm, 1)
            dve.wait_ge(o_norm, 1)

            def split_lo(k0, who, tile, n):
                dve.wait_ge(split_hi, n)
                dve.tensor_tensor(XC[:, k0:k0 + 4, 1, who, :], R[:, tile:tile + 4, :],
                                  XC[:, k0:k0 + 4, 0, who, :].bitcast(F32), ALU.subtract).then_inc(opnd, 4)

            for c in range(2):
                split_lo(4 * c, 1, 40 + 4 * c, c + 1)
            run(st_ga)
            run(st_gb)
            for c in range(4):
                split_lo(4 * c, 0, O_SRC[c], 3 + c)
            run(st_ba)
            run(st_bb)
            for c in range(4):
                split_lo(4 * c, 0, 16 + 4 * c, 7 + c)
            run(st_out)
            dve.wait_ge(evac_done, evacuated(st_out))
            dve.sem_inc(acc_ready, 1)
            invert(6)
            dve.wait_ge(mods_done, st_u1a.ib + 1)
            modulate(2, X, 0, "norm2", 2 * ADA_CTX + 3 * KT, 4)
            run(st_u1a)
            run(st_u1b)
            run(st_d1)
            run(st_u2)
            run(st_d2)

        @block.tensor
        def _(pe):
            def multiply(st, b, j, fresh):
                gb, u = st.entries[j]
                pe.wait_ge(lo_done, unit(st, b, j) + 1 + RING)
                if fresh and st.op is not None:
                    pe.wait_ge(opnd, st.op + 4 * (u + 1))
                if fresh and st.act:
                    pe.wait_ge(evac_done, groups_before(st.after) + min(4 * (u + 1), st.gb - st.after.gb))
                h, l = whi[j % RING], wlo[j % RING]
                for x in range(UK):
                    kt = UK * u + x
                    first, last = kt == 0, kt == UK * st.U - 1
                    for m in range(2):
                        f = slice(P * m, P * m + P)
                        if st.kind == "kv":
                            out_ = PS[:, gb % 2, m, :].rearrange("p (a n) -> p a n", a=2)
                            mov = XC[:, kt, :, :, :]
                        else:
                            out_ = PS[:, gb % 2, m, 0:S]
                            mov = FH[:, kt, :, :] if st.act else XC[:, kt, :, st.who, :]
                        pe.matmul(out_, h[:, x, f], mov[:, 0], start=first, stop=False)
                        pe.matmul(out_, h[:, x, f], mov[:, 1], start=False, stop=False)
                        ins = pe.matmul(out_, l[:, x, f], mov[:, 0], start=False, stop=last)
                ins.then_inc(used, 2 if st.entries[j - 1][0] is None else 1)

            def take_condition(st, b):
                n = b + st.ib
                pe.wait_ge(ada_ops, n * 8 + (ADA_ADDS[-1] + 1))
                pe.wait_ge(mods_done, n + 1)
                for m in range(2):
                    for part in range(2):
                        ins = pe.matmul(AB[:, m:m + 1], CA[:, part, P * m:P * m + P], ones[:, 0:1],
                                        start=part == 0, stop=part == 1)
                ins.then_inc(ada_red, 1)

            def body(st, b, fresh=True, insert=None):
                for j, (gb, u) in enumerate(st.entries):
                    if gb is None:
                        continue
                    if u == 0:
                        pe.wait_ge(evac_done, group(st, b, gb) + 1)
                    multiply(st, b, j, fresh and gb == 0)
                    if insert is not None and gb == u == 0:
                        sum_squares(insert)
                if st.ada:
                    take_condition(st, b)

            def run(st, insert=None):
                if insert is not None:
                    body(st, 0, insert=insert)
                    with pe.Fori(1, st.bodies) as b:
                        body(st, b, fresh=False)
                else:
                    with pe.Fori(0, st.bodies) as b:
                        body(st, b)

            def sum_squares(i):
                pe.wait_ge(acc_ready, ACC[i])
                pe.matmul(NB[:, 0:S], ones, RS[:], start=True, stop=True).then_inc(sum_ready, 1)

            pe.sem_inc(used, RING)
            pe.sem_inc(ada_red, 1)
            pe.wait_ge(in_cst, 48)
            run(st_in, insert=0)

            pe.wait_ge(evac_done, evacuated(st_in))
            pe.wait_ge(masked, 1)
            for j in range(4):
                if j >= 2:
                    pe.wait_ge(vt_copied, j - 1)
                for x in range(4):
                    h, tb = 4 * (j % 2) + x, j // 2
                    ins = pe.transpose(TP[:, j % 2, P * x:P * x + P], R[:, 16 + h, P * tb:P * tb + P], ident)
                ins.then_inc(vt_turned, 1)
            pe.wait_ge(q_scaled, 1)
            N = 2 * H1

            def score(n):
                h, b = divmod(n, 2)
                w = P * (b + 1)
                if n >= 2:
                    pe.wait_ge(exped, n - 1)
                pe.matmul(PS[:, n % 2, 0, 0:w], R[:, h, P * b:P * b + P], R[:, 8 + h, 0:w], start=True, stop=False)
                pe.matmul(PS[:, n % 2, 0, 0:w], flip, hankel(h)[:, P * (1 - b):P * (1 - b) + w], start=False,
                          stop=True).then_inc(scored, 1)

            score(0)
            score(1)
            pe.wait_ge(vt_copied, 4)
            for i in range(N + 1):
                if i < N:
                    pe.wait_ge(probs, i + 1)
                    if i >= 2:
                        pe.wait_ge(pt_copied, i - 1)
                    for t in range(i % 2 + 1):
                        ins = pe.transpose(TP[:, i % 2, P * t:P * t + P], R[:, 48 + i % 2, P * t:P * t + P], ident)
                    ins.then_inc(turned, 1)
                if i + 2 < N:
                    score(i + 2)
                if i >= 1:
                    n = i - 1
                    h, b = divmod(n, 2)
                    pe.wait_ge(pt_copied, n + 1)
                    if b == 0 and h >= 2:
                        pe.wait_ge(opnd, KT + h - 1)
                    for t in range(b + 1):
                        ins = pe.matmul(PS[:, h % 2, 1, P * b:P * b + P],
                                        R[:, 40 + 4 * t + h // 2, P * (h % 2):P * (h % 2) + P],
                                        R[:, 50 + n % 2, P * t:P * t + P], start=t == 0, stop=t == b)
                    ins.then_inc(summed, 1)
            for j in range(8):
                g = j // 2
                pe.wait_ge(pooled, g + 1)
                pe.wait_ge(opnd, KT + H1 + j - 1)
                for c in range(2):
                    ins = pe.matmul(PS[:, j % 2, 1, 0:S], R[:, 32 + 2 * g + c, P * (j % 2):P * (j % 2) + P],
                                    R[:, 24 + 2 * g + c, :], start=c == 0, stop=c == 1)
                ins.then_inc(summed, 1)
            pe.wait_ge(opnd, 2 * KT)
            run(st_o)
            sum_squares(1)
            run(st_up1a, insert=2)
            run(st_up1b)
            run(st_dn1)
            run(st_up2)
            sum_squares(3)
            run(st_dn2)
            sum_squares(4)
            sum_squares(5)
            pe.wait_ge(opnd, 4 * KT)
            run(st_kv)

            pe.wait_ge(evac_done, evacuated(st_kv))
            for j in range(12):
                if j >= 2:
                    pe.wait_ge(v2_copied, j - 1)
                tile = 8 + 2 * j if j < 4 else 24 + 2 * j
                for t in range(4):
                    ins = pe.transpose(TP[:, j % 2, P * t:P * t + P],
                                       R[:, tile + t // 2, P * (t % 2):P * (t % 2) + P], ident)
                ins.then_inc(v2_turned, 1)
            run(st_q1)
            run(st_q2)

            pe.wait_ge(gains, 1)
            pe.matmul(NB[:, 200:202], ones, SM[:, 28:30], start=True, stop=True).then_inc(lam_sum, 1)
            pe.wait_ge(in_rope, 48)
            pe.wait_ge(evac_done, evacuated(st_q2))
            pe.wait_ge(lam_exp, 1)

            def head_sums(c):
                br = CH[c][1]
                pe.wait_ge(n_sq, c + 1)
                for x in range(4):
                    for t in range(2):
                        at = hr_col(c, x, t)
                        ins = pe.matmul(NB[:, at:at + 1 + br], sqb(c)[:, x // 2, x % 2, P * t:P * t + P],
                                        halves[:, 0:128:64] if br else ones[:, 0:1], start=True, stop=True)
                ins.then_inc(n_sum, 1)

            for c in range(NK):
                head_sums(c)
            pe.wait_ge(n_inv, 1)
            for c in range(NK):
                if c >= 2:
                    pe.wait_ge(n_scaled, c - 1)
                br = CH[c][1]
                for x in range(4):
                    for t in range(2):
                        at = hr_col(c, x, t)
                        for i in range(1 + br):
                            col = HR[:, at + i:at + i + 1]
                            n = P >> br
                            ins = pe.matmul(PS[n * i:n * i + n, c % 2, x // 2, S * (x % 2) + P * t:S * (x % 2) + P * t + P],
                                            bass.AP(col.tensor, col.offset, [col.ap[0], [0, n]]), ident,
                                            start=True, stop=True)
                ins.then_inc(n_bcast, 1)
                head_sums(NK + c)

            def turn(n, buf, prob, copied, done):
                pe.wait_ge(prob, n + 1)
                if n >= 2:
                    pe.wait_ge(copied, n - 1)
                for t in range(4):
                    ins = pe.transpose(TP[:, n % 2, P * t:P * t + P], buf[:, t // 2, P * (t % 2):P * (t % 2) + P],
                                       ident)
                ins.then_inc(done, 1)

            def values(n, dst, j, buf, copied, done):
                pe.wait_ge(copied, n + 1)
                for t in range(4):
                    ins = pe.matmul(dst, v_at(j, t), buf[:, t // 2, P * (t % 2):P * (t % 2) + P],
                                    start=t == 0, stop=t == 3)
                ins.then_inc(done, 1)

            def score_a(n):
                h, b = divmod(n, 2)
                if n >= 2:
                    pe.wait_ge(a_exp, n - 1)
                pe.matmul(PS[:, n % 2, 0, :].rearrange("p (a n) -> p a n", a=2),
                          R[:, qa_tile(h), P * b:P * b + P], R[:, 2 * (h // 4):2 * (h // 4) + 2, :],
                          start=True, stop=True).then_inc(a_scored, 1)

            pe.wait_ge(n_rope, len(CH))
            pe.wait_ge(v2_copied, 12)
            score_a(0)
            score_a(1)
            for i in range(NA + 1):
                if i < NA:
                    turn(i, scr(i % 2), a_prob, a_copied, a_turned)
                if i + 2 < NA:
                    score_a(i + 2)
                if i >= 1:
                    n = i - 1
                    h, b = divmod(n, 2)
                    if b == 0 and h >= 2:
                        pe.wait_ge(a_out, h - 1)
                    values(n, PS[:, h % 2, 1, P * b:P * b + P], h // 4, scr(2 + n % 2), a_copied, a_summed)
            pe.wait_ge(a_out, HA)

            def score_b(n):
                h, b = divmod(n, 2)
                if n >= 2:
                    pe.wait_ge(b_exp, 2 * n - 2)
                for x in range(2):
                    rows = slice(64 * x, 64 * x + 64)
                    ins = pe.matmul(PS[:, n % 2, x, :].rearrange("p (a n) -> p a n", a=2),
                                    R[rows, 40 + h, P * b:P * b + P], R[rows, 16 + 2 * h:18 + 2 * h, :],
                                    start=True, stop=True)
                ins.then_inc(b_scored, 1)

            score_b(0)
            score_b(1)
            for i in range(NB_ + 1):
                if i < NB_:
                    turn(i, scr(2 * (i % 2)), b_prob, b_copied, b_turned)
                if i + 2 < NB_:
                    score_b(i + 2)
                if i >= 1:
                    n = i - 1
                    h, b = divmod(n, 2)
                    if b == 0 and h >= 2:
                        pe.wait_ge(b_out, h - 1)
                    values(n, (NB, AB)[h % 2][:, P * b:P * b + P], 4 + h, scr(4 + n % 2), b_copied, b_summed)
            pe.wait_ge(o_sq, 1)
            for t in range(4):
                ins = pe.matmul(PS[:, t // 2, t % 2, :].rearrange("p (a n) -> p a n", a=2), ones,
                                R[:, 16 + 2 * t:18 + 2 * t, :], start=True, stop=True)
            ins.then_inc(o_sum, 1)
            pe.wait_ge(o_root, 1)
            run(st_ga)
            run(st_gb)
            run(st_ba)
            run(st_bb)
            run(st_out)
            sum_squares(6)
            run(st_u1a)
            run(st_u1b)
            run(st_d1)
            run(st_u2)
            run(st_d2)


def rotations():
    rows = np.repeat(np.arange(S // 64, dtype=np.float32), 64)
    col = np.tile(np.arange(64, dtype=np.float32), S // 64)
    out = []
    for hd in (128, 64):
        n = hd // 4
        freqs = np.float32(10000.0) ** (-np.arange(n, dtype=np.float32) / np.float32(n))
        ang = np.concatenate([rows[:, None] * freqs, col[:, None] * freqs], axis=-1).T.astype(np.float32)
        p = np.arange(P)
        sign = np.where(p % hd < hd // 2, -1.0, 1.0).astype(np.float32)[:, None]
        out += [np.cos(ang)[p % (hd // 2)], sign * np.sin(ang)[p % (hd // 2)]]
    return out


def constants():
    p = np.arange(P)
    fix = np.ones((4, 2, 16), np.float32)
    for g, w in enumerate(WINDOWS):
        fix[g, :, :w - 1] = np.float32(w) / np.arange(1, w, dtype=np.float32)
    parts = [np.eye(P), np.ones((P, P)), np.eye(P)[::-1], (p[:, None] // 64 == p[None, :] // 64).astype(np.float32),
             np.tile(fix.reshape(1, -1), (P, 1)), np.zeros((P, 128))] + rotations()
    return np.ascontiguousarray(np.concatenate(parts, axis=1), dtype=np.float32)


def kernel(**inputs):
    import concourse.bacc as bacc
    from concourse.bass_utils import run_bass_kernel_spmd

    a = {k: np.asarray(v) for k, v in inputs.items()}
    tiles = lambda v: v.reshape(-1, P).T
    taps = lambda w: np.concatenate([tiles(r) for r in w], axis=1)
    b_ada = tiles(a["b_ada_2"][0])

    def column(v):
        c = np.zeros((P, 1), v.dtype)
        c[:v.size, 0] = v.reshape(-1)
        return c

    twice = lambda v: np.concatenate([v, v]).reshape(P, 1)
    vec = np.concatenate(
        [tiles(a[n][0]) for n in ("pre_mix_g", "post_mix_g", "pre_ffn_g", "post_ffn_g", "norm1_g_2", "norm2_g_2")]
        + [taps(a["conv_w"][0]), tiles(a["conv_b"][0]), tiles(a["pool_scale"][0]),
           column(a["q_norm_a_2"][0]), column(a["k_norm_a_2"][0]), twice(a["q_norm_b_2"][0]), twice(a["k_norm_b_2"][0]),
           tiles(a["c_ctx_2"]), tiles(a["c_2"][0])]
        + [column(a[n][0]) for n in ("lam_q1_2", "lam_k1_2", "lam_q2_2", "lam_k2_2")]
        + [b_ada[:, :2 * KT], b_ada, column(a["subln_g_2"][0]),
           np.roll(a["q_norm_a_2"][0], HD // 2).reshape(P, 1), twice(np.roll(a["q_norm_b_2"][0], 32))], axis=1)
    feature_major = lambda v: np.ascontiguousarray(v.T.reshape(KT, P, S).transpose(1, 0, 2))
    reach = a["rel_bias"].shape[2] // 2
    order = np.clip(S - 1 - np.arange(S + P - 1), -reach, reach) + reach
    arrays = {
        "xT": feature_major(a["x"][0]), "ctxT": feature_major(a["ctx_2"][0]), "vec": np.ascontiguousarray(vec),
        "cst": constants(), "rel": np.ascontiguousarray(a["rel_bias"][0][:, order]), "w_in": a["w_in"][0],
        "pool_w": np.ascontiguousarray(a["pool_w"][0].reshape(8, P, 256).transpose(1, 0, 2)),
        "w_o": a["w_o"][0], "w_up": a["w_up"][0], "w_down": a["w_down"][0], "w_ada": a["w_ada_2"][0],
        "w_in2": a["w_in_2"][0], "w_bra": a["w_br_a_2"][0], "w_brb": a["w_br_b_2"][0], "w_out2": a["w_out_2"][0],
        "w_fg": a["w_ff_gate_2"][0], "w_fu": a["w_ff_up_2"][0], "w_fd": a["w_ff_down_2"][0],
    }
    nc = bacc.Bacc("TRN2", target_bir_lowering=False, num_devices=1)
    args = {n: nc.dram_tensor(n, v.shape, mybir.dt.from_np(v.dtype), kind="ExternalInput").ap()
            for n, v in arrays.items()}
    args["out"] = nc.dram_tensor("out", (P, KT, S), F32, kind="ExternalOutput").ap()
    build(nc, **args)
    r = run_bass_kernel_spmd(nc, [arrays], core_ids=[0])
    got = r.results[0]["out"]
    return got.transpose(1, 0, 2).reshape(D, S).T.reshape(1, S, D)
```

```python
from contextlib import ExitStack
import math

import numpy as np
import concourse.bass as bass
from concourse import mybir

F32 = mybir.dt.float32
F32R = mybir.dt.float32r
ALU = mybir.AluOpType
ACT = mybir.ActivationFunctionType
AX = mybir.AxisListType
ds = bass.ds

P = 128
S = 256
D = 2048
KT = D // P
DFF = 5632
FT = DFF // P
UK = 4
GW = 256
RING = 4
HD = 128
H1 = 8
HA, HB = 16, 8
EPS = 1e-6
WINDOWS = (2, 4, 8, 16)
FIRST_HALF = 24
KVW, QW = 3072, 3072
ADA_CTX = 16
ADA_ITEMS = 64
ADA_VEC = 2
ADA_AFTER = (0, 2, 4, 5)
ADA_ADDS = {0: 2, 1: 5, 3: 8}
ADA_OPS = 9
LAM_INIT = 0.8 - 0.6 * math.exp(-0.3 * 0)

VEC = {}
_at = 0
for _name, _n in (("pre_mix", KT), ("post_mix", KT), ("pre_ffn", KT), ("post_ffn", KT), ("norm1", KT), ("norm2", KT),
                  ("conv_w", 3 * 2 * FT), ("conv_b", 2 * FT), ("pool_scale", 8), ("q_a", 1), ("k_a", 1), ("q_b", 1),
                  ("k_b", 1), ("cond", 2 * KT), ("lam", 4), ("b_ada", 2 * ADA_ITEMS), ("subln", 1), ("q_a_sw", 1), ("q_b_sw", 1)):
    VEC[_name] = _at
    _at += _n
NVEC = _at

C_FLIP, C_ROPE = 256, 768


class Stage:

    def __init__(self, name, src, groups, units, kind, per_body=2, ada=0, who=0, act=False, tile0=0, feat0=0, op=None, after=None):
        self.name, self.src, self.G, self.U, self.kind = name, src, groups, units, kind
        self.GB, self.ada, self.who, self.act = per_body, ada, who, act
        self.tile0, self.feat0 = tile0, feat0
        self.op = op
        self.after = after
        self.bodies = groups // per_body
        self.entries, self.last, self.cond = [], [], []
        for j in range(units * per_body):
            self.entries.append(divmod(j, units))
            if j % units == units - 1:
                self.last.append(len(self.entries) - 1)
            if ada and j in ADA_AFTER:
                self.cond.append(len(self.entries))
                self.entries.append((None, ADA_AFTER.index(j)))
        self.upb = len(self.entries)
        assert groups % per_body == 0 and self.upb % RING == 0


V_STEPS = {"scale": 0, "mix_out": 3, "conv": (6, 9), "down1": 0, "down2": 3, "kv": 0, "q": 0, "gate": 0,
           "branch_a": 0, "branch_b": 1, "out": 4, "glu": (0, 2), "down_x": 1}
A_STEPS = {"conv": (1, 0), "gate": (1, 1), "glu": (1, 0)}


def steps(table, kind, gb):
    n = table.get(kind, 0)
    return n[gb % 2] if isinstance(n, tuple) else n


def number(stages):
    u = g = v = a = n = 0
    for st in stages:
        st.ub, st.gb, st.vb, st.ab, st.ib = u, g, v, a, n
        st.vpb = sum(steps(V_STEPS, st.kind, i) for i in range(st.GB))
        st.apb = sum(steps(A_STEPS, st.kind, i) for i in range(st.GB))
        u += st.upb * st.bodies
        g += st.G
        v += st.vpb * st.bodies
        a += st.apb * st.bodies
        n += st.ada * st.bodies
    for st, after in zip(stages, stages[1:] + [None]):
        st.next = after
    assert n == ADA_ITEMS
    return stages


def build(nc, xT, ctxT, vec, cst, rel, w_in, pool_w, w_o, w_up, w_down, w_ada, w_in2, w_bra, w_brb, w_out2,
          w_fg, w_fu, w_fd, out):
    km = lambda w: w.rearrange("(k p) n -> p k n", p=P)
    W = {k: km(v) for k, v in dict(w_in=w_in, w_o=w_o, w_up=w_up, w_down=w_down, w_in2=w_in2, bra=w_bra, brb=w_brb,
                                   out=w_out2, fg=w_fg, fu=w_fu, fd=w_fd).items()}
    ada_src = km(w_ada)

    def cols(w, k, c0, stride):
        return lambda b, GB, gb, u: W[w][:, k + UK * u:k + UK * u + UK, ds((b * GB + gb) * stride + c0, GW)]

    def pairs(wg, wu, g0, u0):
        return lambda b, GB, gb, u: W[(wg, wu)[gb % 2]][:, UK * u:UK * u + UK,
                                                          ds(b * GW + (g0, u0)[gb % 2], GW)]

    h1c = FIRST_HALF // 2 * GW
    n1, n2 = FIRST_HALF // 2, (FT - FIRST_HALF) // 2
    st_in = Stage("w_in", cols("w_in", 0, 0, GW), 16, 4, "scale", ada=1, op=0)
    st_o = Stage("w_o", cols("w_o", 0, 0, GW), 8, 4, "mix_out", ada=1, op=16)
    st_up1a = Stage("up1a", pairs("w_up", "w_up", 0, DFF), 8, 4, "conv", ada=1, op=32)
    st_up1b = Stage("up1b", pairs("w_up", "w_up", 4 * GW, DFF + 4 * GW), 2 * n1 - 8, 4, "conv", tile0=8, feat0=8)
    st_dn1 = Stage("down1", cols("w_down", 0, 0, GW), 8, 6, "down1", ada=1, act=True, after=st_up1a)
    st_up2 = Stage("up2", pairs("w_up", "w_up", h1c, DFF + h1c), 2 * n2, 4, "conv", ada=1, feat0=FIRST_HALF)
    st_dn2 = Stage("down2", cols("w_down", FIRST_HALF, 0, GW), 8, 5, "down2", per_body=4, ada=1, act=True, after=st_up2)
    st_kv = Stage("kv", cols("w_in2", 0, 0, GW), KVW // GW, 4, "kv", ada=1, op=64)
    st_q1 = Stage("q_first", cols("w_in2", 0, KVW, GW), 4, 4, "q", ada=1, tile0=8)
    st_q2 = Stage("q_rest", cols("w_in2", 0, KVW + 1024, GW), 8, 4, "q", ada=1, tile0=32)
    st_ga = Stage("gate_a", cols("w_in2", 0, KVW + QW, GW), 8, 4, "gate", ada=1, tile0=16)
    st_gb = Stage("gate_b", cols("w_in2", 0, KVW + QW + D, GW), 8, 4, "gate", ada=1, tile0=48)
    st_ba = Stage("branch_a", cols("bra", 0, 0, GW), 8, 4, "branch_a", ada=1, op=88)
    st_bb = Stage("branch_b", cols("brb", 0, 0, GW), 8, 2, "branch_b", per_body=4, ada=1, who=1)
    st_out = Stage("out", cols("out", 0, 0, GW), 8, 4, "out", op=104)
    st_u1a = Stage("glu1a", pairs("fg", "fu", 0, 0), 12, 4, "glu", ada=1, op=120)
    st_u1b = Stage("glu1b", pairs("fg", "fu", 6 * GW, 6 * GW), 2 * n1 - 12, 4, "glu", tile0=12)
    st_d1 = Stage("fdown1", cols("fd", 0, 0, GW), 8, 6, "down_x", act=True, after=st_u1a)
    st_u2 = Stage("glu2", pairs("fg", "fu", h1c, h1c), 2 * n2, 4, "glu")
    st_d2 = Stage("fdown2", cols("fd", FIRST_HALF, 0, GW), 8, 5, "down_x", per_body=4, act=True, after=st_u2)
    stages = number([st_in, st_o, st_up1a, st_up1b, st_dn1, st_up2, st_dn2, st_kv, st_q1, st_q2, st_ga, st_gb, st_ba, st_bb,
                     st_out, st_u1a, st_u1b, st_d1, st_u2, st_d2])

    with ExitStack() as ctx:
        place = {"at": 16512}

        def here(n_bytes):
            at = place["at"]
            place["at"] += n_bytes
            return at

        def sb(name, shape, dt, at):
            return nc.alloc_sbuf_tensor_at(name, shape, dt, offset=at)

        unit_b = UK * GW * 4
        raw = [sb(f"raw{i}", [P, UK, GW], F32, here(unit_b)) for i in range(RING)]
        whi = [sb(f"whi{i}", [P, UK, GW], F32R, here(unit_b)) for i in range(RING)]
        wlo = [sb(f"wlo{i}", [P, UK, GW], F32R, here(unit_b)) for i in range(RING)]
        prod = [sb(f"cond_products{i}", [P, UK, GW], F32, 16512 + (RING + i) * unit_b) for i in range(RING)]
        X = sb("x_res", [P, KT, S], F32, here(KT * S * 4))
        xc_at = here(KT * 4 * S * 4)
        XC = sb("operand", [P, KT, 2, 2, S], F32R, xc_at)
        XC32 = sb("operand_scratch", [P, KT, 2, 2, S], F32, xc_at)
        r_at = here(72 * S * 4)
        R = sb("tiles", [P, 72, S], F32, r_at)
        FH = sb("ffn_act", [P, FIRST_HALF, 2, S], F32R, r_at)
        Zp = sb("conv_in", [P, 2, S + 2], F32, r_at + 48 * 1024)
        Cb = sb("conv_out", [P, 2, S], F32, r_at + 48 * 1024 + 2 * (S + 2) * 4 + 16)
        Gb = sb("gate_act", [P, 2, S], F32, r_at + 48 * 1024 + 2 * (S + 2) * 4 + 16 + 2048)
        CA = sb("cond_sums", [P, 2, GW], F32, here(2 * GW * 4))
        IO = sb("ident_ones", [P, 256], F32, here(1024))
        RS = sb("rstd", [P, S], F32, here(S * 4))
        V = sb("vectors", [P, NVEC], F32, here(NVEC * 4 + 28 & ~31))
        MOD = sb("mods", [P, 2 * ADA_ITEMS], F32, here(2 * ADA_ITEMS * 4))
        CS = sb("cond_silu", [P, 2 * KT], F32, here(2 * KT * 4))
        GS = sb("gain_scale", [P, KT], F32, here(KT * 4))
        SM = sb("small", [P, 40], F32, here(160))
        assert place["at"] <= nc.sbuf_usable_end, (place["at"], nc.sbuf_usable_end)
        ident, ones = IO[:, 0:128], IO[:, 128:256]
        scr = lambda kt: XC32[:, kt, :, 1, :]
        flip = XC32[:, 13, 0, 1, 0:128]
        halves = XC32[:, 13, 0, 1, 128:256]
        CR = R[:, 55, :]
        hankel = lambda h: XC32[:, h // 2, h % 2, 1, :]
        poolfix = XC32[:, 13, 1, 1, :]
        EPS_C, NEGLAM = 20, 21
        Yt = 56

        PS = ctx.enter_context(nc.psum_tensor("acc", [P, 2, 2, 512], F32))
        TP = ctx.enter_context(nc.psum_tensor("turned", [P, 2, 512], F32))
        NB = ctx.enter_context(nc.psum_tensor("sums", [P, 512], F32))
        AB = ctx.enter_context(nc.psum_tensor("ada_sums", [P, 512], F32))

        def sem(name):
            return ctx.enter_context(nc.semaphore(name))

        raw_in = [sem(f"raw_in{i}") for i in range(RING)]
        hi_done = sem("hi_done")
        lo_done = sem("lo_done")
        used = sem("used")
        evac_done = sem("evac_done")
        vstep = sem("vstep")
        astep = sem("astep")
        ada_ops = sem("ada_ops")
        ada_sum = sem("ada_sum")
        ada_red = sem("ada_red")
        mods_done = sem("mods_done")
        silu_done = sem("silu_done")
        in_x = [sem(f"in_x{c}") for c in range(4)]
        in_vec, in_ones, in_cst, in_att, in_ctx, in_rope = (sem(f"in_{n}") for n in ("vec", "ones", "cst", "att", "ctx", "rope"))
        sq_ready, acc_ready, sum_ready, root_ready, rstd_ready = (
            sem(n) for n in ("squares_ready", "acc_ready", "sum_ready", "root_ready", "rstd_ready"))
        cleared = sem("acc_cleared")
        op_hi = sem("operand_hi")
        opnd = sem("operand_ready")
        x_new = sem("residual_tile")
        y_normed = sem("normed_chunk")
        y_pool = sem("normed_chunk_pool")
        mod_t, mod_v, mod_hi, gains = sem("mod_scaled"), sem("mod_value"), sem("mod_hi"), sem("gains")
        q_scaled, vt_turned, vt_copied, masked, pooled, poolstep = (
            sem(n) for n in ("q_scaled", "vt_turned", "vt_copied", "masked", "pooled", "poolstep"))
        scored, neg_max, exped, inverse, probs, turned, pt_copied, summed = (
            sem(n) for n in ("scored", "neg_max", "exped", "inverse", "probs", "turned", "pt_copied", "summed"))
        v2_turned, v2_copied = sem("v2_turned"), sem("v2_copied")
        n_sq, n_sum, n_root, n_inv, n_scaled, n_swap, n_t1, n_t2, n_rope, n_bcast, n_table, n_late = (
            sem(n) for n in ("n_sq", "n_sum", "n_root", "n_inv", "n_scaled", "n_swap", "n_t1", "n_t2", "n_rope",
                             "n_bcast", "n_table", "n_late"))
        a_scored, a_neg, a_exp, a_inv, a_prob, a_turned, a_copied, a_summed, a_out = (
            sem(n) for n in ("a_scored", "a_neg", "a_exp", "a_inv", "a_prob", "a_turned", "a_copied", "a_summed",
                             "a_out"))
        b_scored, b_neg, b_exp, b_inv, b_nl, b_p1, b_prob, b_turned, b_copied, b_summed, b_out = (
            sem(n) for n in ("b_scored", "b_neg", "b_exp", "b_inv", "b_nl", "b_p1", "b_prob", "b_turned", "b_copied",
                             "b_summed", "b_out"))
        a_max, b_max = sem("a_max"), sem("b_max")
        lam_exp, lam_sum, lam_vec = sem("lam_exp"), sem("lam_sum"), sem("lam_vec")
        o_sq, o_sum, o_root, o_inv, o_norm = (sem(n) for n in ("o_sq", "o_sum", "o_root", "o_inv", "o_norm"))
        split_hi = sem("split_hi")
        out_stored = sem("out_stored")

        def unit(st, b, j):
            return b * st.upb + (st.ub + j)

        def group(st, b, gb):
            return b * st.GB + (st.gb + gb)

        def vst(st, b, gb, i):
            return b * st.vpb + (st.vb + sum(steps(V_STEPS, st.kind, x) for x in range(gb)) + i + 1)

        def ast(st, b, gb, i):
            return b * st.apb + (st.ab + sum(steps(A_STEPS, st.kind, x) for x in range(gb)) + i + 1)

        def filled(st, b, j):
            return b * (st.upb // RING * 16) + ((st.ub + j) // RING + 1) * 16

        def grouped(st, b, gb):
            return unit(st, b, st.last[gb]) + 1 + RING

        def cond_silu(st, u, x):
            k = (KT if st.ib >= ADA_CTX else 0) + UK * u + x
            return CS[:, k:k + 1]

        def groups_before(st):
            return st.gb + 2

        def evacuated(st):
            return st.gb + st.G + 2

        def used_all(st):
            return st.ub + st.upb * st.bodies + RING

        def rep(ap, *n):
            return bass.AP(ap.tensor, ap.offset, [ap.ap[0]] + [[0, x] for x in n] + [ap.ap[-1]])

        ACC = {1: 1, 3: 2, 4: 3, 6: 4}
        SQ = {0: (0, 0), 2: (4, Yt), 5: (9, Yt)}

        CH = [(0, 0, 1), (4, 0, 1), (16, 1, 1), (20, 1, 1), (24, 1, 1), (28, 1, 1),
              (8, 0, 0), (12, 0, 0), (32, 0, 0), (36, 0, 0), (40, 1, 0), (44, 1, 0)]
        NK = 6
        quad = lambda ap: ap.rearrange("p (k a) n -> p k a n", a=2)
        sqb = lambda c: XC32[:, 2 * (c % 2):2 * (c % 2) + 2, :, 1, :]
        SWAP_AT = (12, 10, 6, 7, 8, 9, 4, 10, 4, 10, 4, 10)

        def rotation(c):
            t, br, is_k = CH[c]
            chunk = quad(R[:, t:t + 4, :])
            if is_k:
                return chunk[:, :, 0, :], XC32[:, SWAP_AT[c], :, 1, :], (2,)
            return chunk, XC32[:, SWAP_AT[c]:SWAP_AT[c] + 2, :, 1, :], (2, 2)

        HR = XC32[:, 13, 1, 1, :]

        K_BODY = {"q_first": (0, 0, 0), "q_rest": (1, 16, 16)}

        def hr_col(c, x, t):
            if c < 2:
                return 2 * (4 * c + x) + t
            if c < 6:
                return 16 + 2 * (2 * (4 * (c - 2) + x) + t)
            if c < 10:
                return 80 + 2 * (4 * (c - 6) + x) + t
            return 112 + 2 * (2 * (4 * (c - 10) + x) + t)
        qa_tile = lambda h: 8 + h if h < 8 else 24 + h
        v_at = lambda j, t: R[:, 48 + 6 * t + j // 2, 128 * (j % 2):128 * (j % 2) + 128]
        v_cols = R[:, 48:72, :].rearrange("p (t j) (a d) -> p t j a d", t=4, a=2)
        NA, NB_ = 2 * HA, 2 * HB
        O_SRC = (8, 12, 32, 36)

        block = ctx.enter_context(nc.Block())

        @block.sync
        def _(sp):
            def load(st, b, prior):
                for j, (gb, u) in enumerate(st.entries):
                    if gb is None:
                        src = ada_src[:, UK * u:UK * u + UK,
                                      ds((b + st.ib) * GW - (ADA_CTX * GW if st.ib >= ADA_CTX else 0), GW)]
                    else:
                        src = st.src(b, st.GB, gb, u)
                    before = prior[j] if j < RING else st.entries[j - RING]
                    if before[0] is None and before[1] != ADA_VEC:
                        sp.wait_ge(hi_done, unit(st, b, j) - (RING - 1))
                    else:
                        sp.wait_ge(lo_done, unit(st, b, j) + 1)
                    sp.dma_start(raw[j % RING][:], src).then_inc(raw_in[j % RING], 16)

            mark = lambda entries: [e[0] is None for e in entries]
            prior = [(0, 0)] * RING
            for st in stages:
                own = st.entries[-RING:]
                first = mark(prior) != mark(own)
                if first:
                    load(st, 0, prior)
                with sp.Fori(int(first), st.bodies) as b:
                    load(st, b, own)
                prior = own
            for n, (k0, k1) in enumerate(((0, 8), (8, 12), (12, 14), (14, KT))):
                sp.wait_ge(evac_done, groups_before(st_d2) + k1 // 2)
                sp.dma_start(out[:, k0:k1, :], X[:, k0:k1, :]).then_inc(out_stored, 16)
            sp.wait_ge(out_stored, 4 * 16)

        @block.gpsimd
        def _(pool):
            pool.wait_ge(in_att, 64)
            pool.memset(XC32[64:128, 0:4, :, 1, 192:256], -1e30).then_inc(masked, 1)
            pool.wait_ge(masked, 1)

            def add_condition(st):
                with pool.Fori(0, st.bodies) as b:
                    n = b + st.ib
                    for i, u in enumerate(ADA_ADDS):
                        j = st.cond[u]
                        w = prod[j % RING]
                        at = n * ADA_OPS + (0, *ADA_ADDS.values())[i]
                        pool.wait_ge(hi_done, unit(st, b, j) + 1)
                        pool.wait_ge(ada_ops, at + 1)
                        pool.tensor_tensor(w[:, 0:2, :], w[:, 0:2, :], w[:, 2:4, :], ALU.add).then_inc(ada_ops, 1)
                        pool.wait_ge(ada_ops, at + 2)
                        if u == 0:
                            pool.wait_ge(ada_red, n + 1)
                            pool.tensor_tensor(CA[:, 1, :], w[:, 0, :], w[:, 1, :], ALU.add).then_inc(ada_ops, 1)
                        else:
                            pool.tensor_tensor(w[:, 0, :], w[:, 0, :], w[:, 1, :], ALU.add).then_inc(ada_ops, 1)
                            pool.wait_ge(ada_ops, at + 3)
                            pool.tensor_tensor(CA[:, 1, :], CA[:, 1, :], w[:, 0, :], ALU.add).then_inc(ada_ops, 1)
                    pool.wait_ge(lo_done, unit(st, b, st.cond[ADA_VEC]) + 1 + RING)
                    pool.wait_ge(ada_ops, n * ADA_OPS + ADA_OPS)
                    pool.tensor_tensor(CA[:, 1, :], CA[:, 1, :], CA[:, 0, :], ALU.add).then_inc(ada_ops, 1)

            def normed_chunks(i, before):
                pool.wait_ge(rstd_ready, i + 1)
                for n, c in enumerate((1, 3)):
                    y = R[:, Yt + 4 * c:Yt + 4 * c + 4, :]
                    pool.tensor_tensor(y, y, rep(RS[:], 4), ALU.mult).then_inc(y_pool, 1)
                    pool.wait_ge(y_pool, before + n + 1)

            add_condition(st_in)

            pool.wait_ge(evac_done, evacuated(st_in))
            pool.wait_ge(in_cst, 32)
            count = 0

            def step(ins):
                nonlocal count
                count += 1
                ins.then_inc(poolstep, 1)

            for g, w in enumerate(WINDOWS):
                u_t = R[:, 24 + 2 * g:26 + 2 * g, :]
                src, d, turn = u_t, 1, 0
                while d < w:
                    dst = R[:, 52 + 2 * turn:54 + 2 * turn, :]
                    if count:
                        pool.wait_ge(poolstep, count)
                    step(pool.tensor_copy(dst[:, :, 0:d], src[:, :, 0:d]))
                    step(pool.tensor_tensor(dst[:, :, d:S], src[:, :, d:S], src[:, :, 0:S - d], ALU.add))
                    src, d, turn = dst, 2 * d, 1 - turn
                pool.wait_ge(poolstep, count)
                fix = poolfix[:, 32 * g:32 * g + 32].rearrange("p (a t) -> p a t", a=2)[:, :, 0:w - 1]
                step(pool.tensor_tensor(src[:, :, 0:w - 1], src[:, :, 0:w - 1], fix, ALU.mult))
                pool.wait_ge(poolstep, count)
                step(pool.tensor_scalar(src, src, 1.0 / w, None, ALU.mult))
                pool.wait_ge(poolstep, count)
                step(pool.tensor_tensor(u_t, src, u_t, ALU.subtract))
                pool.wait_ge(poolstep, count)
                pool.sem_inc(pooled, 1)

            add_condition(st_o)
            pool.wait_ge(evac_done, groups_before(st_o) + 1)
            for c in range(2):
                pool.dma_start(XC32[:, 8 * c:8 * c + 8, 0, 1, :], ctxT[:, 8 * c:8 * c + 8, :]).then_inc(in_ctx, 16)
            pool.wait_ge(ada_ops, st_up1a.ib * ADA_OPS + 1)
            normed_chunks(1, 0)
            add_condition(st_up1a)
            pool.wait_ge(sq_ready, SQ[5][0])
            n = KT // 2
            while n:
                pool.wait_ge(poolstep, count)
                a, b = XC32[:, 0:n, 1, 1, :], XC32[:, n:2 * n, 1, 1, :]
                step(pool.tensor_tensor(a, a, b, ALU.add))
                n //= 2
            pool.wait_ge(poolstep, count)
            pool.sem_inc(acc_ready, 1)
            for st in (st_dn1, st_up2, st_dn2):
                add_condition(st)
            pool.wait_ge(ada_ops, st_kv.ib * ADA_OPS + 1)
            normed_chunks(4, 2)
            add_condition(st_kv)
            pool.wait_ge(used, used_all(st_kv))
            for kt in range(3):
                pool.dma_start(XC32[:, 13 + kt, :, 1, :], cst[:, C_FLIP + 512 * kt:C_FLIP + 512 * kt + 512].rearrange(
                    "p (a n) -> p a n", a=2)).then_inc(in_rope, 16)
            add_condition(st_q1)
            add_condition(st_q2)
            pool.wait_ge(in_rope, 48)
            pool.wait_ge(ada_ops, st_ga.ib * ADA_OPS + 1)
            pool.wait_ge(gains, 1)
            late = 0

            def late_step(ins):
                nonlocal late
                late += 1
                ins.then_inc(n_late, 1)
                pool.wait_ge(n_late, late)

            cos, sin = XC32[:, 15, 0, 1, :], XC32[:, 15, 1, 1, :]
            for k, c in enumerate((2, 3, 4, 5, 10, 11)):
                if c == 10:
                    late_step(pool.tensor_scalar(cos, cos, SM[:, 31:32], None, ALU.mult))
                    late_step(pool.tensor_scalar(sin, sin, SM[:, 34:35], None, ALU.mult))
                chunk, sw, dims = rotation(c)
                pool.wait_ge(n_swap, 6 + k + 1)
                late_step(pool.tensor_tensor(chunk, chunk, rep(cos, *dims), ALU.mult))
                late_step(pool.tensor_tensor(sw, sw, rep(sin, *dims), ALU.mult))
                late_step(pool.tensor_tensor(chunk, chunk, sw, ALU.add))
            for st in (st_ga, st_gb, st_ba, st_bb, st_u1a):
                add_condition(st)

        @block.scalar
        def _(act):
            def hi(st, b, j, before=(0, 0), item=None):
                gb, u = st.entries[j % st.upb]
                if gb is None and u == ADA_VEC:
                    return
                act.wait_ge(raw_in[j % RING], filled(st, b, j))
                if before[0] is not None:
                    act.wait_ge(used, unit(st, b, j) + 1)
                elif before[1] != ADA_VEC:
                    act.wait_ge(ada_ops, item * ADA_OPS + (ADA_ADDS[before[1]] + 1))
                else:
                    act.wait_ge(used, unit(st, b, j) + (1 - RING))
                if gb is None:
                    for x in range(UK):
                        ins = act.activation(prod[j % RING][:, x, :], raw[j % RING][:, x, :], ACT.Copy,
                                             scale=cond_silu(st, u, x))
                    ins.then_inc(hi_done, 1)
                    return
                act.activation(whi[j % RING][:], raw[j % RING][:], ACT.Copy).then_inc(
                    hi_done, 2 if st.entries[j % st.upb - 1] == (None, ADA_VEC) else 1)

            def post(st, b, gb):
                g = group(st, b, gb)
                if st.kind == "conv" and gb % 2 == 0:
                    act.wait_ge(evac_done, g + 3)
                    act.activation(Gb[:], Cb[:], ACT.Gelu_apprx_tanh).then_inc(astep, 1)
                elif st.kind == "gate":
                    act.wait_ge(used, grouped(st, b, gb))
                    act.activation(R[:, ds(b * 4 + (st.tile0 + 2 * gb), 2), :], PS[:, gb % 2, :, 0:S],
                                   ACT.Sigmoid).then_inc(astep, 1)
                elif st.kind == "glu" and gb % 2 == 0:
                    act.wait_ge(used, grouped(st, b, gb))
                    act.wait_ge(evac_done, g + 2)
                    act.activation(Gb[:], PS[:, gb % 2, :, 0:S], ACT.Silu).then_inc(astep, 1)

            def body(st, b, final=False):
                for j in range(RING, RING + st.upb):
                    before = st.entries[j - RING]
                    if j < st.upb or not final:
                        hi(st, b, j, before, b + st.ib)
                    elif st.next is not None:
                        hi(st.next, 0, j - st.upb, before, b + st.ib)
                    if st is st_dn1 and j == RING + 10:
                        act.wait_ge(mod_v, b + 1)
                        act.activation(XC[:, ds(4 * b, 4), 0, 1, :], XC32[:, ds(4 * b, 4), 1, 1, :],
                                       ACT.Copy).then_inc(mod_hi, 1)
                    if st is st_ga and j == RING + 8:
                        act.wait_ge(o_norm, b + 1)
                        act.activation(XC[:, ds(2 * b, 2), 0, 1, :], R[:, ds(2 * b + 40, 2), :],
                                       ACT.Copy).then_inc(split_hi, 1)
                    if st.name in K_BODY and j == RING + 2:
                        c = b + (2 if st is st_q2 else 0)
                        if st is st_q1:
                            act.wait_ge(used, used_all(st_kv))
                        act.wait_ge(n_sum, c + 1)
                        act.activation(sqb(0), quad(R[:, ds(4 * b + K_BODY[st.name][1], 4), :]),
                                       ACT.Square).then_inc(n_sq, 1)
                    at = j - RING - (2 if st.kind == "conv" else 0)
                    if at in st.last:
                        post(st, b, st.last.index(at))

            def run(st):
                alone = st.next is None or bool(st.next.ada) != bool(st.ada)
                with act.Fori(0, st.bodies - alone) as b:
                    body(st, b)
                if alone:
                    body(st, st.bodies - 1, final=True)

            def root(i, n=D):
                act.wait_ge(sum_ready, i + 1)
                act.activation(RS[:], NB[:, 0:S], ACT.Sqrt, bias=SM[:, EPS_C:EPS_C + 1],
                               scale=1.0 / n).then_inc(root_ready, 1)

            def square_chunk(c, tile):
                act.activation(R[:, tile + 4 * c:tile + 4 * c + 4, :], X[:, 4 * c:4 * c + 4, :],
                               ACT.Square).then_inc(sq_ready, 1)

            act.dma_start(V[:], vec).then_inc(in_vec, 16)
            for c in range(4):
                act.dma_start(X[:, 4 * c:4 * c + 4, :], xT[:, 4 * c:4 * c + 4, :]).then_inc(in_x[c], 16)
            act.dma_start(IO[:], cst[:, 0:256]).then_inc(in_ones, 16)
            for kt in range(4):
                act.dma_start(XC32[:, kt, :, 1, :], bass.AP(
                    rel.tensor, 2 * kt * rel.shape[1], [[1, P], [rel.shape[1], 2], [1, S]])).then_inc(in_att, 16)
            act.dma_start(XC32[:, 13, :, 1, :], cst[:, C_FLIP:C_FLIP + 512].rearrange(
                "p (a n) -> p a n", a=2)).then_inc(in_cst, 16)
            act.dma_start(R[:, 32:40, :], pool_w).then_inc(in_cst, 16)

            act.wait_ge(in_vec, 16)
            act.activation(CS[:], V[:, VEC["cond"]:VEC["cond"] + 2 * KT], ACT.Silu).then_inc(silu_done, 1)
            act.wait_ge(silu_done, 1)
            for c in range(4):
                act.wait_ge(in_x[c], 16)
                for kt in range(4 * c, 4 * c + 4):
                    act.activation(XC[:, kt, 0, 0, :], X[:, kt, :], ACT.Copy,
                                   scale=V[:, VEC["pre_mix"] + kt:VEC["pre_mix"] + kt + 1]).then_inc(op_hi, 1)
                hi(st_in, 0, c)
            for c in range(4):
                square_chunk(c, 0)
            act.wait_ge(cleared, 1)
            root(0)
            run(st_in)

            def modulated_hi(m, who):
                for c in range(4):
                    act.wait_ge(mod_v, 4 * m + c + 1)
                    act.activation(XC[:, 4 * c:4 * c + 4, 0, who, :], XC32[:, 4 * c:4 * c + 4, 1, who, :],
                                   ACT.Copy).then_inc(mod_hi, 1)

            act.wait_ge(evac_done, evacuated(st_in))
            for j in range(4):
                act.wait_ge(vt_turned, j + 1)
                act.activation(R[:, 40 + 2 * j:42 + 2 * j, :], TP[:, j % 2, :].rearrange("p (a n) -> p a n", a=2),
                               ACT.Copy).then_inc(vt_copied, 1)
            N = 2 * H1
            for i in range(N + 3):
                if i < N:
                    w = 128 * (i % 2 + 1)
                    act.wait_ge(neg_max, i + 1)
                    if i >= 2:
                        act.wait_ge(turned, i - 1)
                    act.activation(R[:, 48 + i % 2, 0:w], PS[:, i % 2, 0, 0:w], ACT.Exp, bias=SM[:, i % 2:i % 2 + 1],
                                   accum_out=SM[:, 2 + i % 2:3 + i % 2]).then_inc(exped, 1)
                if 1 <= i <= N:
                    n = i - 1
                    w = 128 * (n % 2 + 1)
                    act.wait_ge(turned, n + 1)
                    if n >= 2:
                        act.wait_ge(summed, n - 1)
                    act.activation(R[:, 50 + n % 2, 0:w], TP[:, n % 2, 0:w], ACT.Copy).then_inc(pt_copied, 1)
                if i >= 3 and i % 2 == 1:
                    h = (i - 3) // 2
                    act.wait_ge(summed, 2 * h + 2)
                    act.activation(XC[:, h, 0, 0, :], PS[:, h % 2, 1, 0:S], ACT.Copy).then_inc(op_hi, 1)
            for j in range(8):
                act.wait_ge(summed, N + j + 1)
                act.activation(XC[:, 8 + j, 0, 0, :], PS[:, j % 2, 1, 0:S], ACT.Copy,
                               scale=V[:, VEC["pool_scale"] + j:VEC["pool_scale"] + j + 1]).then_inc(op_hi, 1)
            run(st_o)

            root(1)
            for kt in range(KT):
                act.wait_ge(x_new, kt + 1)
                act.activation(XC[:, kt, 0, 0, :], X[:, kt, :], ACT.Copy,
                               scale=V[:, VEC["pre_ffn"] + kt:VEC["pre_ffn"] + kt + 1]).then_inc(op_hi, 1)
                if kt % 4 == 3:
                    square_chunk(kt // 4, Yt)
            root(2)
            run(st_up1a)
            act.wait_ge(in_ctx, 32)
            act.activation(XC32[:, :, 1, 1, :], XC32[:, :, 0, 1, :], ACT.Square).then_inc(sq_ready, 1)
            run(st_up1b)
            act.wait_ge(sum_ready, 4)
            act.activation(CR, NB[:, 0:S], ACT.Sqrt, bias=SM[:, EPS_C:EPS_C + 1], scale=1.0 / D).then_inc(root_ready, 1)
            run(st_dn1)
            run(st_up2)
            run(st_dn2)

            root(4)
            for c in range(4):
                act.wait_ge(x_new, KT + 4 * c + 4)
                square_chunk(c, Yt)
            root(5)
            modulated_hi(1, 0)
            run(st_kv)
            for j in range(12):
                act.wait_ge(v2_turned, j + 1)
                act.activation(v_cols[:, :, j // 2, j % 2, :], TP[:, j % 2, :].rearrange("p (t d) -> p t d", t=4),
                               ACT.Copy).then_inc(v2_copied, 1)
            run(st_q1)
            run(st_q2)

            act.wait_ge(lam_sum, 1)
            act.activation(SM[:, 22:24], NB[:, 200:202], ACT.Exp).then_inc(lam_exp, 1)
            act.wait_ge(evac_done, evacuated(st_q2))
            act.wait_ge(in_rope, 48)

            def squares(c):
                act.wait_ge(n_sum, c)
                act.activation(sqb(c), quad(R[:, CH[c][0]:CH[c][0] + 4, :]), ACT.Square).then_inc(n_sq, 1)

            def head_root(lo_col, mid, hi_col, n):
                act.wait_ge(n_sum, n)
                act.activation(HR[:, lo_col:mid], NB[:, lo_col:mid], ACT.Sqrt, bias=SM[:, EPS_C:EPS_C + 1],
                               scale=1.0 / HD)
                act.activation(HR[:, mid:hi_col], NB[:, mid:hi_col], ACT.Sqrt, bias=SM[:, EPS_C:EPS_C + 1],
                               scale=1.0 / 64).then_inc(n_root, 1)

            SWAP_FREE = {7: 2, 8: 3, 9: 4, 10: 5, 11: 6}

            def swap(c):
                _, br, is_k = CH[c]
                if is_k:
                    act.wait_ge(n_scaled, c + 1)
                if c in SWAP_FREE:
                    act.wait_ge(n_rope, SWAP_FREE[c])
                s = 32 if br else 64
                src, dst, _ = rotation(c)
                for p in range(0, P, 2 * s):
                    for x, y in ((p, p + s), (p + s, p)):
                        last = act.activation(dst[x:x + s], src[y:y + s], ACT.Copy)
                last.then_inc(n_swap, 1)

            head_root(0, 16, 80, NK + 1)
            squares(NK)
            squares(NK + 1)
            swap(0)
            swap(1)
            for c in range(4):
                swap(NK + c)
                squares(NK + 2 + c)
            head_root(80, 112, 144, 2 * NK + 1)
            LATE = {1: 2, 2: 3, 3: 4, 4: 5, 6: 10, 8: 11}

            for i in range(NA + 3):
                if i < NA:
                    act.wait_ge(a_neg, i + 1)
                    if i >= 2:
                        act.wait_ge(a_turned, i - 1)
                    act.activation(scr(i % 2), PS[:, i % 2, 0, :].rearrange("p (a n) -> p a n", a=2), ACT.Exp,
                                   bias=SM[:, i % 2:i % 2 + 1], scale=HR[:, 80 + i:81 + i],
                                   accum_out=SM[:, 2 + i % 2:3 + i % 2]).then_inc(a_exp, 1)
                if 1 <= i <= NA:
                    n = i - 1
                    act.wait_ge(a_turned, n + 1)
                    if n >= 2:
                        act.wait_ge(a_summed, n - 1)
                    act.activation(scr(2 + n % 2), TP[:, n % 2, :].rearrange("p (a n) -> p a n", a=2),
                                   ACT.Copy).then_inc(a_copied, 1)
                if i in LATE:
                    swap(LATE[i])
                if i >= 3 and i % 2 == 1:
                    h = (i - 3) // 2
                    act.wait_ge(a_summed, 2 * h + 2)
                    act.activation(R[:, qa_tile(h), :], PS[:, h % 2, 1, 0:S], ACT.Copy).then_inc(a_out, 1)
            for i in range(NB_ + 3):
                if i < NB_:
                    act.wait_ge(b_neg, i + 1)
                    if i >= 2:
                        act.wait_ge(b_turned, i - 1)
                    for x in range(2):
                        e = 2 * (i % 2) + x
                        act.activation(scr(e), PS[:, i % 2, x, :].rearrange("p (a n) -> p a n", a=2), ACT.Exp,
                                       bias=SM[:, 6 + e:7 + e], scale=HR[:, 112 + 2 * i + x:113 + 2 * i + x],
                                       accum_out=SM[:, 10 + e:11 + e]).then_inc(b_exp, 1)
                if 1 <= i <= NB_:
                    n = i - 1
                    act.wait_ge(b_turned, n + 1)
                    if n >= 2:
                        act.wait_ge(b_summed, n - 1)
                    act.activation(scr(4 + n % 2), TP[:, n % 2, :].rearrange("p (a n) -> p a n", a=2),
                                   ACT.Copy).then_inc(b_copied, 1)
                if i >= 3 and i % 2 == 1:
                    h = (i - 3) // 2
                    act.wait_ge(b_summed, 2 * h + 2)
                    act.activation(R[:, 40 + h, :], (NB, AB)[h % 2][:, 0:S], ACT.Copy).then_inc(b_out, 1)
            act.wait_ge(b_out, HB)
            act.activation(R[:, 64:72, :], R[:, 40:48, :], ACT.Square).then_inc(o_sq, 1)
            act.wait_ge(o_sum, 1)
            act.activation(R[:, 0:8, :], PS[:].rearrange("p a m (h n) -> p (a m h) n", h=2), ACT.Sqrt,
                           bias=SM[:, EPS_C:EPS_C + 1], scale=1.0 / HD).then_inc(o_root, 1)
            run(st_ga)
            run(st_gb)
            for c in range(4):
                act.activation(XC[:, 4 * c:4 * c + 4, 0, 0, :], R[:, O_SRC[c]:O_SRC[c] + 4, :],
                               ACT.Copy).then_inc(split_hi, 1)
            run(st_ba)
            run(st_bb)
            act.wait_ge(evac_done, evacuated(st_bb))
            for c in range(4):
                act.activation(XC[:, 4 * c:4 * c + 4, 0, 0, :], R[:, 16 + 4 * c:20 + 4 * c, :],
                               ACT.Copy).then_inc(split_hi, 1)
            run(st_out)
            root(6)
            modulated_hi(2, 0)
            run(st_u1a)
            run(st_u1b)
            run(st_d1)
            run(st_u2)
            run(st_d2)

        @block.vector
        def _(dve):
            def lo(st, b, j):
                gb, u = st.entries[j % st.upb]
                if gb is None:
                    if u == ADA_VEC:
                        n = b + (st.ib + j // st.upb)
                        dve.wait_ge(raw_in[j % RING], filled(st, b, j))
                        dve.wait_ge(ada_red, n + 1)
                        for x in range(UK):
                            w, c = raw[j % RING][:, x, :], cond_silu(st, u, x)
                            if x:
                                dve.wait_ge(ada_sum, n * (UK - 1) + x)
                                ins = dve.scalar_tensor_tensor(out=CA[:, 0, :], in0=w, scalar=c, in1=CA[:, 0, :],
                                                               op0=ALU.mult, op1=ALU.add)
                            else:
                                ins = dve.tensor_scalar(CA[:, 0, :], w, c, None, ALU.mult)
                            ins.then_inc(lo_done if x == UK - 1 else ada_sum, 1)
                    return
                dve.wait_ge(hi_done, unit(st, b, j) + 1)
                prev = st.entries[j % st.upb - 1]
                dve.tensor_tensor(wlo[j % RING][:], raw[j % RING][:], whi[j % RING][:].bitcast(F32),
                                  ALU.subtract).then_inc(lo_done, 2 if prev[0] is None and prev[1] != ADA_VEC
                                                         else 1)

            def steps_from(st, b, gb, i):
                def did(ins):
                    nonlocal i
                    ins.then_inc(vstep, 1)
                    i += 1

                def settled(n=1):
                    dve.wait_ge(vstep, vst(st, b, gb, i - n))

                return did, settled

            def evac(st, b, gb):
                g = group(st, b, gb)
                k = st.kind
                sums = PS[:, gb % 2, :, 0:S]
                tile = b * (2 * st.GB) + (st.tile0 + 2 * gb)
                if k == "kv":
                    dve.wait_ge(used, grouped(st, b, gb))
                    dve.tensor_copy(R[:, ds(b * (4 * st.GB) + 4 * gb, 4), :],
                                    PS[:, gb % 2, :, :].rearrange("p m (a n) -> p (m a) n", a=2)).then_inc(evac_done, 1)
                    return
                dve.wait_ge(evac_done, g + 2)
                dve.wait_ge(used, grouped(st, b, gb))
                did, settled = steps_from(st, b, gb, 0)
                if k == "q":
                    dve.tensor_copy(R[:, ds(tile, 2), :], sums).then_inc(evac_done, 1)
                elif k == "down1":
                    dve.tensor_copy(R[:, ds(tile + Yt, 2), :], sums).then_inc(evac_done, 1)
                elif k == "gate" or (k == "glu" and gb % 2 == 0):
                    dve.wait_ge(astep, ast(st, b, gb, 0))
                    dve.sem_inc(evac_done, 1)
                elif k == "mix_out":
                    y = R[:, ds(tile + Yt, 2), :]
                    did(dve.tensor_copy(y, sums))
                else:
                    if k == "scale":
                        dve.tensor_tensor(R[:, ds(tile, 2), :], sums, rep(RS[:], 2), ALU.mult).then_inc(evac_done, 1)
                    elif k == "down2":
                        y = R[:, ds(tile + Yt, 2), :]
                        did(dve.tensor_tensor(y, y, sums, ALU.add))
                    elif k == "branch_a":
                        ga = R[:, ds(tile + 16, 2), :]
                        dve.tensor_tensor(ga, sums, ga, ALU.mult).then_inc(evac_done, 1)
                    elif k == "branch_b":
                        ga, gb_ = R[:, ds(tile + 16, 2), :], R[:, ds(tile + 48, 2), :]
                        did(dve.tensor_tensor(gb_, sums, gb_, ALU.mult))
                        settled()
                        dve.tensor_tensor(ga, ga, gb_, ALU.add).then_inc(evac_done, 1)
                    elif k in ("out", "down_x"):
                        chunk = 2 if k == "out" else 5
                        for m in range(2):
                            x = X[:, ds(tile + m, 1), :].rearrange("p a n -> p (a n)")
                            ins = dve.scalar_tensor_tensor(
                                out=x, in0=sums[:, m, :], scalar=MOD[:, ds(tile + (2 * ADA_CTX + KT * chunk + m), 1)],
                                in1=x, op0=ALU.mult, op1=ALU.add)
                            if m == 1 and k == "down_x":
                                ins.then_inc(evac_done, 1)
                            else:
                                did(ins)
                    elif k == "conv":
                        did(dve.tensor_tensor(Zp[:, :, 2:S + 2], sums, rep(RS[:], 2), ALU.mult))
                        settled()
                        t0 = b * 2 + (FT * (gb % 2) + st.feat0 + VEC["conv_w"])
                        tb = b * 2 + (FT * (gb % 2) + st.feat0 + VEC["conv_b"])
                        if gb % 2:
                            dve.wait_ge(astep, ast(st, b, 0, 0))
                        for m in range(2):
                            did(dve.tensor_scalar(Cb[:, m, :], Zp[:, m, 2:S + 2], V[:, ds(t0 + (4 * FT + m), 1)],
                                                  V[:, ds(tb + m, 1)], ALU.mult, ALU.add))
                        for tap in (1, 0):
                            for m in range(2):
                                settled(2)
                                ins = dve.scalar_tensor_tensor(
                                    out=Cb[:, m, :], in0=Zp[:, m, tap:S + tap],
                                    scalar=V[:, ds(t0 + (2 * FT * tap + m), 1)], in1=Cb[:, m, :],
                                    op0=ALU.mult, op1=ALU.add)
                                if gb % 2 == 0 and tap == 0 and m == 1:
                                    ins.then_inc(evac_done, 1)
                                else:
                                    did(ins)
                    if gb % 2 and k == "glu":
                        dve.wait_ge(astep, ast(st, b, 0, 0))
                        did(dve.tensor_tensor(Gb[:], sums, Gb[:], ALU.mult))

            def finish(st, b, gb):
                k = st.kind
                if k in ("mix_out", "down2", "out"):
                    tile = b * (2 * st.GB) + (st.tile0 + 2 * gb)
                    src = X[:, ds(tile, 2), :] if k == "out" else R[:, ds(tile + Yt, 2), :]
                    did, settled = steps_from(st, b, gb, 2 if k == "out" else 1)
                    settled()
                    did(dve.tensor_tensor(Cb[:], src, src, ALU.mult))
                    settled()
                    did(dve.tensor_tensor(RS[:], RS[:], Cb[:, 0, :], ALU.add))
                    settled()
                    dve.tensor_tensor(RS[:], RS[:], Cb[:, 1, :], ALU.add).then_inc(evac_done, 1)
                elif gb % 2 and k in ("conv", "glu"):
                    val = Cb if k == "conv" else Gb
                    did, settled = steps_from(st, b, gb, 7 if k == "conv" else 1)
                    settled()
                    if k == "conv":
                        did(dve.tensor_tensor(val[:], val[:], Gb[:], ALU.mult))
                        settled()
                    f = b * 2 + st.tile0
                    fh, fl = FH[:, ds(f, 2), 0, :], FH[:, ds(f, 2), 1, :]
                    did(dve.tensor_copy(fh, val[:]))
                    settled()
                    dve.tensor_tensor(fl, val[:], fh.bitcast(F32), ALU.subtract).then_inc(evac_done, 1)

            def store_mods(st, b):
                n = b + st.ib
                dve.wait_ge(ada_red, n + 2)
                dve.tensor_tensor(MOD[:, ds(n * 2, 2)], AB[:, 0:2], V[:, ds(n * 2 + VEC["b_ada"], 2)],
                                  ALU.add).then_inc(mods_done, 1)

            def output_norm(b, at):
                if at in (0, 2):
                    root_ = R[:, ds(2 * b + at // 2, 1), :]
                    dve.wait_ge(o_root, 1)
                    dve.reciprocal(root_, root_).then_inc(o_inv, 1)
                elif at == 5:
                    heads = R[:, ds(2 * b + 40, 2), :]
                    dve.wait_ge(o_inv, b * 2 + 2)
                    dve.scalar_tensor_tensor(out=heads, in0=heads, scalar=SM[:, 32:33], in1=R[:, ds(2 * b, 2), :],
                                             op0=ALU.mult, op1=ALU.mult).then_inc(o_norm, 1)
                elif at == 11:
                    dve.wait_ge(split_hi, b + 1)
                    dve.tensor_tensor(XC[:, ds(2 * b, 2), 1, 1, :], R[:, ds(2 * b + 40, 2), :],
                                      XC[:, ds(2 * b, 2), 0, 1, :].bitcast(F32), ALU.subtract).then_inc(opnd, 2)

            def context_operand(b, at):
                if at == 1:
                    dve.tensor_tensor(XC32[:, ds(4 * b, 4), 1, 1, :], XC32[:, ds(4 * b, 4), 0, 1, :], rep(CR, 4),
                                      ALU.mult).then_inc(mod_t, 1)
                elif at == 3:
                    dve.wait_ge(mod_t, b + 1)
                    for x in range(4):
                        v = XC32[:, ds(4 * b + x, 1), 1, 1, :].rearrange("p a n -> p (a n)")
                        last = dve.tensor_scalar(v, v, GS[:, ds(4 * b + x, 1)], MOD[:, ds(4 * b + x, 1)],
                                                 ALU.mult, ALU.add)
                    last.then_inc(mod_v, 1)
                elif at == 12:
                    dve.wait_ge(mod_hi, b + 1)
                    dve.tensor_tensor(XC[:, ds(4 * b, 4), 1, 1, :], XC32[:, ds(4 * b, 4), 1, 1, :],
                                      XC[:, ds(4 * b, 4), 0, 1, :].bitcast(F32), ALU.subtract).then_inc(opnd, 4)

            def body(st, b, final=False):
                for j in range(RING, RING + st.upb):
                    gb = st.last.index(j - RING) if j - RING in st.last else None
                    gate = st.kind == "gate" or (st.kind == "glu" and gb == 0)
                    if st is st_dn1:
                        context_operand(b, j - RING)
                    if st is st_ga:
                        output_norm(b, j - RING)
                    if gb is not None and not gate:
                        evac(st, b, gb)
                    if j < st.upb or not final:
                        lo(st, b, j)
                    elif st.next is not None:
                        lo(st.next, 0, j - st.upb)
                    if gb is not None and gate:
                        evac(st, b, gb)
                    if gb is not None:
                        finish(st, b, gb)
                if st.ada:
                    store_mods(st, b)

            def run(st):
                alone = st.next is None or bool(st.next.ada) != bool(st.ada)
                with dve.Fori(0, st.bodies - alone) as b:
                    body(st, b)
                if alone:
                    body(st, st.bodies - 1, final=True)

            def invert(i):
                dve.wait_ge(root_ready, i + 1)
                dve.reciprocal(RS[:], RS[:]).then_inc(rstd_ready, 1)
                dve.wait_ge(rstd_ready, i + 1)

            n_clear = 0

            def clear(ap, value=0.0):
                nonlocal n_clear
                dve.memset(ap, value).then_inc(cleared, 1)
                n_clear += 1
                dve.wait_ge(cleared, n_clear)

            dve.sem_inc(lo_done, RING)
            dve.sem_inc(evac_done, 2)
            dve.sem_inc(ada_ops, 1)
            dve.sem_inc(mods_done, 1)
            clear(SM[:, EPS_C:EPS_C + 1], EPS)
            dve.wait_ge(in_vec, 16)
            dve.tensor_scalar(SM[:, 30:31], V[:, VEC["q_a"]:VEC["q_a"] + 1], HD ** -0.5, None, ALU.mult)
            dve.tensor_scalar(SM[:, 31:32], V[:, VEC["q_b"]:VEC["q_b"] + 1], 64 ** -0.5, None, ALU.mult)
            dve.tensor_scalar(SM[:, 33:34], V[:, VEC["q_a_sw"]:VEC["q_a_sw"] + 1], HD ** -0.5, None, ALU.mult)
            dve.tensor_scalar(SM[:, 34:35], V[:, VEC["q_b_sw"]:VEC["q_b_sw"] + 1], 64 ** -0.5, None, ALU.mult)
            dve.tensor_scalar(SM[:, 32:33], V[:, VEC["subln"]:VEC["subln"] + 1], 1 - LAM_INIT, None,
                              ALU.mult)
            dve.tensor_tensor(SM[:, 28:30], V[:, VEC["lam"]:VEC["lam"] + 4:2], V[:, VEC["lam"] + 1:VEC["lam"] + 4:2],
                              ALU.mult).then_inc(gains, 1)
            dve.wait_ge(gains, 1)

            def scaled_lo(kt, gain, n_hi, source):
                dve.wait_ge(op_hi, n_hi)
                dve.scalar_tensor_tensor(out=XC[:, kt, 1, 0, :], in0=source, scalar=gain,
                                         in1=XC[:, kt, 0, 0, :].bitcast(F32), op0=ALU.mult,
                                         op1=ALU.subtract).then_inc(opnd, 1)

            gain_col = lambda name, kt: V[:, VEC[name] + kt:VEC[name] + kt + 1]
            dve.wait_ge(silu_done, 1)
            for kt in range(KT):
                scaled_lo(kt, gain_col("pre_mix", kt), kt + 1, X[:, kt, :])
                if kt % 4 == 3:
                    lo(st_in, 0, kt // 4)
            invert(0)
            run(st_in)

            dve.wait_ge(evac_done, evacuated(st_in))
            dve.tensor_scalar(R[:, 0:8, :], R[:, 0:8, :], HD ** -0.5, None, ALU.mult).then_inc(q_scaled, 1)
            clear(RS[:])
            N = 2 * H1
            for i in range(N + 4):
                if 1 <= i <= N:
                    n = i - 1
                    w = 128 * (n % 2 + 1)
                    dve.wait_ge(exped, n + 1)
                    dve.reciprocal(SM[:, 4 + n % 2:5 + n % 2], SM[:, 2 + n % 2:3 + n % 2]).then_inc(inverse, 1)
                    dve.wait_ge(inverse, n + 1)
                    dve.tensor_scalar(R[:, 48 + n % 2, 0:w], R[:, 48 + n % 2, 0:w], SM[:, 4 + n % 2:5 + n % 2], None,
                                      ALU.mult).then_inc(probs, 1)
                if i < N:
                    w = 128 * (i % 2 + 1)
                    dve.wait_ge(scored, i + 1)
                    dve.tensor_reduce(SM[:, i % 2:i % 2 + 1], PS[:, i % 2, 0, 0:w], AX.X, ALU.max,
                                      negate=True).then_inc(neg_max, 1)
                if i >= 4 and i % 2 == 0:
                    h = (i - 4) // 2
                    dve.wait_ge(op_hi, KT + h + 1)
                    dve.tensor_tensor(XC[:, h, 1, 0, :], PS[:, h % 2, 1, 0:S], XC[:, h, 0, 0, :].bitcast(F32),
                                      ALU.subtract).then_inc(opnd, 1)
            for j in range(8):
                scaled_lo(8 + j, gain_col("pool_scale", j), KT + H1 + j + 1, PS[:, j % 2, 1, 0:S])
            run(st_o)

            def modulation_gain(gain, base, n_gains):
                dve.scalar_tensor_tensor(out=GS[:], in0=MOD[:, base + KT:base + 2 * KT], scalar=1.0,
                                         in1=V[:, VEC[gain]:VEC[gain] + KT], op0=ALU.add, op1=ALU.mult
                                         ).then_inc(gains, 1)
                dve.wait_ge(gains, n_gains)

            def add_normed(c, i, name):
                y = R[:, Yt + 4 * c:Yt + 4 * c + 4, :]
                if c % 2:
                    dve.wait_ge(y_pool, 2 * i + c // 2 + 1)
                else:
                    dve.tensor_tensor(y, y, rep(RS[:], 4), ALU.mult).then_inc(y_normed, 1)
                    dve.wait_ge(y_normed, 2 * i + c // 2 + 1)
                for kt in range(4 * c, 4 * c + 4):
                    dve.scalar_tensor_tensor(out=X[:, kt, :], in0=R[:, Yt + kt, :], scalar=gain_col(name, kt),
                                             in1=X[:, kt, :], op0=ALU.mult, op1=ALU.add).then_inc(x_new, 1)

            dve.wait_ge(evac_done, evacuated(st_o))
            dve.sem_inc(acc_ready, 1)
            invert(1)
            for c in range(5):
                if c < 4:
                    add_normed(c, 0, "post_mix")
                if c >= 1:
                    for kt in range(4 * c - 4, 4 * c):
                        scaled_lo(kt, gain_col("pre_ffn", kt), 2 * KT + kt + 1, X[:, kt, :])
            clear(Zp[:, :, 0:2])
            invert(2)
            run(st_up1a)
            dve.wait_ge(mods_done, ADA_CTX + 1)
            modulation_gain("norm1", 0, 2)
            run(st_up1b)
            dve.wait_ge(root_ready, 4)
            dve.reciprocal(CR, CR).then_inc(rstd_ready, 1)
            dve.wait_ge(rstd_ready, 4)
            run(st_dn1)
            run(st_up2)
            dve.wait_ge(evac_done, evacuated(st_up2))
            clear(RS[:])
            run(st_dn2)

            def modulate(m, src, who, gain, base, n_gains):
                modulation_gain(gain, base, n_gains)
                for c in range(5):
                    if c < 4:
                        k = slice(4 * c, 4 * c + 4)
                        dve.tensor_tensor(XC32[:, k, 1, who, :], src[:, k, :], rep(RS[:], 4),
                                          ALU.mult).then_inc(mod_t, 1)
                    if c >= 1:
                        k = slice(4 * c - 4, 4 * c)
                        dve.wait_ge(mod_hi, 4 * m + c)
                        dve.tensor_tensor(XC[:, k, 1, who, :], XC32[:, k, 1, who, :], XC[:, k, 0, who, :].bitcast(F32),
                                          ALU.subtract).then_inc(opnd, 4)
                    if c < 4:
                        dve.wait_ge(mod_t, 4 * m + c + 1)
                        for kt in range(4 * c, 4 * c + 4):
                            v = XC32[:, kt, 1, who, :]
                            last = dve.tensor_scalar(v, v, GS[:, kt:kt + 1], MOD[:, base + kt:base + kt + 1],
                                                     ALU.mult, ALU.add)
                        last.then_inc(mod_v, 1)

            dve.wait_ge(evac_done, evacuated(st_dn2))
            dve.sem_inc(acc_ready, 1)
            invert(4)
            for c in range(4):
                add_normed(c, 1, "post_ffn")
            invert(5)
            dve.wait_ge(mods_done, st_kv.ib + 1)
            modulate(1, X, 0, "norm1", 2 * ADA_CTX, 3)
            clear(RS[:])
            run(st_kv)
            run(st_q1)
            run(st_q2)

            dve.wait_ge(lam_exp, 1)
            dve.tensor_tensor(SM[:, 24:25], SM[:, 23:24], SM[:, 22:23], ALU.subtract).then_inc(lam_vec, 1)
            dve.wait_ge(lam_vec, 1)
            dve.tensor_scalar(SM[:, NEGLAM:NEGLAM + 1], SM[:, 24:25], -LAM_INIT, None, ALU.add).then_inc(lam_vec, 1)
            dve.wait_ge(lam_vec, 2)
            dve.wait_ge(evac_done, evacuated(st_q2))
            dve.wait_ge(in_rope, 48)
            dve.wait_ge(n_root, 1)
            dve.reciprocal(HR[:, 0:80], HR[:, 0:80]).then_inc(n_inv, 1)

            def rotate(c, n):
                chunk, sw, dims = rotation(c)
                cos, sin = XC32[:, 14, 0, 1, :], XC32[:, 14, 1, 1, :]
                dve.wait_ge(n_swap, n + 1)
                dve.tensor_tensor(chunk, chunk, rep(cos, *dims), ALU.mult).then_inc(n_t1, 1)
                dve.tensor_tensor(sw, sw, rep(sin, *dims), ALU.mult).then_inc(n_t2, 1)
                dve.wait_ge(n_t1, n + 1)
                dve.wait_ge(n_t2, n + 1)
                dve.tensor_tensor(chunk, chunk, sw, ALU.add).then_inc(n_rope, 1)

            for c in range(NK):
                t, br, _ = CH[c]
                chunk = quad(R[:, t:t + 4, :])
                dve.wait_ge(n_bcast, c + 1)
                dve.scalar_tensor_tensor(
                    out=chunk, in0=chunk, scalar=gain_col("k_b" if br else "k_a", 0),
                    in1=PS[:, c % 2, :, :].rearrange("p k (a n) -> p k a n", a=2), op0=ALU.mult,
                    op1=ALU.mult).then_inc(n_scaled, 1)
                if c in (1, 2):
                    rotate(c - 1, c - 1)
            dve.wait_ge(n_rope, 2)
            dve.tensor_scalar(XC32[:, 14, 0, 1, :], XC32[:, 14, 0, 1, :], SM[:, 30:31], None, ALU.mult)
            dve.tensor_scalar(XC32[:, 14, 1, 1, :], XC32[:, 14, 1, 1, :], SM[:, 33:34], None,
                              ALU.mult).then_inc(n_table, 1)
            dve.wait_ge(n_table, 1)
            for c in range(NK, NK + 4):
                rotate(c, c - 4)
            dve.wait_ge(n_root, 2)
            dve.reciprocal(HR[:, 80:144], HR[:, 80:144]).then_inc(n_inv, 1)
            dve.wait_ge(n_inv, 2)

            for i in range(NA + 1):
                if i >= 1:
                    n = i - 1
                    dve.wait_ge(a_exp, n + 1)
                    dve.reciprocal(SM[:, 4 + n % 2:5 + n % 2], SM[:, 2 + n % 2:3 + n % 2]).then_inc(a_inv, 1)
                    dve.wait_ge(a_inv, n + 1)
                    dve.tensor_scalar(scr(n % 2), scr(n % 2), SM[:, 4 + n % 2:5 + n % 2], None,
                                      ALU.mult).then_inc(a_prob, 1)
                if i < NA:
                    dve.wait_ge(a_scored, i + 1)
                    dve.tensor_reduce(SM[:, i % 2:i % 2 + 1], PS[:, i % 2, 0, :], AX.X, ALU.max,
                                      negate=True).then_inc(a_max, 1)
                    dve.wait_ge(a_max, i + 1)
                    dve.tensor_tensor(SM[:, i % 2:i % 2 + 1], SM[:, i % 2:i % 2 + 1],
                                      HR[:, 80 + i:81 + i], ALU.mult).then_inc(a_neg, 1)
            for i in range(NB_ + 1):
                if i >= 1:
                    n = i - 1
                    e = 2 * (n % 2)
                    dve.wait_ge(b_exp, 2 * n + 2)
                    dve.reciprocal(SM[:, 14 + e:16 + e], SM[:, 10 + e:12 + e]).then_inc(b_inv, 1)
                    dve.wait_ge(b_inv, n + 1)
                    dve.tensor_tensor(SM[:, 18 + n % 2:19 + n % 2], SM[:, 15 + e:16 + e], SM[:, NEGLAM:NEGLAM + 1],
                                      ALU.mult).then_inc(b_nl, 1)
                    dve.wait_ge(b_nl, n + 1)
                    dve.tensor_scalar(scr(e + 1), scr(e + 1), SM[:, 18 + n % 2:19 + n % 2], None,
                                      ALU.mult).then_inc(b_p1, 1)
                    dve.wait_ge(b_p1, n + 1)
                    dve.scalar_tensor_tensor(out=scr(e), in0=scr(e), scalar=SM[:, 14 + e:15 + e], in1=scr(e + 1),
                                             op0=ALU.mult, op1=ALU.add).then_inc(b_prob, 1)
                if i < NB_:
                    dve.wait_ge(b_scored, i + 1)
                    e = 6 + 2 * (i % 2)
                    dve.tensor_reduce(SM[:, e:e + 2], PS[:, i % 2, :, :], AX.X, ALU.max,
                                      negate=True).then_inc(b_max, 1)
                    dve.wait_ge(b_max, i + 1)
                    dve.tensor_tensor(SM[:, e:e + 2], SM[:, e:e + 2], HR[:, 112 + 2 * i:114 + 2 * i],
                                      ALU.mult).then_inc(b_neg, 1)
            def split_lo(k0, who, tile, n):
                dve.wait_ge(split_hi, n)
                dve.tensor_tensor(XC[:, k0:k0 + 4, 1, who, :], R[:, tile:tile + 4, :],
                                  XC[:, k0:k0 + 4, 0, who, :].bitcast(F32), ALU.subtract).then_inc(opnd, 4)

            run(st_ga)
            run(st_gb)
            for c in range(4):
                split_lo(4 * c, 0, O_SRC[c], 5 + c)
            run(st_ba)
            run(st_bb)
            for c in range(4):
                split_lo(4 * c, 0, 16 + 4 * c, 9 + c)
            run(st_out)
            dve.wait_ge(evac_done, evacuated(st_out))
            dve.sem_inc(acc_ready, 1)
            invert(6)
            dve.wait_ge(mods_done, st_u1a.ib + 1)
            modulate(2, X, 0, "norm2", 2 * ADA_CTX + 3 * KT, 4)
            run(st_u1a)
            run(st_u1b)
            run(st_d1)
            run(st_u2)
            run(st_d2)

        @block.tensor
        def _(pe):
            def multiply(st, b, j, fresh):
                gb, u = st.entries[j]
                pe.wait_ge(lo_done, unit(st, b, j) + 1 + RING)
                if fresh and st.op is not None:
                    pe.wait_ge(opnd, st.op + 4 * (u + 1))
                if fresh and st.act:
                    pe.wait_ge(evac_done, groups_before(st.after) + min(4 * (u + 1), st.gb - st.after.gb))
                h, l = whi[j % RING], wlo[j % RING]
                for x in range(UK):
                    kt = UK * u + x
                    first, last = kt == 0, kt == UK * st.U - 1
                    for m in range(2):
                        f = slice(P * m, P * m + P)
                        if st.kind == "kv":
                            out_ = PS[:, gb % 2, m, :].rearrange("p (a n) -> p a n", a=2)
                            mov = XC[:, kt, :, :, :]
                        else:
                            out_ = PS[:, gb % 2, m, 0:S]
                            mov = FH[:, kt, :, :] if st.act else XC[:, kt, :, st.who, :]
                        pe.matmul(out_, h[:, x, f], mov[:, 0], start=first, stop=False)
                        pe.matmul(out_, h[:, x, f], mov[:, 1], start=False, stop=False)
                        ins = pe.matmul(out_, l[:, x, f], mov[:, 0], start=False, stop=last)
                ins.then_inc(used, 2 if st.entries[j - 1][0] is None else 1)

            def take_condition(st, b):
                n = b + st.ib
                pe.wait_ge(ada_ops, n * ADA_OPS + (ADA_OPS + 1))
                pe.wait_ge(mods_done, n + 1)
                for m in range(2):
                    ins = pe.matmul(AB[:, m:m + 1], CA[:, 1, P * m:P * m + P], ones[:, 0:1], start=True, stop=True)
                ins.then_inc(ada_red, 1)

            def key_sums(st, b):
                br, _, first = K_BODY[st.name]
                w = 1 + br
                pe.wait_ge(n_sq, b + (3 if br else 1))
                for x in range(4):
                    for t in range(2):
                        ins = pe.matmul(NB[:, ds(b * (8 * w) + (first + w * (2 * x + t)), w)],
                                        sqb(0)[:, x // 2, x % 2, P * t:P * t + P],
                                        halves[:, 0:128:64] if br else ones[:, 0:1], start=True, stop=True)
                ins.then_inc(n_sum, 1)

            def body(st, b, fresh=True, insert=None):
                for j, (gb, u) in enumerate(st.entries):
                    if gb is None:
                        continue
                    if u == 0:
                        pe.wait_ge(evac_done, group(st, b, gb) + 1)
                    multiply(st, b, j, fresh and gb == 0)
                    if st.name in K_BODY and gb == 1 and u == 0:
                        key_sums(st, b)
                    if insert is not None and gb == u == 0:
                        sum_squares(insert)
                if st.ada:
                    take_condition(st, b)

            def run(st, insert=None):
                if insert is not None:
                    body(st, 0, insert=insert)
                    with pe.Fori(1, st.bodies) as b:
                        body(st, b, fresh=False)
                else:
                    with pe.Fori(0, st.bodies) as b:
                        body(st, b)

            def sum_squares(i):
                if i in ACC:
                    pe.wait_ge(acc_ready, ACC[i])
                    ins = pe.matmul(NB[:, 0:S], ones, XC32[:, 0, 1, 1, :] if i == 3 else RS[:], start=True, stop=True)
                else:
                    before, tile = SQ[i]
                    if i == 0:
                        pe.wait_ge(in_ones, 16)
                    for kt in range(KT):
                        pe.wait_ge(sq_ready, before + kt // 4 + 1)
                        ins = pe.matmul(NB[:, 0:S], ones, R[:, tile + kt, :], start=kt == 0, stop=kt == KT - 1)
                ins.then_inc(sum_ready, 1)

            pe.sem_inc(used, RING)
            pe.sem_inc(ada_red, 1)
            pe.sem_inc(n_sum, 1)
            run(st_in, insert=0)
            pe.wait_ge(in_cst, 32)

            pe.wait_ge(evac_done, evacuated(st_in))
            pe.wait_ge(masked, 1)
            for j in range(4):
                if j >= 2:
                    pe.wait_ge(vt_copied, j - 1)
                for x in range(4):
                    h, tb = 4 * (j % 2) + x, j // 2
                    ins = pe.transpose(TP[:, j % 2, P * x:P * x + P], R[:, 16 + h, P * tb:P * tb + P], ident)
                ins.then_inc(vt_turned, 1)
            pe.wait_ge(q_scaled, 1)
            N = 2 * H1

            def score(n):
                h, b = divmod(n, 2)
                w = P * (b + 1)
                if n >= 2:
                    pe.wait_ge(exped, n - 1)
                pe.matmul(PS[:, n % 2, 0, 0:w], R[:, h, P * b:P * b + P], R[:, 8 + h, 0:w], start=True, stop=False)
                pe.matmul(PS[:, n % 2, 0, 0:w], flip, hankel(h)[:, P * (1 - b):P * (1 - b) + w], start=False,
                          stop=True).then_inc(scored, 1)

            score(0)
            score(1)
            pe.wait_ge(vt_copied, 4)
            for i in range(N + 1):
                if i < N:
                    pe.wait_ge(probs, i + 1)
                    if i >= 2:
                        pe.wait_ge(pt_copied, i - 1)
                    for t in range(i % 2 + 1):
                        ins = pe.transpose(TP[:, i % 2, P * t:P * t + P], R[:, 48 + i % 2, P * t:P * t + P], ident)
                    ins.then_inc(turned, 1)
                if i + 2 < N:
                    score(i + 2)
                if i >= 1:
                    n = i - 1
                    h, b = divmod(n, 2)
                    pe.wait_ge(pt_copied, n + 1)
                    if b == 0 and h >= 2:
                        pe.wait_ge(opnd, KT + h - 1)
                    for t in range(b + 1):
                        ins = pe.matmul(PS[:, h % 2, 1, P * b:P * b + P],
                                        R[:, 40 + 4 * t + h // 2, P * (h % 2):P * (h % 2) + P],
                                        R[:, 50 + n % 2, P * t:P * t + P], start=t == 0, stop=t == b)
                    ins.then_inc(summed, 1)
            for j in range(8):
                g = j // 2
                pe.wait_ge(pooled, g + 1)
                pe.wait_ge(opnd, KT + H1 + j - 1)
                for c in range(2):
                    ins = pe.matmul(PS[:, j % 2, 1, 0:S], R[:, 32 + 2 * g + c, P * (j % 2):P * (j % 2) + P],
                                    R[:, 24 + 2 * g + c, :], start=c == 0, stop=c == 1)
                ins.then_inc(summed, 1)
            pe.wait_ge(opnd, 2 * KT)
            run(st_o)
            sum_squares(1)
            run(st_up1a, insert=2)
            with pe.Fori(0, st_up1b.bodies - 1) as b:
                body(st_up1b, b)
            body(st_up1b, st_up1b.bodies - 1, insert=3)
            run(st_dn1)
            run(st_up2)
            run(st_dn2)
            sum_squares(4)
            sum_squares(5)
            pe.wait_ge(opnd, 4 * KT)
            run(st_kv)

            pe.wait_ge(evac_done, evacuated(st_kv))
            for j in range(12):
                if j >= 2:
                    pe.wait_ge(v2_copied, j - 1)
                tile = 8 + 2 * j if j < 4 else 24 + 2 * j
                for t in range(4):
                    ins = pe.transpose(TP[:, j % 2, P * t:P * t + P],
                                       R[:, tile + t // 2, P * (t % 2):P * (t % 2) + P], ident)
                ins.then_inc(v2_turned, 1)
            run(st_q1)
            pe.wait_ge(in_rope, 48)
            run(st_q2)

            pe.wait_ge(gains, 1)
            pe.matmul(NB[:, 200:202], ones, SM[:, 28:30], start=True, stop=True).then_inc(lam_sum, 1)
            pe.wait_ge(evac_done, evacuated(st_q2))
            pe.wait_ge(lam_exp, 1)

            def head_sums(c):
                br = CH[c][1]
                pe.wait_ge(n_sq, c + 1)
                for x in range(4):
                    for t in range(2):
                        at = hr_col(c, x, t)
                        ins = pe.matmul(NB[:, at:at + 1 + br], sqb(c)[:, x // 2, x % 2, P * t:P * t + P],
                                        halves[:, 0:128:64] if br else ones[:, 0:1], start=True, stop=True)
                ins.then_inc(n_sum, 1)

            pe.wait_ge(n_inv, 1)
            for c in range(NK):
                if c >= 2:
                    pe.wait_ge(n_scaled, c - 1)
                br = CH[c][1]
                for x in range(4):
                    for t in range(2):
                        at = hr_col(c, x, t)
                        for i in range(1 + br):
                            col = HR[:, at + i:at + i + 1]
                            n = P >> br
                            ins = pe.matmul(PS[n * i:n * i + n, c % 2, x // 2, S * (x % 2) + P * t:S * (x % 2) + P * t + P],
                                            bass.AP(col.tensor, col.offset, [col.ap[0], [0, n]]), ident,
                                            start=True, stop=True)
                ins.then_inc(n_bcast, 1)
            for c in range(NK):
                head_sums(NK + c)

            def turn(n, buf, prob, copied, done):
                pe.wait_ge(prob, n + 1)
                if n >= 2:
                    pe.wait_ge(copied, n - 1)
                for t in range(4):
                    ins = pe.transpose(TP[:, n % 2, P * t:P * t + P], buf[:, t // 2, P * (t % 2):P * (t % 2) + P],
                                       ident)
                ins.then_inc(done, 1)

            def values(n, dst, j, buf, copied, done):
                pe.wait_ge(copied, n + 1)
                for t in range(4):
                    ins = pe.matmul(dst, v_at(j, t), buf[:, t // 2, P * (t % 2):P * (t % 2) + P],
                                    start=t == 0, stop=t == 3)
                ins.then_inc(done, 1)

            def score_a(n):
                h, b = divmod(n, 2)
                if n >= 2:
                    pe.wait_ge(a_exp, n - 1)
                pe.matmul(PS[:, n % 2, 0, :].rearrange("p (a n) -> p a n", a=2),
                          R[:, qa_tile(h), P * b:P * b + P], R[:, 2 * (h // 4):2 * (h // 4) + 2, :],
                          start=True, stop=True).then_inc(a_scored, 1)

            pe.wait_ge(n_rope, 6)
            pe.wait_ge(v2_copied, 12)
            score_a(0)
            score_a(1)
            for i in range(NA + 1):
                if i < NA:
                    turn(i, scr(i % 2), a_prob, a_copied, a_turned)
                if i + 2 < NA:
                    score_a(i + 2)
                if i >= 1:
                    n = i - 1
                    h, b = divmod(n, 2)
                    if b == 0 and h >= 2:
                        pe.wait_ge(a_out, h - 1)
                    values(n, PS[:, h % 2, 1, P * b:P * b + P], h // 4, scr(2 + n % 2), a_copied, a_summed)
            pe.wait_ge(a_out, HA)

            def score_b(n):
                h, b = divmod(n, 2)
                if n >= 2:
                    pe.wait_ge(b_exp, 2 * n - 2)
                for x in range(2):
                    rows = slice(64 * x, 64 * x + 64)
                    ins = pe.matmul(PS[:, n % 2, x, :].rearrange("p (a n) -> p a n", a=2),
                                    R[rows, 40 + h, P * b:P * b + P], R[rows, 16 + 2 * h:18 + 2 * h, :],
                                    start=True, stop=True)
                ins.then_inc(b_scored, 1)

            pe.wait_ge(n_late, 20)
            score_b(0)
            score_b(1)
            for i in range(NB_ + 1):
                if i < NB_:
                    turn(i, scr(2 * (i % 2)), b_prob, b_copied, b_turned)
                if i + 2 < NB_:
                    score_b(i + 2)
                if i >= 1:
                    n = i - 1
                    h, b = divmod(n, 2)
                    if b == 0 and h >= 2:
                        pe.wait_ge(b_out, h - 1)
                    values(n, (NB, AB)[h % 2][:, P * b:P * b + P], 4 + h, scr(4 + n % 2), b_copied, b_summed)
            pe.wait_ge(o_sq, 1)
            for t in range(4):
                ins = pe.matmul(PS[:, t // 2, t % 2, :].rearrange("p (a n) -> p a n", a=2), ones,
                                R[:, 64 + 2 * t:66 + 2 * t, :], start=True, stop=True)
            ins.then_inc(o_sum, 1)
            pe.wait_ge(o_root, 1)
            run(st_ga)
            run(st_gb)
            run(st_ba)
            run(st_bb)
            run(st_out)
            sum_squares(6)
            run(st_u1a)
            run(st_u1b)
            run(st_d1)
            run(st_u2)
            run(st_d2)


def rotations():
    rows = np.repeat(np.arange(S // 64, dtype=np.float32), 64)
    col = np.tile(np.arange(64, dtype=np.float32), S // 64)
    out = []
    for hd in (128, 64):
        n = hd // 4
        freqs = np.float32(10000.0) ** (-np.arange(n, dtype=np.float32) / np.float32(n))
        ang = np.concatenate([rows[:, None] * freqs, col[:, None] * freqs], axis=-1).T.astype(np.float32)
        p = np.arange(P)
        sign = np.where(p % hd < hd // 2, -1.0, 1.0).astype(np.float32)[:, None]
        out += [np.cos(ang)[p % (hd // 2)], sign * np.sin(ang)[p % (hd // 2)]]
    return out


def constants():
    p = np.arange(P)
    fix = np.ones((4, 2, 16), np.float32)
    for g, w in enumerate(WINDOWS):
        fix[g, :, :w - 1] = np.float32(w) / np.arange(1, w, dtype=np.float32)
    parts = [np.eye(P), np.ones((P, P)), np.eye(P)[::-1], (p[:, None] // 64 == p[None, :] // 64).astype(np.float32),
             np.tile(fix.reshape(1, -1), (P, 1)), np.zeros((P, 128))] + rotations()
    return np.ascontiguousarray(np.concatenate(parts, axis=1), dtype=np.float32)


def kernel(**inputs):
    import concourse.bacc as bacc
    from concourse.bass_utils import run_bass_kernel_spmd

    a = {k: np.asarray(v) for k, v in inputs.items()}
    tiles = lambda v: v.reshape(-1, P).T
    taps = lambda w: np.concatenate([tiles(r) for r in w], axis=1)
    b_ada = tiles(a["b_ada_2"][0])

    def column(v):
        c = np.zeros((P, 1), v.dtype)
        c[:v.size, 0] = v.reshape(-1)
        return c

    twice = lambda v: np.concatenate([v, v]).reshape(P, 1)
    vec = np.concatenate(
        [tiles(a[n][0]) for n in ("pre_mix_g", "post_mix_g", "pre_ffn_g", "post_ffn_g", "norm1_g_2", "norm2_g_2")]
        + [taps(a["conv_w"][0]), tiles(a["conv_b"][0]), tiles(a["pool_scale"][0]),
           column(a["q_norm_a_2"][0]), column(a["k_norm_a_2"][0]), twice(a["q_norm_b_2"][0]), twice(a["k_norm_b_2"][0]),
           tiles(a["c_ctx_2"]), tiles(a["c_2"][0])]
        + [column(a[n][0]) for n in ("lam_q1_2", "lam_k1_2", "lam_q2_2", "lam_k2_2")]
        + [b_ada[:, :2 * KT], b_ada, column(a["subln_g_2"][0]),
           np.roll(a["q_norm_a_2"][0], HD // 2).reshape(P, 1), twice(np.roll(a["q_norm_b_2"][0], 32))], axis=1)
    feature_major = lambda v: np.ascontiguousarray(v.T.reshape(KT, P, S).transpose(1, 0, 2))
    reach = a["rel_bias"].shape[2] // 2
    order = np.clip(S - 1 - np.arange(S + P - 1), -reach, reach) + reach
    arrays = {
        "xT": feature_major(a["x"][0]), "ctxT": feature_major(a["ctx_2"][0]), "vec": np.ascontiguousarray(vec),
        "cst": constants(), "rel": np.ascontiguousarray(a["rel_bias"][0][:, order]), "w_in": a["w_in"][0],
        "pool_w": np.ascontiguousarray(a["pool_w"][0].reshape(8, P, 256).transpose(1, 0, 2)),
        "w_o": a["w_o"][0], "w_up": a["w_up"][0], "w_down": a["w_down"][0], "w_ada": a["w_ada_2"][0],
        "w_in2": a["w_in_2"][0], "w_bra": a["w_br_a_2"][0], "w_brb": a["w_br_b_2"][0], "w_out2": a["w_out_2"][0],
        "w_fg": a["w_ff_gate_2"][0], "w_fu": a["w_ff_up_2"][0], "w_fd": a["w_ff_down_2"][0],
    }
    nc = bacc.Bacc("TRN2", target_bir_lowering=False, num_devices=1)
    args = {n: nc.dram_tensor(n, v.shape, mybir.dt.from_np(v.dtype), kind="ExternalInput").ap()
            for n, v in arrays.items()}
    args["out"] = nc.dram_tensor("out", (P, KT, S), F32, kind="ExternalOutput").ap()
    build(nc, **args)
    r = run_bass_kernel_spmd(nc, [arrays], core_ids=[0])
    got = r.results[0]["out"]
    return got.transpose(1, 0, 2).reshape(D, S).T.reshape(1, S, D)
```
